# Optimizing a Trainium2 kernel written in Bass

```python
import math
import jax, jax.numpy as jnp
from jax import lax
import numpy as np

D_MODEL = 1024
BATCH = 1
SEQ = 512
DEPTH = 1

CHUNK = 64
HEAD_DIM = 64
A_HEADS = 16
A_KV_HEADS = 2
WINDOW = 128
WIN_CHUNKS = -(-WINDOW // CHUNK)
BAND = WIN_CHUNKS * CHUNK
B_HEADS = 16
KV_RANK = 128
IDX_HEADS = 8
IDX_DIM = 64
TOPK_MAX = 256
Q_BLOCK = 128
N_GROUPS = 4
EXPERTS_PER_GROUP = 8
EXPERT_FF = 256
TOP_K_EXPERTS = 2
ALPHA = (2.0 * DEPTH) ** 0.25
BETA = (8.0 * DEPTH) ** -0.25
LN_EPS = 1e-5
RMS_EPS = 1e-6

A_Q_COLS = A_HEADS * HEAD_DIM
A_KV_COLS = A_KV_HEADS * HEAD_DIM
B_Q_COLS = B_HEADS * HEAD_DIM
IDX_Q_COLS = IDX_HEADS * IDX_DIM
SPLIT_SIZES = (A_Q_COLS, A_KV_COLS, A_KV_COLS, B_Q_COLS, KV_RANK, IDX_Q_COLS, IDX_DIM, IDX_HEADS, D_MODEL, D_MODEL)
IN_COLS = sum(SPLIT_SIZES)
V_A_START = A_Q_COLS + A_KV_COLS
V_A_END = V_A_START + A_KV_COLS

kernel_name = "hybrid_swa_dsa_hmoe_block"

def _split_points():
    pts, acc = [], 0
    for s in SPLIT_SIZES[:-1]:
        acc += s
        pts.append(acc)
    return pts

def _alibi_slopes(n):
    return jnp.exp2(-8.0 * jnp.arange(1, n + 1, dtype=jnp.float32) / n)

def _layernorm(x, g, b):
    xf = x.astype(jnp.float32)
    mu = jnp.mean(xf, -1, keepdims=True)
    var = jnp.mean(jnp.square(xf - mu), -1, keepdims=True)
    y = (xf - mu) * lax.rsqrt(var + LN_EPS) * g.astype(jnp.float32) + b.astype(jnp.float32)
    return y.astype(x.dtype)

def _rmsnorm(x, g):
    xf = x.astype(jnp.float32)
    y = xf * lax.rsqrt(jnp.mean(jnp.square(xf), -1, keepdims=True) + RMS_EPS) * g.astype(jnp.float32)
    return y.astype(x.dtype)

def _chunk_band(kc):
    nC = kc.shape[1]
    kp = jnp.concatenate([jnp.zeros_like(kc[:, :WIN_CHUNKS - 1]), kc], axis=1)
    return jnp.concatenate([kp[:, w:w + nC] for w in range(WIN_CHUNKS)], axis=2)

def _swa_sink_attention(q, k, v, sinks):
    B, T = q.shape[:2]
    nC = T // CHUNK
    G = A_HEADS // A_KV_HEADS
    qc = q.reshape(B, nC, CHUNK, A_KV_HEADS, G, HEAD_DIM)
    kb = _chunk_band(k.reshape(B, nC, CHUNK, A_KV_HEADS, HEAD_DIM))
    vb = _chunk_band(v.reshape(B, nC, CHUNK, A_KV_HEADS, HEAD_DIM))
    s = jnp.einsum('bcikgd,bcjkd->bckgij', qc, kb).astype(jnp.float32) * (HEAD_DIM ** -0.5)
    i = jnp.arange(CHUNK)[:, None]
    j = jnp.arange(BAND)[None, :]
    dist = jnp.abs(i - j + (WIN_CHUNKS - 1) * CHUNK).astype(jnp.float32)
    slopes = _alibi_slopes(A_HEADS).reshape(A_KV_HEADS, G)[:, :, None, None]
    s = s - slopes * dist
    chunk_ok = (jnp.arange(nC)[:, None] + jnp.arange(BAND)[None, :] // CHUNK - (WIN_CHUNKS - 1)) >= 0
    s = jnp.where(chunk_ok[None, :, None, None, None, :], s, jnp.float32(-jnp.inf))
    sink = sinks.astype(jnp.float32).reshape(A_KV_HEADS, G)[None, None, :, :, None, None]
    m = jnp.maximum(jnp.max(s, -1, keepdims=True), sink)
    e = jnp.exp(s - m)
    p = (e / (jnp.sum(e, -1, keepdims=True) + jnp.exp(sink - m))).astype(v.dtype)
    o = jnp.einsum('bckgij,bcjkd->bcikgd', p, vb)
    return o.reshape(B, T, A_HEADS * HEAD_DIM)

def _dsa_attention(q, k, v, q_idx, k_idx, w_idx):
    B, T = q.shape[:2]
    n_sel = min(TOPK_MAX, T // 4)
    nb = T // Q_BLOCK
    slopes = _alibi_slopes(B_HEADS)
    key_chunk = jnp.arange(T) // CHUNK
    idx_scale = (IDX_DIM ** -0.5) * (IDX_HEADS ** -0.5)
    neg_inf = jnp.float32(-jnp.inf)

    def block(bi):
        t0 = bi * Q_BLOCK
        qb = lax.dynamic_slice_in_dim(q, t0, Q_BLOCK, axis=1)
        qib = lax.dynamic_slice_in_dim(q_idx, t0, Q_BLOCK, axis=1)
        wb = lax.dynamic_slice_in_dim(w_idx, t0, Q_BLOCK, axis=1)
        t_pos = t0 + jnp.arange(Q_BLOCK)
        rel = jax.nn.relu(jnp.einsum('bqhd,bsd->bqhs', qib, k_idx).astype(jnp.float32))
        score = jnp.einsum('bqh,bqhs->bqs', wb.astype(jnp.float32) * idx_scale, rel)
        adm = key_chunk[None, :] <= (t_pos // CHUNK)[:, None]
        score = jnp.where(adm[None], score, neg_inf)
        vals, sel = lax.top_k(score, n_sel)
        valid = jnp.isfinite(vals)
        k_sel = jax.vmap(lambda kk, ii: kk[ii])(k, sel)
        v_sel = jax.vmap(lambda vv, ii: vv[ii])(v, sel)
        s = jnp.einsum('bqhd,bqkd->bqhk', qb, k_sel).astype(jnp.float32) * (HEAD_DIM ** -0.5)
        dist = jnp.abs(t_pos[None, :, None] - sel).astype(jnp.float32)
        s = s - slopes[None, None, :, None] * dist[:, :, None, :]
        s = jnp.where(valid[:, :, None, :], s, neg_inf)
        p = jax.nn.softmax(s, axis=-1).astype(v.dtype)
        return jnp.einsum('bqhk,bqkd->bqhd', p, v_sel)

    o = lax.map(block, jnp.arange(nb))
    return o.transpose(1, 0, 2, 3, 4).reshape(B, T, B_HEADS * HEAD_DIM)

def _hybrid_mixer(h, w_in, a_sinks, kv_norm_g, w_uk, w_uv, w_branch_a, w_branch_b, w_out):
    B, T, _ = h.shape
    z = h @ w_in
    qa, ka, va, qb, ckv, qi, ki, wi, ga, gb = jnp.split(z, _split_points(), axis=-1)
    oa = _swa_sink_attention(qa.reshape(B, T, A_HEADS, HEAD_DIM),
                             ka.reshape(B, T, A_KV_HEADS, HEAD_DIM),
                             va.reshape(B, T, A_KV_HEADS, HEAD_DIM), a_sinks)
    c = _rmsnorm(ckv, kv_norm_g)
    ob = _dsa_attention(qb.reshape(B, T, B_HEADS, HEAD_DIM), c @ w_uk, c @ w_uv,
                        qi.reshape(B, T, IDX_HEADS, IDX_DIM), ki, wi)
    m = jax.nn.sigmoid(ga) * (oa @ w_branch_a) + jax.nn.sigmoid(gb) * (ob @ w_branch_b)
    return m @ w_out

def _hier_moe(x, rg_w, rg_b, re_w, re_b, w_gate, w_up, w_down):
    B, T, D = x.shape
    xf = x.reshape(B * T, D)
    g_prob = jax.nn.softmax((xf @ rg_w).astype(jnp.float32) + rg_b.astype(jnp.float32), axis=-1)
    p_g, g_sel = lax.top_k(g_prob, 1)
    e_logits = jnp.einsum('nd,dge->nge', xf, re_w).astype(jnp.float32) + re_b.astype(jnp.float32)
    e_logits = jnp.take_along_axis(e_logits, g_sel[:, :, None], axis=1)[:, 0]
    e_prob = jax.nn.softmax(e_logits, axis=-1)
    top_w, top_i = lax.top_k(e_prob, TOP_K_EXPERTS)
    top_w = top_w / jnp.sum(top_w, -1, keepdims=True)
    w_e = jnp.sum(jax.nn.one_hot(top_i, EXPERTS_PER_GROUP, dtype=jnp.float32) * top_w[..., None], axis=1)
    combine = jax.nn.one_hot(g_sel[:, 0], N_GROUPS, dtype=jnp.float32)[:, :, None] * (p_g * w_e)[:, None, :]
    combine = combine.astype(x.dtype)
    y = jnp.zeros_like(xf)
    for g in range(N_GROUPS):
        hg = jax.nn.silu(jnp.einsum('nd,edf->nef', xf, w_gate[g])) * jnp.einsum('nd,edf->nef', xf, w_up[g])
        y = y + jnp.einsum('nef,efd->nd', hg * combine[:, g, :, None], w_down[g])
    return y.reshape(B, T, D)

def setup_inputs(seed: int = 0) -> dict:
    key = jax.random.key(seed)
    ks = jax.random.split(key, 20)
    f32 = jnp.float32
    L = DEPTH
    nrm = lambda k, shape, scale: jax.random.normal(k, shape, f32) * scale
    x = jax.random.normal(ks[0], (BATCH, SEQ, D_MODEL), f32)
    w_in = nrm(ks[1], (L, D_MODEL, IN_COLS), D_MODEL ** -0.5)
    w_in = w_in.at[:, :, V_A_START:V_A_END].multiply(BETA)
    return {
        "x": x,
        "w_in": w_in,
        "a_sinks": nrm(ks[2], (L, A_HEADS), 0.5),
        "kv_norm_g": 1.0 + nrm(ks[3], (L, KV_RANK), 0.02),
        "w_uk": nrm(ks[4], (L, KV_RANK, HEAD_DIM), KV_RANK ** -0.5),
        "w_uv": nrm(ks[5], (L, KV_RANK, HEAD_DIM), BETA * KV_RANK ** -0.5),
        "w_branch_a": nrm(ks[6], (L, A_Q_COLS, D_MODEL), A_Q_COLS ** -0.5),
        "w_branch_b": nrm(ks[7], (L, B_Q_COLS, D_MODEL), B_Q_COLS ** -0.5),
        "w_out": nrm(ks[8], (L, D_MODEL, D_MODEL), BETA * D_MODEL ** -0.5),
        "ln1_g": 1.0 + nrm(ks[9], (L, D_MODEL), 0.02),
        "ln1_b": nrm(ks[10], (L, D_MODEL), 0.02),
        "router_group_w": nrm(ks[11], (L, D_MODEL, N_GROUPS), D_MODEL ** -0.5),
        "router_group_b": nrm(ks[12], (L, N_GROUPS), 0.01),
        "router_expert_w": nrm(ks[13], (L, D_MODEL, N_GROUPS, EXPERTS_PER_GROUP), D_MODEL ** -0.5),
        "router_expert_b": nrm(ks[14], (L, N_GROUPS, EXPERTS_PER_GROUP), 0.01),
        "w_gate": nrm(ks[15], (L, N_GROUPS, EXPERTS_PER_GROUP, D_MODEL, EXPERT_FF), D_MODEL ** -0.5),
        "w_up": nrm(ks[16], (L, N_GROUPS, EXPERTS_PER_GROUP, D_MODEL, EXPERT_FF), D_MODEL ** -0.5),
        "w_down": nrm(ks[17], (L, N_GROUPS, EXPERTS_PER_GROUP, EXPERT_FF, D_MODEL), BETA * EXPERT_FF ** -0.5),
        "ln2_g": 1.0 + nrm(ks[18], (L, D_MODEL), 0.02),
        "ln2_b": nrm(ks[19], (L, D_MODEL), 0.02),
    }

def reference(x, w_in, a_sinks, kv_norm_g, w_uk, w_uv, w_branch_a, w_branch_b, w_out, ln1_g, ln1_b,
              router_group_w, router_group_b, router_expert_w, router_expert_b, w_gate, w_up, w_down,
              ln2_g, ln2_b):
    h = x
    for l in range(DEPTH):
        y = _hybrid_mixer(h, w_in[l], a_sinks[l], kv_norm_g[l], w_uk[l], w_uv[l],
                          w_branch_a[l], w_branch_b[l], w_out[l])
        h = _layernorm(ALPHA * h + y, ln1_g[l], ln1_b[l])
        f = _hier_moe(h, router_group_w[l], router_group_b[l], router_expert_w[l], router_expert_b[l],
                      w_gate[l], w_up[l], w_down[l])
        h = _layernorm(ALPHA * h + f, ln2_g[l], ln2_b[l])
    return h


_drawn_inputs = setup_inputs


def setup_inputs(seed=0):
    import zlib

    import numpy as np

    out = dict(_drawn_inputs(seed))
    spreads = {}
    factors = {'a_sinks': 23.016,
     'kv_norm_g': 8.0,
     'router_group_b': 7.249,
     'router_expert_b': 21.327,
     'ln2_g': 8.472,
     'ln2_b': 8.283}
    for name, (base, spread) in spreads.items():
        noise = np.random.default_rng([zlib.crc32(name.encode()), seed]).standard_normal(out[name].shape)
        drawn = base * np.exp(spread * noise) if base else spread * noise
        out[name] = __import__('jax').numpy.asarray(drawn.astype(out[name].dtype))
    for name, factor in factors.items():
        out[name] = (out[name] * factor).astype(out[name].dtype)
    return out
```

```python
import concourse.bass as bass
from concourse import mybir
from contextlib import ExitStack

F32 = mybir.dt.float32
I32 = mybir.dt.int32
ALU = mybir.AluOpType
ACT = mybir.ActivationFunctionType
AX = mybir.AxisListType

P = 128
T, D = 512, 1024
TT, DT = T // P, D // P
CHUNK, HD = 64, 64
AH, AG = 16, 2
BH = 16
RANK = 128
IH = 8
TOPK = min(256, T // 4)
NG, EPG, FF = 4, 8, 256
NE = NG * EPG
CAP = 64
N_TOP = 2
PAIRS = N_TOP * T
MAX_OVER = 16
NBLK = NE + MAX_OVER
ALPHA = 2.0 ** 0.25
LN_EPS, RMS_EPS = 1e-5, 1e-6
IDX_SCALE = (HD ** -0.5) * (IH ** -0.5)
MASKED = -1e30
OUT_OF_REACH = -1e38
TAKEN = -3e38

C_QA = 0
C_KA = C_QA + AH * HD
C_VA = C_KA + AG * HD
C_QB = C_VA + AG * HD
C_CKV = C_QB + BH * HD
C_QI = C_CKV + RANK
C_KI = C_QI + IH * HD
C_WI = C_KI + HD
C_GA = C_WI + IH
C_GB = C_GA + D
C_END = C_GB + D

SLOPE = [2.0 ** (-8.0 * (h + 1) / 16) for h in range(16)]
WSLOT = DT * 512
EXW = DT * 2 * FF + 2 * D


def weight_chunks():
    out = [("in", C_CKV, 512), ("in", C_CKV + 512, C_GA - C_CKV - 512), ("in", C_KA, 256)]
    out += [("in", C_QA + 512 * i, 512) for i in range(2)]
    out += [("in", C_QB + 512 * i, 512) for i in range(2)]
    out += [("in", C_GA + 512 * i, 512) for i in range(4)]
    for i in range(2):
        out += [("a", 512 * i, 512), ("b", 512 * i, 512)]
    out += [("out", 512 * i, 512) for i in range(2)]
    return out


def units():
    out = [("ckv", 0, 0, 0)] + [("qi", m, 0, 128 + 128 * m) for m in range(3)]
    out += [("qi", 3, 1, 0), ("ki", 0, 1, 128), ("wi", 0, 1, 192)]
    out += [("ka", 0, 2, 0), ("va", 0, 2, 128)]
    out += [("qa", m, 3 + m // 4, 128 * (m % 4)) for m in range(8)]
    out += [("qb", m, 5 + m // 4, 128 * (m % 4)) for m in range(8)]
    out += [("gate", m, 7 + m // 4, 128 * (m % 4)) for m in range(16)]
    for m in range(8):
        out += [("a", m, 11 + 2 * (m // 4), 128 * (m % 4)), ("b", m, 12 + 2 * (m // 4), 128 * (m % 4))]
    out += [("out", 2 * t + i, 15 + i, 0) for t in range(TT) for i in range(2)]
    return out


CHUNKS, UNITS = weight_chunks(), units()
UNIT = {(kind, i): n for n, (kind, i, _, _) in enumerate(UNITS)}
LAST_OF_CHUNK = {c: n for n, (_, _, c, _) in enumerate(UNITS)}
RING = 3


def bank_of(u):
    kind, i, _, _ = UNITS[u]
    if kind == "out":
        return 4 + 2 * ((i // 2) % 2) + i % 2
    if kind in "ab":
        return 2 * (i % 2) + (kind == "b")
    if kind in ("qb", "gate"):
        return 6
    return 6 + u % 2


ITEMS = [("A", q, t) for q in range(4) for t in range(TT)] + [("B", j, t) for t in range(TT) for j in range(8)]


def build(nc, x, w_in, a_sinks, kv_norm_g, w_uk, w_uv, w_branch_a, w_branch_b, w_out, ln1_g, ln1_b,
          rg_w, rg_b, re_w, re_b, w_gate, w_up, w_down, ln2_g, ln2_b, out):
    ctx = ExitStack()
    with ctx:
        sem = lambda name: ctx.enter_context(nc.semaphore(name))
        sb = lambda name, shape, dt=F32: ctx.enter_context(nc.sbuf_tensor(name, shape, dt))

        h1_dram = nc.dram_tensor("h1_rows", (T, D), F32, kind="Internal").ap()
        table_dram = nc.dram_tensor("slot_token", ((NBLK + 1) * CAP, 1), F32, kind="Internal").ap()
        y_dram = nc.dram_tensor("expert_rows", (NBLK * CAP, D), F32, kind="Internal").ap()

        arena = sb("arena", [P, 46208])
        at = [0]

        def region(n):
            at[0] += n
            return at[0] - n

        def view(off, *shape):
            n = 1
            for s in shape:
                n *= s
            v = arena[:, off:off + n]
            if len(shape) == 2:
                return v.rearrange("p (a b) -> p a b", a=shape[0])
            if len(shape) == 3:
                return v.rearrange("p (a b c) -> p a b c", a=shape[0], b=shape[1])
            return v

        r_ring = region(RING * WSLOT)
        r_gb = region(DT * T)
        r_att = region(4096 + 6144 + 1152)
        r_qi = region(2048)
        r_sp = region(4096)
        r_xt = region(4096)
        r_qa = region(4096)
        r_qb = region(4096)
        r_x = r_att
        ga_off = region(0)
        assert at[0] <= 46208, at
        ga_t = sb("gate_a_T", [P, DT, T])
        wslot = [view(r_ring + i * WSLOT, DT, 512) for i in range(RING)]
        gaT = ga_t[:, :, :]
        gbT = view(r_gb, DT, T)
        x_nat = view(r_x, TT, D)
        biasA = view(r_att, 4, 4, 192)
        rel = [view(r_att + 3072 + 512 * i, 512) for i in range(2)]
        o = r_att + 4096

        def take(n):
            nonlocal o
            o += n
            return o - n

        kiT = view(take(512), T)
        kaT = view(take(1024), AG, T)
        va = view(take(512), TT, AG * HD)
        va_hi = view(take(512), TT, AG * HD)
        c_nat = view(take(512), TT, RANK)
        cT = view(take(512), T)
        kbT = view(take(512), T)
        vb = view(take(256), TT, HD)
        negd = view(take(512), 512)
        dm_off = take(1280)
        work_off = take(1152)
        assert o <= r_qi
        dm = [view(dm_off + P * t * (t + 1) // 2, P * (t + 1)) for t in range(TT)]
        work = [None] + [view(work_off + P * (t * (t + 1) // 2 - 1), P * (t + 1)) for t in range(1, TT)]
        qiT = view(r_qi, 4, T)
        s_sb = [view(r_sp + 1024 * i, 1024) for i in range(2)]
        pt_sb = [view(r_sp + 2048 + 1024 * i, 1024) for i in range(2)]
        xT = view(r_xt, DT, T)
        qaT = view(r_qa, DT, T)
        qbT = view(r_qb, DT, T)
        ln1g, ln1b = view(r_qi, D), view(r_qi + D, D)
        ax = view(r_sp, TT, D)
        h1 = view(r_qa, TT, D)
        h1T = view(r_xt, DT, T)
        ln2g, ln2b = view(r_xt, D), view(r_xt + D, D)
        xg = [view(r_qb + 1024 * i, D) for i in range(4)]
        ex_off = [r_gb, r_gb + EXW, r_ring, r_ring + EXW]
        assert r_gb + 2 * EXW <= r_qi and 2 * EXW <= RING * WSLOT
        ex_gu = [view(f, 2, DT, FF) for f in ex_off]
        ex_d = [view(f + 2 * DT * FF, 2, D) for f in ex_off]
        e = r_sp
        xgT = [view(e + 512 * i, DT, CAP) for i in range(2)]
        th = [view(e + 1024 + 256 * i, FF) for i in range(2)]
        gated = [view(e + 1536 + 256 * i, FF) for i in range(2)]
        hid = [view(e + 2048 + 256 * i, FF) for i in range(2)]
        hidT = [view(e + 2560 + 128 * i, 2, CAP) for i in range(2)]
        y_sb = [view(e + 2816 + 512 * i, 512) for i in range(2)]
        yk = [[ga_t[:, 4 * i + 2 * k:4 * i + 2 * k + 2, :].rearrange("p a b -> p (a b)") for k in range(2)]
              for i in range(2)]

        ident = sb("ident", [P, P])
        ones = sb("ones", [P, P])
        upper = sb("upper", [P, P])
        wuk = sb("wuk", [P, HD])
        wuv = sb("wuv", [P, HD])
        kvg = sb("kvg", [P, RANK])
        sinks_row = sb("sinks_row", [P, AH])
        sinks = sb("sinks", [P, 4, 4])
        rw = sb("rw", [P, DT, NG + NE])
        rb = sb("rb", [P, NG + NE])
        wis = sb("wis", [P, TT, IH])
        m8 = sb("m8", [P, 3, 8])
        css = sb("css", [P, 8])
        rstd_c = sb("rstd_c", [P, 4])
        half_neg = sb("half_neg", [P, 4])
        mx = sb("mx", [P, len(ITEMS), 4])
        negm = sb("negm", [P, len(ITEMS), 4])
        den = sb("den", [P, len(ITEMS), 4])
        sink_e = sb("sink_e", [P, 16, 4])
        ln = sb("ln", [P, 2, 5, 4])
        lg = sb("lg", [P, TT, NG + NE])
        desc = sb("desc", [P, NE])
        base0 = sb("base0", [P, NE])
        jrow = sb("jrow", [1, MAX_OVER])
        g4 = sb("g4", [P, 4, TT, NG])
        g1 = sb("g1", [P, 10, TT])
        e32 = view(r_qb + 1024, 8, TT * NE).rearrange("p a (t e) -> p a t e", t=TT)
        oh = view(r_qb + 2048, 3, TT * NE).rearrange("p a (t e) -> p a t e", t=TT)
        cnt = sb("cnt", [P, 4, NE])
        over_cmp = view(r_qb + 2560, MAX_OVER, NE)[0:1]
        over_f = sb("over_f", [1, MAX_OVER + 1])
        over_i = sb("over_i", [1, MAX_OVER + 1], I32)
        slot_f = sb("slot_f", [P, 2, TT])
        slot_i = sb("slot_i", [P, 2, TT], I32)
        comb = sb("comb", [P, 2, TT])
        tokid = sb("tokid", [P, TT])
        table_sb = sb("table_sb", [NBLK + 1, CAP])
        zero_tab = sb("zero_tab", [NBLK + 1, CAP])
        tok_i = sb("tok_i", [CAP, NBLK + 1], I32)
        idx = [sb(f"idx{i}", [CAP, 1], I32) for i in range(4)]
        psum = ctx.enter_context(nc.psum_tensor("psum", [P, 8, 512], F32))

        x_landed = sem("x_landed")
        small_landed = sem("small_landed")
        ln1_landed, ln2_landed, ax_landed = sem("ln1_landed"), sem("ln2_landed"), sem("ax_landed")
        w_landed = [sem(f"w_landed{i}") for i in range(RING)]
        const_ready, base_ready = sem("const_ready"), sem("base_ready")
        pool_step = sem("pool_step")
        abs_ready, bias_ready = sem("abs_ready"), sem("bias_ready")
        xt_done, xt_act, xt_dve = sem("xt_done"), sem("xt_act"), sem("xt_dve")
        unit_done, unit_copied = sem("unit_done"), sem("unit_copied")
        act_step, dve_step = sem("act_step"), sem("dve_step")
        css_ready, var_c_ready, rstd_c_ready, c_ready = (sem("css_ready"), sem("var_c_ready"),
                                                         sem("rstd_c_ready"), sem("c_ready"))
        c_done, c_copied = sem("c_done"), sem("c_copied")
        idx_scored, rel_ready, rel_added = sem("idx_scored"), sem("rel_ready"), sem("rel_added")
        s_done, s_taken, negm_ready, exp_done = sem("s_done"), sem("s_taken"), sem("negm_ready"), sem("exp_done")
        p_ready, pt_done, pt_copied = sem("p_ready"), sem("pt_done"), sem("pt_copied")
        pv_done, o_copied = sem("pv_done"), sem("o_copied")
        merged_read, m_ready = sem("merged_read"), sem("m_ready")
        ax_ready = sem("ax_ready")
        r_ready, mean_ready, ssq_ready, var_ready, rstd_ready, h1_ready = (
            sem("r_ready"), sem("mean_ready"), sem("ssq_ready"), sem("var_ready"), sem("rstd_ready"),
            sem("h1_ready"))
        h1_stored, h1t_done, h1t_copied = sem("h1_stored"), sem("h1t_done"), sem("h1t_copied")
        routed, gd_ready, ge_ready, md_ready, me_ready = (sem("routed"), sem("gd_ready"), sem("ge_ready"),
                                                          sem("md_ready"), sem("me_ready"))
        oh_ready, ranked, slots_ready, over_ready = (sem("oh_ready"), sem("ranked"), sem("slots_ready"),
                                                     sem("over_ready"))
        zero_ready, table_zeroed, table_set, table_loaded = (sem("zero_ready"), sem("table_zeroed"),
                                                             sem("table_set"), sem("table_loaded"))
        table_t, tok_ready = sem("table_t"), sem("tok_ready")
        ah_ready = sem("ah_ready")
        gu_landed = [sem(f"gu_landed{i}") for i in range(4)]
        d_landed = [sem(f"d_landed{i}") for i in range(4)]
        xg_landed = [sem(f"xg_landed{i}") for i in range(4)]
        idx_ready = sem("idx_ready")
        xgt_done, xgt_copied, gu_done, th_done, h_ready, ht_done, ht_copied, d_done, y_copied = (
            sem("xgt_done"), sem("xgt_copied"), sem("gu_done"), sem("th_done"), sem("h_ready"), sem("ht_done"),
            sem("ht_copied"), sem("d_done"), sem("y_copied"))
        gated_ready, rows_zeroed = sem("gated_ready"), sem("rows_zeroed")
        pe_passed, pool_passed = sem("pe_passed"), sem("pool_passed")
        y_stored = [sem(f"y_stored{i}") for i in range(2)]
        yk_landed = [[sem(f"yk_landed{i}{k}") for k in range(2)] for i in range(2)]
        r2_ready, mean2_ready, ssq2_ready, var2_ready, rstd2_ready, out_ready, out_stored = (
            sem("r2_ready"), sem("mean2_ready"), sem("ssq2_ready"), sem("var2_ready"), sem("rstd2_ready"),
            sem("out_ready"), sem("out_stored"))

        class Steps:

            def __init__(self, eng, s, count=0):
                self.eng, self.s, self.count = eng, s, count

            def __call__(self, ins):
                self.count += 1
                ins.then_inc(self.s, 1)
                self.eng.wait_ge(self.s, self.count)

        def item_shape(n):
            kind, g, t = ITEMS[n]
            if kind == "A":
                w0 = 0 if t else CHUNK
                return kind, g, t, w0, 192 - w0
            return kind, g, t, 0, P * (t + 1)

        def unit_wait(eng, u):
            before = [v for v in range(u) if bank_of(v) == bank_of(u)]
            kind = UNITS[u][0]
            if kind in ("a", "b"):
                if UNITS[u][1] >= 2:
                    eng.wait_ge(merged_read, 2 * (UNITS[u][1] - 2) + 1 + (kind == "b"))
            elif kind == "out":
                if UNITS[u][1] >= 4:
                    eng.wait_ge(r_ready, UNITS[u][1] // 2 - 1)
            elif before:
                eng.wait_ge(unit_copied, before[-1] + 1)

        block = ctx.enter_context(nc.Block())

        @block.sync
        def _(sp):
            mats = {"in": w_in, "a": w_branch_a, "b": w_branch_b, "out": w_out}

            def chunk(c):
                mat, c0, width = CHUNKS[c]
                if c >= RING:
                    sp.wait_ge(unit_done, LAST_OF_CHUNK[c - RING] + 1)
                sp.dma_start(wslot[c % RING][:, :, 0:width],
                             mats[mat][0, :, c0:c0 + width].rearrange("(k p) n -> p k n", p=P)
                             ).then_inc(w_landed[c % RING], 16)

            sp.dma_start(x_nat, x[0].rearrange("(t p) d -> p t d", p=P)).then_inc(x_landed, 16)
            for c in range(12):
                chunk(c)

            def expert(e, slot):
                sp.dma_start(ex_gu[slot][:, 0].rearrange("p k f -> p (k f)"),
                             w_gate[0, e].rearrange("(p k) f -> p (k f)", p=P)).then_inc(gu_landed[slot], 16)
                sp.dma_start(ex_gu[slot][:, 1].rearrange("p k f -> p (k f)"),
                             w_up[0, e].rearrange("(p k) f -> p (k f)", p=P)).then_inc(gu_landed[slot], 16)
                sp.dma_start(ex_d[slot].rearrange("p k n -> p (k n)"),
                             w_down[0, e].rearrange("(p k) n -> p (k n)", p=P)).then_inc(d_landed[slot], 16)

            sp.wait_ge(o_copied, len(ITEMS))
            sp.dma_start(ax, x[0].rearrange("(t p) d -> p t d", p=P)).then_inc(ax_landed, 16)
            sp.dma_start(ln1g, ln1_g[0].partition_broadcast(P)).then_inc(ln1_landed, 16)
            sp.dma_start(ln1b, ln1_b[0].partition_broadcast(P)).then_inc(ln1_landed, 16)
            for c in range(12, len(CHUNKS)):
                chunk(c)
            sp.wait_ge(m_ready, 8)
            expert(0, 0)
            expert(1, 1)
            for t in range(TT):
                sp.wait_ge(h1_ready, t + 1)
                if t == 0:
                    pass
                sp.dma_start(h1_dram[t * P:(t + 1) * P, :], h1[:, t, :]).then_inc(h1_stored, 16)
                if t == TT - 1:
                    expert(2, 2)
                    expert(3, 3)
            sp.wait_ge(routed, 1)
            sp.dma_start(ln2g, ln2_g[0].partition_broadcast(P)).then_inc(ln2_landed, 16)
            sp.dma_start(ln2b, ln2_b[0].partition_broadcast(P)).then_inc(ln2_landed, 16)
            sp.wait_ge(table_set, 16 * 2 * TT)
            sp.dma_start(table_sb[:, :], table_dram.rearrange("(b s) o -> b (s o)", s=CAP)
                         ).then_inc(table_loaded, 16)

            def store_y(b, s):
                sp.wait_ge(y_copied, b + 2)
                for half in range(2):
                    sp.dma_start(y_dram[bass.ds(b * CAP, CAP), half * 512:(half + 1) * 512],
                                 y_sb[s % 2][half * CAP:(half + 1) * CAP, :]).then_inc(y_stored[s % 2], 16)

            with sp.Fori(0, NE // 4 - 1) as i:
                for s in range(4):
                    b = i * 4 + s
                    sp.wait_ge(d_done, b + 1)
                    expert(b + 4, s)
                    store_y(b, s)
            for s in range(4):
                store_y(NE - 4 + s, s)
            sp.wait_ge(over_ready, 1)
            n_over = sp.value_load(over_i[0:1, MAX_OVER:MAX_OVER + 1], min_val=0, max_val=MAX_OVER - 1)
            with sp.If(n_over > 0):
                with sp.Fori(0, MAX_OVER // 4) as i:
                    for s in range(4):
                        b = i * 4 + (NE + s)
                        eid = sp.value_load(over_i[0:1, bass.ds(i * 4 + s, 1)], min_val=0, max_val=NE - 1)
                        sp.wait_ge(d_done, b - 3)
                        expert(eid, s)
                        store_y(b, s)
            for t in range(TT):
                sp.wait_ge(out_ready, t + 1)
                sp.dma_start(out[0, t * P:(t + 1) * P, :], h1[:, t, :]).then_inc(out_stored, 16)
            sp.wait_ge(out_stored, 16 * TT)

        @block.gpsimd
        def _(pool):
            step = Steps(pool, pool_step)
            small = [(wuk[:, :], w_uk[0]), (wuv[:, :], w_uv[0]),
                     (kvg[:, :], kv_norm_g[0].partition_broadcast(P)),
                     (rw[:, :, 0:NG], rg_w[0].rearrange("(k p) g -> p k g", p=P)),
                     (rw[:, :, NG:], re_w[0].rearrange("(k p) g e -> p k (g e)", p=P)),
                     (rb[:, 0:NG], rg_b[0].partition_broadcast(P)),
                     (rb[:, NG:], re_b[0].rearrange("g e -> (g e)").partition_broadcast(P))]
            small.append((sinks_row[:, :], a_sinks[0].partition_broadcast(P)))
            nc.gpsimd.memset(ident[:, :], 0.0).then_inc(pool_step, 1)
            nc.gpsimd.memset(ones[:, :], 1.0).then_inc(pool_step, 1)
            step.count = 2
            pool.wait_ge(pool_step, 2)
            nc.gpsimd.affine_select(out=ident[:, :], in_=ident[:, :], compare_op=ALU.not_equal, fill=1.0, base=0,
                                    pattern=[[-1, P]], channel_multiplier=1).then_inc(const_ready, 1)
            for dst, src in small:
                pool.dma_start(dst, src).then_inc(small_landed, 16)
            nc.gpsimd.affine_select(out=upper[:, :], in_=ones[:, :], compare_op=ALU.is_gt, fill=0.0, base=0,
                                    pattern=[[1, P]], channel_multiplier=-1).then_inc(const_ready, 1)
            nc.gpsimd.iota(negd, [[1, 512]], base=-384, channel_multiplier=-1,
                           allow_small_or_imprecise_dtypes=True).then_inc(const_ready, 1)
            nc.gpsimd.iota(desc[:, :], [[-1, NE]], base=NE, channel_multiplier=0,
                           allow_small_or_imprecise_dtypes=True).then_inc(const_ready, 1)
            nc.gpsimd.iota(base0[:, :], [[CAP, NE]], base=0, channel_multiplier=0,
                           allow_small_or_imprecise_dtypes=True).then_inc(const_ready, 1)
            nc.gpsimd.iota(jrow[:, :], [[1, MAX_OVER]], base=0, channel_multiplier=0,
                           allow_small_or_imprecise_dtypes=True).then_inc(const_ready, 1)
            nc.gpsimd.iota(tokid[:, :], [[P, TT]], base=0, channel_multiplier=1,
                           allow_small_or_imprecise_dtypes=True).then_inc(const_ready, 1)
            nc.gpsimd.memset(half_neg[:, :], -0.5).then_inc(const_ready, 1)
            nc.gpsimd.memset(zero_tab[:, :], 0.0).then_inc(zero_ready, 1)
            nc.gpsimd.memset(pt_sb[1], 0.0).then_inc(zero_ready, 1)
            pool.wait_ge(zero_ready, 2)
            pool.dma_start(y_dram[NE * CAP:, :].rearrange("(p r) d -> p r d", p=P),
                           pt_sb[1].unsqueeze(1).to_broadcast([P, MAX_OVER * CAP // P, D])).then_inc(rows_zeroed, 16)
            pool.dma_start(table_dram.rearrange("(b s) o -> b (s o)", s=CAP), zero_tab[:, :]
                           ).then_inc(table_zeroed, 16)
            pool.wait_ge(base_ready, 1)
            for q in range(4):
                for par in range(2):
                    for i in range(2):
                        ins = nc.gpsimd.tensor_scalar(biasA[:, q, 2 * par + i, :], rel[0][:, 0:192],
                                                      SLOPE[4 * q + 2 * i + par], None, ALU.mult)
                        ins.then_inc(bias_ready, 1)
            pool.wait_ge(small_landed, 16 * 8)
            for q in range(4):
                nc.gpsimd.tensor_copy(sinks[:, q, :].rearrange("p (r i) -> p r i", r=2),
                                      sinks_row[:, 4 * q:4 * q + 4].rearrange("p (i r) -> p r i", r=2)
                                      ).then_inc(bias_ready, 1)
            pool.wait_ge(const_ready, 8)
            pool.wait_ge(var_c_ready, 1)
            nc.gpsimd.tensor_tensor(rstd_c[:, :], css[:, 4:8], half_neg[:, :], ALU.pow).then_inc(rstd_c_ready, 1)
            for t in range(TT):
                pool.wait_ge(var_ready, t + 1)
                nc.gpsimd.tensor_tensor(ln[:, 0, 4, t:t + 1], ln[:, 0, 3, t:t + 1], half_neg[:, 0:1], ALU.pow
                                        ).then_inc(rstd_ready, 1)
            pool.wait_ge(table_zeroed, 16)
            pool.wait_ge(slots_ready, 1)
            for k in range(2):
                for t in range(TT):
                    pool.indirect_dma_start(out=table_dram, out_offset=bass.IndirectOffsetOnAxis(
                        ap=slot_i[:, k, t:t + 1], axis=0), in_=tokid[:, t:t + 1], in_offset=None
                        ).then_inc(table_set, 16)
            pool.wait_ge(tok_ready, 1)
            pool.wait_ge(h1_stored, 16 * TT)

            def gather(b, s, n):
                nc.gpsimd.tensor_copy(idx[s][:, :], tok_i[:, bass.ds(b, 1)]).then_inc(idx_ready, 1)
                pool.wait_ge(idx_ready, n + 1)
                pool.sem_inc(pool_passed, 1)
                pool.indirect_dma_start(out=xg[s][0:CAP, :], out_offset=None, in_=h1_dram,
                                        in_offset=bass.IndirectOffsetOnAxis(ap=idx[s][:, 0:1], axis=0)
                                        ).then_inc(xg_landed[s], 16)

            for b in range(4):
                gather(b, b, b)
            with pool.Fori(0, NE // 4 - 1) as i:
                for s in range(4):
                    b = i * 4 + (4 + s)
                    pool.wait_ge(xgt_done, b - 3)
                    gather(b, s, b)
            pool.wait_ge(xgt_done, NE - 3)
            gather(NE, 0, NE)
            pool.wait_ge(over_ready, 1)
            n_over = pool.value_load(over_i[0:1, MAX_OVER:MAX_OVER + 1], min_val=0, max_val=MAX_OVER - 1)
            for p in range(2):
                pool.wait_ge(y_stored[p], 32 * NE // 2 + 1)
            with pool.If(n_over > 0):
                with pool.Fori(0, MAX_OVER // 4) as i:
                    for s in range(4):
                        b = i * 4 + (NE + 1 + s)
                        pool.wait_ge(xgt_done, b - 3)
                        gather(b, (s + 1) % 4, b)
                for p in range(2):
                    pool.wait_ge(y_stored[p], 32 * NBLK // 2 + 1)
            for t in range(TT):
                for k in range(2):
                    if t >= 2:
                        pool.wait_ge(r2_ready, t - 1)
                    pool.indirect_dma_start(out=yk[t % 2][k], out_offset=None, in_=y_dram,
                                            in_offset=bass.IndirectOffsetOnAxis(ap=slot_i[:, k, t:t + 1], axis=0)
                                            ).then_inc(yk_landed[t % 2][k], 16)
                if t >= 1:
                    pool.wait_ge(var2_ready, t)
                    nc.gpsimd.tensor_tensor(ln[:, 1, 4, t - 1:t], ln[:, 1, 3, t - 1:t], half_neg[:, 0:1], ALU.pow
                                            ).then_inc(rstd2_ready, 1)
            pool.wait_ge(var2_ready, TT)
            nc.gpsimd.tensor_tensor(ln[:, 1, 4, TT - 1:TT], ln[:, 1, 3, TT - 1:TT], half_neg[:, 0:1], ALU.pow
                                    ).then_inc(rstd2_ready, 1)

        @block.tensor
        def _(pe):
            pe.wait_ge(const_ready, 1)
            pe.wait_ge(x_landed, 16)
            for t in range(TT):
                for h in range(2):
                    n = 2 * t + h
                    if n >= 6:
                        pe.wait_ge(xt_act if n % 2 == 0 else xt_dve, (n - 6) // 2 + 1)
                    for k in range(4):
                        ins = nc.tensor.transpose(psum[:, n % 6, k * P:(k + 1) * P],
                                                  x_nat[:, t, (4 * h + k) * P:(4 * h + k + 1) * P], ident[:, :])
                    ins.then_inc(xt_done, 1)
            pe.wait_ge(xt_act, TT)
            pe.wait_ge(xt_dve, TT)

            def unit(u, k0=0, k1=DT):
                kind, i, c, col = UNITS[u]
                w = wslot[c % RING]
                if k0 == 0:
                    pe.wait_ge(w_landed[c % RING], 16 * (c // RING + 1))
                    unit_wait(pe, u)
                ps = psum[:, bank_of(u), :]
                if kind in ("ckv", "va", "wi"):
                    n = {"ckv": RANK, "va": AG * HD, "wi": IH}[kind]
                    for t in range(TT):
                        for k in range(DT):
                            ins = nc.tensor.matmul(ps[:, t * n:(t + 1) * n], xT[:, k, t * P:(t + 1) * P],
                                                   w[:, k, col:col + n], start=k == 0, stop=k == DT - 1)
                elif kind == "out":
                    t = i // 2
                    for k in range(DT):
                        ins = nc.tensor.matmul(ps, gaT[:, k, t * P:(t + 1) * P], w[:, k, :],
                                               start=k == 0, stop=k == DT - 1)
                else:
                    m = HD if kind == "ki" else P
                    src = {"a": qaT, "b": qbT}.get(kind, xT)
                    for k in range(k0, k1):
                        ins = nc.tensor.matmul(ps[0:m, :], w[:, k, col:col + m], src[:, k, :],
                                               start=k == 0, stop=k == DT - 1)
                if k1 == DT:
                    ins.then_inc(unit_done, 1)

            for u in range(UNIT["wi", 0] + 1):
                unit(u)
            pe.wait_ge(unit_copied, UNIT["ki", 0] + 1)
            n = 0
            for t in range(1, TT):
                for h in range(IH):
                    if n >= 4:
                        pe.wait_ge(rel_ready, n - 3)
                    r = slice(HD * (h % 2), HD * (h % 2) + HD)
                    nc.tensor.matmul(psum[:, n % 4, 0:P * (t + 1)], qiT[r, h // 2, t * P:(t + 1) * P],
                                     kiT[r, 0:P * (t + 1)], start=True, stop=True).then_inc(idx_scored, 1)
                    n += 1
            pe.wait_ge(c_ready, TT)
            for t in range(TT):
                ins = nc.tensor.transpose(psum[:, 4, t * P:(t + 1) * P], c_nat[:, t, :], ident[:, :])
            ins.then_inc(c_done, 1)
            pe.wait_ge(c_copied, 1)
            pe.wait_ge(small_landed, 16 * 8)
            nc.tensor.matmul(psum[0:HD, 5, :], wuk[:, :], cT, start=True, stop=True).then_inc(c_done, 1)
            for t in range(TT):
                ins = nc.tensor.matmul(psum[:, 4, t * HD:(t + 1) * HD], cT[:, t * P:(t + 1) * P], wuv[:, :],
                                       start=True, stop=True)
            ins.then_inc(c_done, 1)
            for u in range(UNIT["ka", 0], UNIT["qa", 7] + 1):
                unit(u)

            def scores(n):
                kind, g, t, w0, w = item_shape(n)
                if n >= 2:
                    pe.wait_ge(s_taken, n - 1)
                if n == 0:
                    pe.wait_ge(rel_ready, 3 * IH)
                if kind == "A":
                    pe.wait_ge(unit_copied, UNIT["qa", 2 * g + 1] + 1)
                else:
                    pe.wait_ge(unit_copied, UNIT["qb", g] + 1)
                for i in range(2 if kind == "A" else 1):
                    for par in range(2):
                        r = slice(HD * par, HD * par + HD)
                        if kind == "A":
                            q, k = qaT[r, 2 * g + i, t * P:(t + 1) * P], kaT[r, g // 2, P * t - CHUNK + w0:P * (t + 1)]
                        else:
                            q, k = qbT[r, g, t * P:(t + 1) * P], kbT[r, 0:w]
                        ins = nc.tensor.matmul(psum[:, 2 * (n % 2) + par, 256 * i:256 * i + w], q, k,
                                               start=True, stop=True)
                ins.then_inc(s_done, 1)

            def turn(n):
                kind, g, t, w0, w = item_shape(n)
                pe.wait_ge(p_ready, n + 1)
                if n >= 1:
                    pe.wait_ge(pt_copied, n)
                else:
                    pe.wait_ge(c_copied, 3)
                if kind == "A":
                    s = s_sb[n % 2][:, 0:4 * w].rearrange("p (h w) -> p h w", h=4)
                    for h in range(4):
                        ins = nc.tensor.transpose(psum[:, 4, h * P:(h + 1) * P], s[:, h, w - P:w], ident[:, :])
                    if t:
                        for h in range(4):
                            ins = nc.tensor.transpose(psum[0:CHUNK, 5, h * P:(h + 1) * P], s[:, h, 0:CHUNK],
                                                      ident[:, :])
                else:
                    s = s_sb[n % 2][:, 0:2 * w].rearrange("p (h w) -> p h w", h=2)
                    for kt in range(t + 1):
                        for par in range(2):
                            c = (kt % 2) * 256 + par * P
                            ins = nc.tensor.transpose(psum[:, 4 + kt // 2, c:c + P], s[:, par, kt * P:(kt + 1) * P],
                                                      ident[:, :])
                ins.then_inc(pt_done, 1)

            def values(n):
                kind, g, t, w0, w = item_shape(n)
                pe.wait_ge(pt_copied, n + 1)
                if n >= 1:
                    pe.wait_ge(o_copied, n)
                pt = pt_sb[n % 2]
                if kind == "A":
                    kv = slice(HD * (g // 2), HD * (g // 2) + HD)
                    for par in range(2):
                        ins = nc.tensor.matmul(psum[HD * par:HD * par + HD, 7, 0:256], va[:, t, kv],
                                               pt[:, 256 * par:256 * par + 256], start=True, stop=t == 0)
                    if t:
                        for par in range(2):
                            ins = nc.tensor.matmul(psum[HD * par:HD * par + HD, 7, 0:256], va_hi[0:CHUNK, t - 1, kv],
                                                   pt[0:CHUNK, 512 + 256 * par:512 + 256 * par + 256],
                                                   start=False, stop=True)
                else:
                    for kt in range(t + 1):
                        for par in range(2):
                            c = 256 * kt + P * par
                            ins = nc.tensor.matmul(psum[HD * par:HD * par + HD, 7, 0:P], vb[:, kt, :],
                                                   pt[:, c:c + P], start=kt == 0, stop=kt == t)
                ins.then_inc(pv_done, 1)

            pe.wait_ge(unit_copied, UNIT["qa", 7] + 1)
            scores(0)
            for n in range(len(ITEMS)):
                if n + 1 < len(ITEMS):
                    scores(n + 1)
                u, k = UNIT["qb", 0] + n // 2, 4 * (n % 2)
                unit(u, k, k + 2)
                turn(n)
                unit(u, k + 2, k + 4)
                if n >= 1:
                    values(n - 1)
            values(len(ITEMS) - 1)

            pe.wait_ge(o_copied, len(ITEMS))
            for u in range(UNIT["a", 0], UNIT["out", 0]):
                unit(u)
            pe.wait_ge(m_ready, 8)

            def turn_h1(t):
                pe.wait_ge(h1_ready, t + 1)
                for h in range(2):
                    n = 2 * t + h
                    if n >= 2:
                        pe.wait_ge(h1t_copied, n - 1)
                    for k in range(4):
                        ins = nc.tensor.transpose(psum[:, n % 2, k * P:(k + 1) * P],
                                                  h1[:, t, (4 * h + k) * P:(4 * h + k + 1) * P], ident[:, :])
                    ins.then_inc(h1t_done, 1)

            for t in range(TT):
                unit(UNIT["out", 2 * t])
                unit(UNIT["out", 2 * t + 1])
                if t:
                    turn_h1(t - 1)
            turn_h1(TT - 1)
            pe.wait_ge(h1t_copied, 2 * TT)
            for t in range(TT):
                for k in range(DT):
                    ins = nc.tensor.matmul(psum[:, 2, t * (NG + NE):(t + 1) * (NG + NE)], h1T[:, k, t * P:(t + 1) * P],
                                           rw[:, k, :], start=k == 0, stop=k == DT - 1)
            ins.then_inc(routed, 1)
            pe.wait_ge(oh_ready, 1)
            pe.wait_ge(const_ready, 8)
            for t in range(TT + 1):
                for v in range(min(t + 1, TT)):
                    ins = nc.tensor.matmul(psum[:, 3, t * NE:(t + 1) * NE], (upper if v == t else ones)[:, :],
                                           oh[:, 2, v, :], start=v == 0, stop=v == min(t, TT - 1))
            ins.then_inc(ranked, 1)
            pe.wait_ge(table_loaded, 16)
            nc.tensor.transpose(psum[0:CAP, 0, 0:NBLK + 1], table_sb[:, :], ident[0:NBLK + 1, 0:NBLK + 1]
                                ).then_inc(table_t, 1)

            def turn_x(b, s, use):
                pe.wait_ge(xg_landed[s], use * 16 + 16)
                pe.sem_inc(pe_passed, 1)
                rows = xg[s][0:CAP, :].rearrange("s (p k) -> s k p", k=DT)
                for k in range(DT):
                    ins = nc.tensor.transpose(psum[:, 0, k * CAP:(k + 1) * CAP], rows[:, k, :],
                                              ident[0:CAP, 0:CAP])
                ins.then_inc(xgt_done, 1)

            def expert(b, i, s):
                pe.wait_ge(gu_landed[s], i * 32 + 32)
                pe.wait_ge(xgt_copied, b + 1)
                for k in range(DT):
                    for g in range(2):
                        ins = nc.tensor.matmul(psum[CAP * g:CAP * g + CAP, 2 + s % 2, 0:FF], xgT[s % 2][:, k, :],
                                               ex_gu[s][:, g, k, :], start=k == 0, stop=k == DT - 1)
                ins.then_inc(gu_done, 1)
                turn_x(b + 1, (s + 1) % 4, i + (s + 1) // 4)
                pe.wait_ge(h_ready, b + 1)
                pe.sem_inc(pe_passed, 1)
                rows = hid[s % 2][0:CAP, :].rearrange("s (p k) -> s k p", k=2)
                for k in range(2):
                    ins = nc.tensor.transpose(psum[:, 1, k * CAP:(k + 1) * CAP], rows[:, k, :],
                                              ident[0:CAP, 0:CAP])
                ins.then_inc(ht_done, 1)
                pe.wait_ge(ht_copied, b + 1)
                pe.wait_ge(d_landed[s], i * 16 + 16)
                pe.wait_ge(y_copied, b + 1)
                for k in range(2):
                    for half in range(2):
                        ins = nc.tensor.matmul(psum[CAP * half:CAP * half + CAP, 4 + s % 2, :], hidT[s % 2][:, k, :],
                                               ex_d[s][:, k, 512 * half:512 * half + 512], start=k == 0, stop=k == 1)
                ins.then_inc(d_done, 1)

            pe.wait_ge(tok_ready, 1)
            turn_x(0, 0, 0)
            with pe.Fori(0, NE // 4) as i:
                for s in range(4):
                    expert(i * 4 + s, i, s)
            pe.wait_ge(over_ready, 1)
            n_over = pe.value_load(over_i[0:1, MAX_OVER:MAX_OVER + 1], min_val=0, max_val=MAX_OVER - 1)
            with pe.If(n_over > 0):
                with pe.Fori(NE // 4, NBLK // 4) as i:
                    for s in range(4):
                        expert(i * 4 + s, i, s)

        @block.scalar
        def _(act):
            step = Steps(act, act_step)
            act.wait_ge(const_ready, 3)
            step(nc.scalar.activation(negd, negd, ACT.Abs))
            nc.scalar.activation(negd, negd, ACT.Copy, scale=-1.0).then_inc(abs_ready, 1)
            for n in range(0, 2 * TT, 2):
                act.wait_ge(xt_done, n + 1)
                t, h = n // 2, n % 2
                nc.scalar.activation(xT[:, 4 * h:4 * h + 4, t * P:(t + 1) * P],
                                     psum[:, n % 6, :].rearrange("p (k c) -> p k c", k=4), ACT.Copy
                                     ).then_inc(xt_act, 1)

            def copy_unit(u):
                kind, i, _, _ = UNITS[u]
                act.wait_ge(unit_done, u + 1)
                ps = psum[:, bank_of(u), :]
                if kind == "ckv":
                    ins = nc.scalar.activation(c_nat, ps.rearrange("p (t c) -> p t c", t=TT), ACT.Copy)
                elif kind == "qi":
                    ins = nc.scalar.activation(qiT[:, i, :], ps, ACT.Copy)
                elif kind == "ki":
                    nc.scalar.activation(kiT[0:HD, :], ps[0:HD, :], ACT.Copy)
                    ins = nc.scalar.activation(kiT[HD:P, :], ps[0:HD, :], ACT.Copy)
                elif kind == "wi":
                    ins = nc.scalar.activation(wis[:, :, :], ps[:, 0:TT * IH].rearrange("p (t c) -> p t c", t=TT),
                                               ACT.Copy, scale=IDX_SCALE)
                elif kind == "ka":
                    for g in range(AG):
                        for half in range(2):
                            ins = nc.scalar.activation(kaT[HD * half:HD * half + HD, g, :],
                                                       ps[HD * g:HD * g + HD, :], ACT.Copy)
                elif kind == "va":
                    v = ps.rearrange("p (t c) -> p t c", t=TT)
                    nc.scalar.activation(va, v, ACT.Copy)
                    ins = nc.scalar.activation(va_hi[0:CHUNK], v[CHUNK:P], ACT.Copy)
                elif kind in ("qa", "qb"):
                    ins = nc.scalar.activation((qaT if kind == "qa" else qbT)[:, i, :], ps, ACT.Copy,
                                               scale=HD ** -0.5)
                else:
                    ins = nc.scalar.activation((gaT if i < 8 else gbT)[:, i % 8, :], ps, ACT.Tanh, scale=0.5)
                ins.then_inc(unit_copied, 1)

            copy_unit(0)
            act.wait_ge(unit_copied, 1)
            for t in range(TT):
                nc.scalar.activation(rel[1][:, t * P:(t + 1) * P], c_nat[:, t, :], ACT.Square,
                                     accum_out=css[:, t:t + 1]).then_inc(css_ready, 1)
            for u in range(1, UNIT["wi", 0] + 1):
                copy_unit(u)
            n = 0
            act.wait_ge(bias_ready, 16)
            for t in range(1, TT):
                for h in range(IH):
                    act.wait_ge(idx_scored, n + 1)
                    if n >= 2:
                        act.wait_ge(rel_added, n - 1)
                    elif n == 1:
                        act.wait_ge(css_ready, TT)
                    nc.scalar.activation(rel[n % 2][:, 0:P * (t + 1)], psum[:, n % 4, 0:P * (t + 1)], ACT.Relu
                                         ).then_inc(rel_ready, 1)
                    n += 1
            act.wait_ge(c_done, 1)
            nc.scalar.activation(cT, psum[:, 4, :], ACT.Copy).then_inc(c_copied, 1)
            act.wait_ge(c_done, 2)
            nc.scalar.activation(kbT[0:HD, :], psum[0:HD, 5, :], ACT.Copy)
            nc.scalar.activation(kbT[HD:P, :], psum[0:HD, 5, :], ACT.Copy).then_inc(c_copied, 1)
            act.wait_ge(c_done, 3)
            nc.scalar.activation(vb, psum[:, 4, 0:TT * HD].rearrange("p (t c) -> p t c", t=TT), ACT.Copy
                                 ).then_inc(c_copied, 1)
            for u in range(UNIT["ka", 0], UNIT["qa", 7] + 1):
                copy_unit(u)

            def exps(n):
                kind, g, t, w0, w = item_shape(n)
                heads = 4 if kind == "A" else 2
                s = s_sb[n % 2][:, 0:heads * w].rearrange("p (h w) -> p h w", h=heads)
                act.wait_ge(negm_ready, n + 1)
                for h in range(heads):
                    ins = nc.scalar.activation(s[:, h, :], s[:, h, :], ACT.Exp, bias=negm[:, n, h:h + 1],
                                               accum_out=den[:, n, h:h + 1])
                if kind == "A":
                    ins = nc.scalar.activation(sink_e[:, n, :], sink_e[:, n, :], ACT.Exp)
                ins.then_inc(exp_done, 1)

            def copy_pt(n):
                kind, g, t, w0, w = item_shape(n)
                act.wait_ge(pt_done, n + 1)
                if n >= 2:
                    act.wait_ge(pv_done, n - 1)
                pt = pt_sb[n % 2]
                if kind == "A":
                    ins = nc.scalar.activation(pt[:, 0:512], psum[:, 4, :], ACT.Copy)
                    if t:
                        ins = nc.scalar.activation(pt[0:CHUNK, 512:1024], psum[0:CHUNK, 5, :], ACT.Copy)
                else:
                    ins = nc.scalar.activation(pt[:, 0:256 * (t + 1)],
                                               psum[:, 4:6, :].rearrange("p b c -> p (b c)")[:, 0:256 * (t + 1)],
                                               ACT.Copy)
                ins.then_inc(pt_copied, 1)

            def copy_o(n):
                kind, g, t, w0, w = item_shape(n)
                act.wait_ge(pv_done, n + 1)
                if kind == "A":
                    ins = nc.scalar.activation(qaT[:, 2 * g:2 * g + 2, t * P:(t + 1) * P],
                                               psum[:, 7, 0:256].rearrange("p (i c) -> p i c", i=2), ACT.Copy)
                else:
                    ins = nc.scalar.activation(qbT[:, g, t * P:(t + 1) * P], psum[:, 7, 0:P], ACT.Copy)
                ins.then_inc(o_copied, 1)

            act.wait_ge(rows_zeroed, 16)
            exps(0)
            for n in range(len(ITEMS)):
                if n + 1 < len(ITEMS):
                    exps(n + 1)
                copy_pt(n)
                if n % 2:
                    copy_unit(UNIT["qb", 0] + n // 2)
                if n >= 1:
                    copy_o(n - 1)
            copy_o(len(ITEMS) - 1)

            act.wait_ge(ax_landed, 16)
            nc.scalar.activation(ax, ax, ACT.Copy, scale=ALPHA).then_inc(ax_ready, 1)

            def squares(i, t, ready, done):
                act.wait_ge(ready, t + 1)
                nc.scalar.activation(junk, h1[:, t, :], ACT.Square, bias=ln[:, i, 1, t:t + 1],
                                     accum_out=ln[:, i, 2, t:t + 1]).then_inc(done, 1)

            def copy_h1t(t):
                for h in range(2):
                    n = 2 * t + h
                    act.wait_ge(h1t_done, n + 1)
                    nc.scalar.activation(h1T[:, 4 * h:4 * h + 4, t * P:(t + 1) * P],
                                         psum[:, n % 2, :].rearrange("p (k c) -> p k c", k=4), ACT.Copy
                                         ).then_inc(h1t_copied, 1)

            junk = qbT.rearrange("p k c -> p (k c)")[:, 0:D]
            for t in range(TT):
                squares(0, t, mean_ready, ssq_ready)
                if t:
                    copy_h1t(t - 1)
            copy_h1t(TT - 1)
            act.wait_ge(gd_ready, 1)
            nc.scalar.activation(g4[:, 1], g4[:, 0], ACT.Exp).then_inc(ge_ready, 1)
            act.wait_ge(md_ready, 1)
            nc.scalar.activation(g1[:, 6, :], g1[:, 5, :], ACT.Exp).then_inc(me_ready, 1)
            act.wait_ge(h1_stored, 16 * TT)
            for t in range(TT):
                nc.scalar.activation(h1[:, t, :], h1[:, t, :], ACT.Copy, scale=ALPHA).then_inc(ah_ready, 1)

            def copy_xgt(n, s):
                act.wait_ge(xgt_done, n + 1)
                nc.scalar.activation(xgT[s % 2], psum[:, 0, :].rearrange("p (k c) -> p k c", k=DT), ACT.Copy
                                     ).then_inc(xgt_copied, 1)

            def expert(b, i, s):
                act.wait_ge(gu_done, b + 1)
                nc.scalar.activation(th[s % 2][0:CAP, :], psum[0:CAP, 2 + s % 2, 0:FF], ACT.Tanh, scale=0.5
                                     ).then_inc(th_done, 1)
                copy_xgt(b + 1, s + 1)
                act.wait_ge(d_done, b + 1)
                act.wait_ge(y_stored[s % 2], i * 64 + (32 * (s // 2) + 1))
                nc.scalar.activation(y_sb[s % 2], psum[:, 4 + s % 2, :], ACT.Copy).then_inc(y_copied, 1)

            act.sem_inc(y_copied, 1)
            for p in range(2):
                act.sem_inc(y_stored[p], 1)
            copy_xgt(0, 0)
            with act.Fori(0, NE // 4) as i:
                for s in range(4):
                    expert(i * 4 + s, i, s)
            act.wait_ge(over_ready, 1)
            n_over = act.value_load(over_i[0:1, MAX_OVER:MAX_OVER + 1], min_val=0, max_val=MAX_OVER - 1)
            with act.If(n_over > 0):
                with act.Fori(NE // 4, NBLK // 4) as i:
                    for s in range(4):
                        expert(i * 4 + s, i, s)
            for t in range(TT):
                squares(1, t, mean2_ready, ssq2_ready)

        @block.vector
        def _(dve):
            step = Steps(dve, dve_step)
            V = nc.vector
            for n in range(1, 2 * TT, 2):
                dve.wait_ge(xt_done, n + 1)
                t, h = n // 2, n % 2
                V.tensor_copy(xT[:, 4 * h:4 * h + 4, t * P:(t + 1) * P],
                              psum[:, n % 6, :].rearrange("p (k c) -> p k c", k=4)).then_inc(xt_dve, 1)
            dve.wait_ge(abs_ready, 1)
            dve.wait_ge(xt_done, 2 * TT)
            step(V.tensor_copy(rel[0][:, 0:192], negd[:, 320:512]))
            V.memset(rel[0][0:CHUNK, 128:192], MASKED).then_inc(dve_step, 1)
            V.memset(rel[0][CHUNK:P, 0:CHUNK], MASKED).then_inc(base_ready, 1)
            step.count += 1
            dve.wait_ge(dve_step, step.count)
            step(V.tensor_copy(dm[0], negd[:, 384:512]))
            step(V.memset(dm[0][0:CHUNK, CHUNK:P], MASKED))
            dve.wait_ge(css_ready, TT)
            V.tensor_scalar(css[:, 4:8], css[:, 0:4], 1.0 / RANK, RMS_EPS, ALU.mult, ALU.add).then_inc(var_c_ready, 1)
            dve.wait_ge(rstd_c_ready, 1)
            dve.wait_ge(small_landed, 16 * 8)
            for t in range(TT):
                V.scalar_tensor_tensor(c_nat[:, t, :], c_nat[:, t, :], rstd_c[:, t:t + 1], kvg[:, :],
                                       ALU.mult, ALU.mult).then_inc(c_ready, 1)
            dve.wait_ge(unit_copied, UNIT["wi", 0] + 1)
            n = 0
            for t in range(1, TT):
                w = P * (t + 1)
                for h in range(IH):
                    dve.wait_ge(rel_ready, n + 1)
                    if h:
                        dve.wait_ge(rel_added, n)
                        ins = V.scalar_tensor_tensor(work[t], rel[n % 2][:, 0:w], wis[:, t, h:h + 1], work[t],
                                                     ALU.mult, ALU.add)
                    else:
                        ins = V.tensor_scalar(work[t], rel[n % 2][:, 0:w], wis[:, t, 0:1], None, ALU.mult)
                    ins.then_inc(rel_added, 1)
                    n += 1
            dve.wait_ge(rel_added, n)
            for t in range(1, TT):
                w = P * (t + 1)
                step(V.memset(work[t][0:CHUNK, w - CHUNK:w], OUT_OF_REACH))
                for _ in range(TOPK // 8):
                    step(V.max(m8[:, t - 1, :], work[t]))
                    step(V.match_replace(work[t], m8[:, t - 1, :], work[t], TAKEN))
                step(V.tensor_scalar(work[t], work[t], 2 * OUT_OF_REACH, MASKED, ALU.is_gt, ALU.mult))
                step(V.tensor_tensor(dm[t], work[t], negd[:, 512 - w:512], ALU.add))

            def soften(n):
                kind, g, t, w0, w = item_shape(n)
                heads = 4 if kind == "A" else 2
                s = s_sb[n % 2][:, 0:heads * w].rearrange("p (h w) -> p h w", h=heads)
                dve.wait_ge(s_done, n + 1)
                if n >= 2:
                    dve.wait_ge(pt_done, n - 1)
                if kind == "A":
                    V.tensor_tensor(s.rearrange("p (r i) w -> p r i w", r=2),
                                    psum[:, 2 * (n % 2):2 * (n % 2) + 2, :].rearrange("p r (i c) -> p r i c", i=2)
                                    [:, :, :, 0:w],
                                    biasA[:, g, :, w0:192].rearrange("p (r i) w -> p r i w", r=2), ALU.add
                                    ).then_inc(s_taken, 1)
                else:
                    for par in range(2):
                        ins = V.scalar_tensor_tensor(s[:, par, :], dm[t], SLOPE[2 * g + par],
                                                     psum[:, 2 * (n % 2) + par, 0:w], ALU.mult, ALU.add)
                    ins.then_inc(s_taken, 1)
                dve.wait_ge(s_taken, n + 1)
                step(V.tensor_reduce(mx[:, n, 0:heads], s, AX.X, ALU.max))
                if kind == "A":
                    step(V.tensor_tensor(mx[:, n, :], mx[:, n, :], sinks[:, g, :], ALU.max))
                    step(V.tensor_tensor(sink_e[:, n, :], sinks[:, g, :], mx[:, n, :], ALU.subtract))
                V.tensor_scalar(negm[:, n, 0:heads], mx[:, n, 0:heads], -1.0, None, ALU.mult).then_inc(negm_ready, 1)

            def normalise(n):
                kind, g, t, w0, w = item_shape(n)
                heads = 4 if kind == "A" else 2
                s = s_sb[n % 2][:, 0:heads * w].rearrange("p (h w) -> p h w", h=heads)
                dve.wait_ge(exp_done, n + 1)
                if kind == "A":
                    step(V.tensor_tensor(den[:, n, :], den[:, n, :], sink_e[:, n, :], ALU.add))
                step(V.reciprocal(mx[:, n, 0:heads], den[:, n, 0:heads]))
                for h in range(heads):
                    ins = V.tensor_scalar(s[:, h, :], s[:, h, :], mx[:, n, h:h + 1], None, ALU.mult)
                ins.then_inc(p_ready, 1)

            dve.wait_ge(bias_ready, 20)
            for n in range(len(ITEMS)):
                soften(n)
                normalise(n)

            dve.wait_ge(unit_copied, UNIT["gate", 15] + 1)
            for m in range(8):
                for kind, g in (("a", gaT), ("b", gbT)):
                    u = UNIT[kind, m]
                    dve.wait_ge(unit_done, u + 1)
                    V.scalar_tensor_tensor(g[:, m, :], g[:, m, :], 1.0, psum[:, bank_of(u), :], ALU.add, ALU.mult
                                           ).then_inc(merged_read, 1)
                dve.wait_ge(merged_read, 2 * m + 2)
                V.tensor_tensor(gaT[:, m, :], gaT[:, m, :], gbT[:, m, :], ALU.add).then_inc(m_ready, 1)

            def norm(i, t, read, mean, ssq, var, rstd, g, b, ready):
                V.tensor_scalar(ln[:, i, 1, t:t + 1], ln[:, i, 0, t:t + 1], -1.0 / D, None, ALU.mult
                                ).then_inc(mean, 1)
                dve.wait_ge(ssq, t + 1)
                V.tensor_scalar(ln[:, i, 3, t:t + 1], ln[:, i, 2, t:t + 1], 1.0 / D, LN_EPS, ALU.mult, ALU.add
                                ).then_inc(var, 1)
                dve.wait_ge(rstd, t + 1)
                step(V.tensor_scalar(h1[:, t, :], h1[:, t, :], ln[:, i, 1, t:t + 1], ln[:, i, 4, t:t + 1],
                                     ALU.add, ALU.mult))
                step(V.tensor_tensor(h1[:, t, :], h1[:, t, :], g, ALU.mult))
                V.tensor_tensor(h1[:, t, :], h1[:, t, :], b, ALU.add).then_inc(ready, 1)

            dve.wait_ge(ax_ready, 1)
            dve.wait_ge(ln1_landed, 32)
            for t in range(TT):
                u = UNIT["out", 2 * t + 1]
                dve.wait_ge(unit_done, u + 1)
                V.scalar_tensor_tensor(h1[:, t, :], psum[:, bank_of(u) - 1:bank_of(u) + 1, :].rearrange(
                    "p b c -> p (b c)"), 0.5, ax[:, t, :], ALU.mult, ALU.add, accum_out=ln[:, 0, 0, t:t + 1]
                    ).then_inc(r_ready, 1)
                dve.wait_ge(r_ready, t + 1)
                norm(0, t, r_ready, mean_ready, ssq_ready, var_ready, rstd_ready, ln1g, ln1b, h1_ready)

            N36 = NG + NE
            dve.wait_ge(routed, 1)
            step(V.tensor_tensor(lg[:, :, :], psum[:, 2, 0:TT * N36].rearrange("p (t c) -> p t c", t=TT),
                                 rb[:, :].unsqueeze(1).to_broadcast([P, TT, N36]), ALU.add))

            def row(v):
                return v.unsqueeze(2)

            gl = lg[:, :, 0:NG]
            step(V.tensor_reduce(g1[:, 0, :], gl, AX.X, ALU.max))
            V.tensor_tensor(g4[:, 0], gl, row(g1[:, 0, :]).to_broadcast([P, TT, NG]), ALU.subtract
                            ).then_inc(gd_ready, 1)

            def first_best(dst, score, best, v, m, n):
                step(V.tensor_tensor(v, score, row(best).to_broadcast([P, TT, n]), ALU.is_equal))
                step(V.tensor_tensor(v, v, desc[:, 0:n].unsqueeze(1).to_broadcast([P, TT, n]), ALU.mult))
                step(V.tensor_reduce(m, v, AX.X, ALU.max))
                step(V.tensor_tensor(dst, v, row(m).to_broadcast([P, TT, n]), ALU.is_equal))

            first_best(g4[:, 3], gl, g1[:, 0, :], g4[:, 2], g1[:, 1, :], NG)
            step(V.tensor_scalar(g4[:, 3], g4[:, 3], -MASKED, MASKED, ALU.mult, ALU.add))
            step(V.tensor_tensor(e32[:, 0].rearrange("p t (g e) -> p t g e", g=NG),
                                 lg[:, :, NG:].rearrange("p t (g e) -> p t g e", g=NG),
                                 g4[:, 3].unsqueeze(3).to_broadcast([P, TT, NG, EPG]), ALU.add))
            step(V.tensor_reduce(g1[:, 2, :], e32[:, 0], AX.X, ALU.max))
            first_best(oh[:, 0], e32[:, 0], g1[:, 2, :], e32[:, 1], g1[:, 3, :], NE)
            step(V.scalar_tensor_tensor(e32[:, 2], oh[:, 0], 2 * MASKED, e32[:, 0], ALU.mult, ALU.add))
            step(V.tensor_reduce(g1[:, 4, :], e32[:, 2], AX.X, ALU.max))
            first_best(oh[:, 1], e32[:, 2], g1[:, 4, :], e32[:, 3], g1[:, 3, :], NE)
            V.tensor_tensor(oh[:, 2], oh[:, 0], oh[:, 1], ALU.add).then_inc(oh_ready, 1)
            V.tensor_tensor(g1[:, 5, :], g1[:, 4, :], g1[:, 2, :], ALU.subtract).then_inc(md_ready, 1)
            dve.wait_ge(ranked, 1)
            step(V.tensor_copy(e32[:, 4].rearrange("p t e -> p (t e)"), psum[:, 3, 0:TT * NE]))
            step(V.tensor_copy(cnt[:, 0, :], psum[:, 3, TT * NE:(TT + 1) * NE]))
            step(V.tensor_scalar(cnt[:, 1, :], cnt[:, 0, :], float(CAP), None, ALU.is_gt))
            for m in range(2, T // CAP):
                step(V.scalar_tensor_tensor(cnt[:, 1, :], cnt[:, 0, :], float(CAP * m), cnt[:, 1, :],
                                            ALU.is_gt, ALU.add))
            step(V.tensor_tensor_scan(cnt[:, 2, :], ones[:, 0:NE], cnt[:, 1, :], 0.0, ALU.mult, ALU.add))
            step(V.tensor_tensor(cnt[:, 3, :], cnt[:, 2, :], cnt[:, 1, :], ALU.subtract))
            step(V.tensor_scalar(cnt[:, 3, :], cnt[:, 3, :], float(CAP), float(CAP * (NE - 1)), ALU.mult, ALU.add))
            step(V.tensor_tensor(cnt[:, 3, :], cnt[:, 3, :], base0[:, :], ALU.subtract))
            step(V.tensor_scalar(e32[:, 5], e32[:, 4], float(CAP), None, ALU.is_ge))
            step(V.tensor_tensor(e32[:, 5], e32[:, 5], cnt[:, 3, :].unsqueeze(1).to_broadcast([P, TT, NE]), ALU.mult))
            step(V.tensor_tensor(e32[:, 4], e32[:, 4], base0[:, :].unsqueeze(1).to_broadcast([P, TT, NE]), ALU.add))
            step(V.tensor_tensor(e32[:, 4], e32[:, 4], e32[:, 5], ALU.add))
            for k in range(2):
                step(V.tensor_tensor(e32[:, 6], oh[:, k], e32[:, 4], ALU.mult))
                step(V.tensor_reduce(slot_f[:, k, :], e32[:, 6], AX.X, ALU.add))
            V.tensor_copy(slot_i[:, :, :], slot_f[:, :, :]).then_inc(slots_ready, 1)
            step(V.tensor_tensor(over_cmp[:, :, :], cnt[0:1, 2, :].unsqueeze(1).to_broadcast([1, MAX_OVER, NE]),
                                 jrow[:, :].unsqueeze(2).to_broadcast([1, MAX_OVER, NE]), ALU.is_le))
            step(V.tensor_reduce(over_f[:, 0:MAX_OVER], over_cmp[:, :, :], AX.X, ALU.add))
            step(V.tensor_scalar(over_f[:, 0:MAX_OVER], over_f[:, 0:MAX_OVER], float(NE - 1), None, ALU.min))
            step(V.tensor_copy(over_f[:, MAX_OVER:], cnt[0:1, 2, NE - 1:NE]))
            V.tensor_copy(over_i[:, :], over_f[:, :]).then_inc(over_ready, 1)
            dve.wait_ge(ge_ready, 1)
            dve.wait_ge(me_ready, 1)
            step(V.tensor_reduce(g1[:, 7, :], g4[:, 1], AX.X, ALU.add))
            step(V.tensor_scalar(g1[:, 8, :], g1[:, 6, :], 1.0, None, ALU.add))
            step(V.tensor_tensor(g1[:, 7, :], g1[:, 7, :], g1[:, 8, :], ALU.mult))
            step(V.reciprocal(g1[:, 8, :], g1[:, 7, :]))
            step(V.tensor_scalar(comb[:, 0, :], g1[:, 8, :], 0.5, None, ALU.mult))
            step(V.tensor_tensor(comb[:, 1, :], comb[:, 0, :], g1[:, 6, :], ALU.mult))
            dve.wait_ge(table_t, 1)
            V.tensor_copy(tok_i[:, :], psum[0:CAP, 0, 0:NBLK + 1]).then_inc(tok_ready, 1)

            def expert(b, i, s):
                dve.wait_ge(th_done, b + 1)
                V.scalar_tensor_tensor(gated[s % 2][CAP:P, :], th[s % 2][0:CAP, :], 1.0,
                                       psum[0:CAP, 2 + s % 2, 0:FF], ALU.add, ALU.mult).then_inc(gated_ready, 1)
                dve.wait_ge(gated_ready, b + 1)
                V.tensor_tensor(hid[s % 2][0:CAP, :], gated[s % 2][CAP:P, :], psum[CAP:P, 2 + s % 2, 0:FF], ALU.mult
                                ).then_inc(h_ready, 1)
                dve.wait_ge(ht_done, b + 1)
                V.tensor_copy(hidT[s % 2], psum[:, 1, 0:2 * CAP].rearrange("p (k c) -> p k c", k=2)
                              ).then_inc(ht_copied, 1)

            with dve.Fori(0, NE // 4) as i:
                for s in range(4):
                    expert(i * 4 + s, i, s)
            n_over = dve.value_load(over_i[0:1, MAX_OVER:MAX_OVER + 1], min_val=0, max_val=MAX_OVER - 1)
            with dve.If(n_over > 0):
                with dve.Fori(NE // 4, NBLK // 4) as i:
                    for s in range(4):
                        expert(i * 4 + s, i, s)
            dve.wait_ge(ah_ready, TT)
            dve.wait_ge(ln2_landed, 32)
            for t in range(TT):
                dve.wait_ge(yk_landed[t % 2][0], 16 * (t // 2 + 1))
                step(V.scalar_tensor_tensor(h1[:, t, :], yk[t % 2][0], comb[:, 0, t:t + 1], h1[:, t, :],
                                            ALU.mult, ALU.add))
                dve.wait_ge(yk_landed[t % 2][1], 16 * (t // 2 + 1))
                V.scalar_tensor_tensor(h1[:, t, :], yk[t % 2][1], comb[:, 1, t:t + 1], h1[:, t, :],
                                       ALU.mult, ALU.add, accum_out=ln[:, 1, 0, t:t + 1]).then_inc(r2_ready, 1)
                dve.wait_ge(r2_ready, t + 1)
                norm(1, t, r2_ready, mean2_ready, ssq2_ready, var2_ready, rstd2_ready, ln2g, ln2b, out_ready)


_INS = ['x', 'w_in', 'a_sinks', 'kv_norm_g', 'w_uk', 'w_uv', 'w_branch_a', 'w_branch_b', 'w_out', 'ln1_g', 'ln1_b',
        'router_group_w', 'router_group_b', 'router_expert_w', 'router_expert_b', 'w_gate', 'w_up', 'w_down',
        'ln2_g', 'ln2_b']
_OUTS = [((1, T, D), 'float32')]


def kernel(**inputs):
    import numpy as _np
    import concourse.bacc as _bacc
    from concourse import mybir as _mybir
    from concourse.bass_utils import run_bass_kernel_spmd as _run

    nc = _bacc.Bacc("TRN2", target_bir_lowering=False, num_devices=1)
    arrays, args = {}, []
    for name in _INS:
        a = _np.ascontiguousarray(inputs[name])
        if name in ('w_gate', 'w_up', 'w_down'):
            a = a.reshape(a.shape[0], NE, *a.shape[3:])
        arrays[f"in_{name}_dram"] = a
        args.append(nc.dram_tensor(f"in_{name}_dram", a.shape, _mybir.dt.from_np(a.dtype), kind="ExternalInput").ap())
    for i, (shape, dtype) in enumerate(_OUTS):
        dt = _mybir.dt.from_np(_np.dtype(dtype))
        args.append(nc.dram_tensor(f"out_{i}_dram", shape, dt, kind="ExternalOutput").ap())
    build(nc, *args)
    r = _run(nc, [arrays], core_ids=[0])
    got = tuple(r.results[0][f"out_{i}_dram"] for i in range(len(_OUTS)))
    return got[0]
```

```python
import concourse.bass as bass
from concourse import mybir
from contextlib import ExitStack
import math

F32 = mybir.dt.float32
F32R = mybir.dt.float32r
I32 = mybir.dt.int32
ALU = mybir.AluOpType
ACT = mybir.ActivationFunctionType
AX = mybir.AxisListType

P = 128
T, D = 512, 1024
TT, DT = T // P, D // P
CHUNK, HD = 64, 64
AH, AG = 16, 2
BH = 16
RANK = 128
IH = 8
TOPK = min(256, T // 4)
NG, EPG, FF = 4, 8, 256
NE = NG * EPG
CAP = 64
N_TOP = 2
PAIRS = N_TOP * T
MAX_OVER = 18
NBLK = NE + MAX_OVER
ALPHA = 2.0 ** 0.25
LN_EPS, RMS_EPS = 1e-5, 1e-6
IDX_SCALE = (HD ** -0.5) * (IH ** -0.5)
MASKED = -1e30
OUT_OF_REACH = -1e38
TAKEN = -3e38

C_QA = 0
C_KA = C_QA + AH * HD
C_VA = C_KA + AG * HD
C_QB = C_VA + AG * HD
C_CKV = C_QB + BH * HD
C_QI = C_CKV + RANK
C_KI = C_QI + IH * HD
C_WI = C_KI + HD
C_GA = C_WI + IH
C_GB = C_GA + D
C_END = C_GB + D

SLOPE = [2.0 ** (-8.0 * (h + 1) / 16) for h in range(16)]
WCOLS = 256
WPART = DT * WCOLS
EXW = DT * 2 * FF + 2 * D


def weight_chunks():
    out = [("in", C_CKV + WCOLS * i) for i in range(3)] + [("in", C_KA)]
    out += [("in", C_QA + WCOLS * i) for i in range(4)]
    out += [("in", C_QB + WCOLS * i) for i in range(4)]
    out += [("in", C_GA + WCOLS * i) for i in range(8)]
    for i in range(4):
        out += [("a", WCOLS * i), ("b", WCOLS * i)]
    return out


def units():
    out = [("ckv", 0, 0, 0), ("qi", 0, 0, 128), ("qi", 1, 1, 0), ("qi", 2, 1, 128), ("qi", 3, 2, 0)]
    out += [("ki", 0, 2, 128)]
    out += [("ka", 0, 3, 0), ("va", 0, 3, 128)]
    out += [("qa", m, 4 + m // 2, 128 * (m % 2)) for m in range(8)]
    out += [("qb", m, 8 + m // 2, 128 * (m % 2)) for m in range(8)]
    out += [("gate", m, 12 + m // 2, 128 * (m % 2)) for m in range(16)]
    for m in range(8):
        out += [("a", m, 20 + 2 * (m // 2), 128 * (m % 2)), ("b", m, 21 + 2 * (m // 2), 128 * (m % 2))]
    out += [("out", 2 * t + i, None, 512 * i) for t in range(TT) for i in range(2)]
    return out


CHUNKS, UNITS = weight_chunks(), units()
UNIT = {(kind, i): n for n, (kind, i, _, _) in enumerate(UNITS)}
LAST_OF_CHUNK = {c: n for n, (_, _, c, _) in enumerate(UNITS)}
RING = 3
EXS = 6
XGS = 3


def bank_of(u):
    kind, i, _, _ = UNITS[u]
    if kind == "out":
        return 4 + 2 * ((i // 2) % 2) + i % 2
    if kind in "ab":
        return 2 * (i % 2) + (kind == "b")
    if kind in ("qb", "gate"):
        return 6
    return 6 + u % 2


ITEMS = [("A", q, t) for q in range(4) for t in range(TT)] + [("B", j, t) for t in range(TT) for j in range(8)]


def build(nc, x, w_in, a_sinks, kv_norm_g, w_uk, w_uv, w_branch_a, w_branch_b, w_out, ln1_g, ln1_b,
          rg_w, rg_b, re_w, re_b, w_gate, w_up, w_down, ln2_g, ln2_b, out):
    ctx = ExitStack()
    with ctx:
        sem = lambda name: ctx.enter_context(nc.semaphore(name))
        sb = lambda name, shape, dt=F32: ctx.enter_context(nc.sbuf_tensor(name, shape, dt))

        h1_dram = nc.dram_tensor("h1_rows", (T, D), F32, kind="Internal").ap()
        table_dram = nc.dram_tensor("slot_token", ((NBLK + 1) * CAP, 1), F32, kind="Internal").ap()
        y_dram = nc.dram_tensor("expert_rows", (NBLK * CAP, D), F32, kind="Internal").ap()

        ARENA = EXS * EXW + 2 * D + DT * T + TT * D
        arena_at = -(-nc.sbuf_base // 32) * 32
        sb("arena", [P, ARENA])

        def shaped(v, shape):
            if len(shape) == 2:
                return v.rearrange("p (a b) -> p a b", a=shape[0])
            if len(shape) == 3:
                return v.rearrange("p (a b c) -> p a b c", a=shape[0], b=shape[1])
            return v

        names = [0]

        def view(off, *shape, dt=F32):
            names[0] += 1
            v = nc.alloc_sbuf_tensor_at(f"arena_{names[0]}", [P, math.prod(shape)], dt, offset=arena_at + 4 * off)
            return shaped(v[:, :], shape)

        def view_r(off, *shape):
            return view(off, *shape, dt=F32R)

        at = [0]

        def region(n):
            at[0] += n
            return at[0] - n

        r_ring = region(RING * 2 * WPART)
        r_gb = region(DT * T)
        r_xlo = region(DT * T)
        r_att = region(7296)
        r_qi = region(4 * T)
        r_sp = region(4096)
        region(896)
        r_xhi = region(DT * T)
        r_qb = region(DT * T)
        r_qa = region(DT * T)
        assert at[0] == ARENA, at
        ga_t = sb("gate_a_T", [P, DT, T])
        slot_off = [r_ring + 2 * WPART * ((i + 2) % RING) for i in range(RING)]
        w_raw = [view(f, DT, WCOLS) for f in slot_off]
        w_lo = [view_r(f, DT, WCOLS) for f in slot_off]
        w_hi = [view_r(f + WPART, DT, WCOLS) for f in slot_off]
        gaT = ga_t[:, :, :]
        gbT = view(r_gb, DT, T)
        x_nat = view(r_gb, TT, D)
        o = r_att

        def take(n):
            nonlocal o
            o += n
            return o - n

        kiT = view(take(512), T)
        kaT = view(take(1024), AG, T)
        va = view(take(512), TT, AG * HD)
        va_hi = view(take(512), TT, AG * HD)
        ckvT = view(take(512), T)
        cT = view(take(512), T)
        kbT = view(take(512), T)
        vb = view(take(256), TT, HD)
        negd = view(take(512), 512)
        dm_off = take(1280)
        work_off = take(1152)
        assert o == r_qi
        dm = [view(dm_off + P * t * (t + 1) // 2, P * (t + 1)) for t in range(TT)]
        work = [None] + [view(work_off + P * (t * (t + 1) // 2 - 1), P * (t + 1)) for t in range(1, TT)]
        qiT = view(r_qi, 4, T)
        rel = [view(r_sp + 512 * i, 512) for i in range(2)]
        c_sq, rstd_diag, wiT = (view(r_sp + 1024 + 512 * i, 512) for i in range(3))
        s_sb = [view(r_sp + 1024 * i, 1024) for i in range(2)]
        pt_sb = [view(r_sp + 2048 + 1024 * i, 1024) for i in range(2)]
        x_hi, x_lo = view_r(r_xhi, DT, T), view_r(r_xlo, DT, T)
        qaT = view(r_qa, DT, T)
        qbT = view(r_qb, DT, T)
        branch_hi = {"a": x_hi, "b": x_lo}
        branch_lo = {"a": view_r(r_qa, DT, T), "b": view_r(r_qb, DT, T)}
        ln1g, ln1b = view(0, D), view(D, D)
        ln2g, ln2b = ln1g, ln1b
        w_o = view(r_xhi - DT * D, DT, D)
        h1 = view(r_qa, TT, D)
        h1T = view(r_xhi, DT, T)
        xg = [view(r_qb + D * i, D) for i in range(XGS)]
        ex_off = [2 * D + EXW * i for i in range(EXS)]
        assert ex_off[-1] + EXW == r_qb and ex_off[3] + EXW <= r_xhi - DT * D
        assert ex_off[3] >= r_att and ex_off[5] + EXW > r_xhi
        ex_gu = [view(f, 2, DT, FF) for f in ex_off]
        ex_d = [view(f + 2 * DT * FF, 2, D) for f in ex_off]
        moe = ga_t[:, :, :].rearrange("p k c -> p (k c)")

        def small(off, *shape):
            return shaped(moe[:, off:off + math.prod(shape)], shape)

        xgT = [small(512 * i, DT, CAP) for i in range(2)]
        th = [small(1024 + 256 * i, FF) for i in range(2)]
        gated = [small(1536 + 256 * i, FF) for i in range(2)]
        hid = [small(2048 + 256 * i, FF) for i in range(2)]
        hidT = [small(2560 + 128 * i, 2, CAP) for i in range(2)]
        y_sb = [small(2816 + 512 * i, 512) for i in range(2)]
        yk = [[view(2 * D + D * (2 * t + k), D) for k in range(2)] for t in range(TT)]

        ident = sb("ident", [P, P])
        ones = sb("ones", [P, P])
        upper = sb("upper", [P, P])
        wuk = sb("wuk", [P, HD])
        wuv = sb("wuv", [P, HD])
        kvg = sb("kvg", [P, 1])
        var_c = sb("var_c", [P, TT])
        rstd_c = sb("rstd_c", [P, TT])
        sinks_row = sb("sinks_row", [P, AH])
        sinks = sb("sinks", [P, 4, 4])
        rw = sb("rw", [P, DT, NG + NE])
        rb = sb("rb", [P, NG + NE])
        wis = sb("wis", [P, TT, IH])
        m8 = sb("m8", [P, 3, 8])
        half_neg = sb("half_neg", [P, 4])
        strip = sb("strip", [P, 192])
        mx = sb("mx", [P, 4, 4])
        negm = sb("negm", [P, 4, 4])
        den = sb("den", [P, 4, 4])
        sink_e = sb("sink_e", [P, 4, 4])
        ln = sb("ln", [P, 2, 5, 4])
        r_route = r_qb + XGS * D
        lg = view(r_route, TT, NG + NE)
        g4 = view(r_route + 144, 4, TT * NG).rearrange("p a (t g) -> p a t g", t=TT)
        g1 = view(r_route + 208, 10, TT)
        cnt = view(r_route + 248, 4, NE)
        table_sb = view(r_route + 376, CAP)[0:NBLK + 1]
        desc = sb("desc", [P, NE])
        base0 = sb("base0", [P, NE])
        jrow = sb("jrow", [1, MAX_OVER])
        e32 = view(r_qb, 8, TT * NE).rearrange("p a (t e) -> p a t e", t=TT)
        oh = view(r_qb + 1024, 3, TT * NE).rearrange("p a (t e) -> p a t e", t=TT)
        over_cmp = view(r_qb + 1536, MAX_OVER, NE)[0:1]
        over_f = sb("over_f", [1, MAX_OVER + 1])
        over_i = sb("over_i", [1, MAX_OVER + 1], I32)
        slot_f = sb("slot_f", [P, 2, TT])
        slot_i = sb("slot_i", [P, 2, TT], I32)
        comb = sb("comb", [P, 2, TT])
        tokid = sb("tokid", [P, TT])
        zero_tab = sb("zero_tab", [NBLK + 1, CAP])
        tok_i = sb("tok_i", [CAP, NBLK + 1], I32)
        idx = [sb(f"idx{i}", [CAP, 1], I32) for i in range(XGS)]
        psum = ctx.enter_context(nc.psum_tensor("psum", [P, 8, 512], F32))

        x_landed = [sem(f"x_landed{t}") for t in range(TT)]
        small_landed = sem("small_landed")
        ln1_landed, ln2_landed, x2_landed = sem("ln1_landed"), sem("ln2_landed"), [sem(f"x2_landed{t}") for t in range(TT)]
        w_high, w_split, wo_landed = sem("w_high"), sem("w_split"), sem("wo_landed")
        o_high, o_split = sem("o_high"), sem("o_split")
        w_landed = [sem(f"w_landed{i}") for i in range(RING)]
        const_ready = sem("const_ready")
        pool_step = sem("pool_step")
        abs_ready, sinks_ready = sem("abs_ready"), sem("sinks_ready")
        xt_done, xt_high, xt_split = sem("xt_done"), sem("xt_high"), sem("xt_split")
        unit_done, unit_copied = sem("unit_done"), sem("unit_copied")
        act_step, dve_step = sem("act_step"), sem("dve_step")
        csq_ready, css_done, var_c_ready, rstd_c_ready, diag_ready, rstd_spread, c_ready = (
            sem("csq_ready"), sem("css_done"), sem("var_c_ready"), sem("rstd_c_ready"),
            sem("diag_ready"), sem("rstd_spread"), sem("c_ready"))
        c_done, c_copied = sem("c_done"), sem("c_copied")
        wi_turned, wi_copied, va_turned, va_copied = (sem("wi_turned"), sem("wi_copied"), sem("va_turned"),
                                                      sem("va_copied"))
        idx_scored, rel_ready, rel_added = sem("idx_scored"), sem("rel_ready"), sem("rel_added")
        s_done, s_taken, negm_ready, exp_done = sem("s_done"), sem("s_taken"), sem("negm_ready"), sem("exp_done")
        p_ready, pt_done, pt_copied = sem("p_ready"), sem("pt_done"), sem("pt_copied")
        pv_done, o_copied = sem("pv_done"), sem("o_copied")
        merged_read, m_ready = sem("merged_read"), sem("m_ready")
        ax_ready = sem("ax_ready")
        r_ready, mean_ready, ssq_ready, var_ready, rstd_ready, h1_ready = (
            sem("r_ready"), sem("mean_ready"), sem("ssq_ready"), sem("var_ready"), sem("rstd_ready"),
            sem("h1_ready"))
        h1_stored, h1t_done, h1t_copied = sem("h1_stored"), sem("h1t_done"), sem("h1t_copied")
        routed, gd_ready, ge_ready, md_ready, me_ready = (sem("routed"), sem("gd_ready"), sem("ge_ready"),
                                                          sem("md_ready"), sem("me_ready"))
        oh_ready, ranked, slots_ready, over_ready = (sem("oh_ready"), sem("ranked"), sem("slots_ready"),
                                                     sem("over_ready"))
        zero_ready, table_zeroed, table_set, table_loaded = (sem("zero_ready"), sem("table_zeroed"),
                                                             sem("table_set"), sem("table_loaded"))
        table_t, tok_ready = sem("table_t"), sem("tok_ready")
        ah_ready = sem("ah_ready")
        gu_landed = [sem(f"gu_landed{i}") for i in range(EXS)]
        d_landed = [sem(f"d_landed{i}") for i in range(EXS)]
        xg_landed = [sem(f"xg_landed{i}") for i in range(XGS)]
        idx_ready = sem("idx_ready")
        xgt_done, xgt_copied, gu_done, th_done, h_ready, ht_done, ht_copied, d_done, y_copied = (
            sem("xgt_done"), sem("xgt_copied"), sem("gu_done"), sem("th_done"), sem("h_ready"), sem("ht_done"),
            sem("ht_copied"), sem("d_done"), sem("y_copied"))
        gated_ready, rows_zeroed = sem("gated_ready"), sem("rows_zeroed")
        pe_passed, pool_passed = sem("pe_passed"), sem("pool_passed")
        y_stored = [sem(f"y_stored{i}") for i in range(2)]
        yk_landed = [[sem(f"yk_landed{i}{k}") for k in range(2)] for i in range(TT)]
        r2_ready, mean2_ready, ssq2_ready, var2_ready, rstd2_ready, out_ready, out_stored = (
            sem("r2_ready"), sem("mean2_ready"), sem("ssq2_ready"), sem("var2_ready"), sem("rstd2_ready"),
            sem("out_ready"), sem("out_stored"))

        class Steps:

            def __init__(self, eng, s, count=0):
                self.eng, self.s, self.count = eng, s, count

            def __call__(self, ins):
                self.count += 1
                ins.then_inc(self.s, 1)
                self.eng.wait_ge(self.s, self.count)

        def item_shape(n):
            kind, g, t = ITEMS[n]
            if kind == "A":
                w0 = 0 if t else CHUNK
                return kind, g, t, w0, 192 - w0
            return kind, g, t, 0, P * (t + 1)

        def unit_wait(eng, u):
            before = [v for v in range(u) if bank_of(v) == bank_of(u)]
            kind = UNITS[u][0]
            if kind in ("a", "b"):
                if UNITS[u][1] >= 2:
                    eng.wait_ge(merged_read, 2 * (UNITS[u][1] - 2) + 1 + (kind == "b"))
            elif kind == "out":
                if UNITS[u][1] >= 4:
                    eng.wait_ge(r_ready, UNITS[u][1] // 2 - 1)
            elif before:
                eng.wait_ge(unit_copied, before[-1] + 1)

        def blocks(eng, expert):
            with eng.Fori(0, NE // EXS) as i:
                for s in range(EXS):
                    expert(i * EXS + s, i, s)
            for b in range(NE // EXS * EXS, NE):
                expert(b, b // EXS, b % EXS)
            eng.wait_ge(over_ready, 1)
            n_over = eng.value_load(over_i[0:1, MAX_OVER:MAX_OVER + 1], min_val=0, max_val=MAX_OVER - 1)
            with eng.If(n_over > 0):
                with eng.Fori(NE // EXS, NBLK // EXS) as i:
                    for s in range(NE % EXS, NE % EXS + EXS):
                        expert(i * EXS + s, i, s)

        block = ctx.enter_context(nc.Block())

        @block.sync
        def _(sp):
            mats = {"in": w_in, "a": w_branch_a, "b": w_branch_b}

            def chunk(c):
                mat, c0 = CHUNKS[c]
                if c >= RING:
                    sp.wait_ge(unit_done, LAST_OF_CHUNK[c - RING] + 1)
                sp.dma_start(w_raw[c % RING], mats[mat][0, :, c0:c0 + WCOLS].rearrange("(k p) n -> p k n", p=P)
                             ).then_inc(w_landed[c % RING], 16)

            chunk(0)
            for t in range(TT):
                sp.dma_start(x_nat[:, t, :], x[0, t * P:(t + 1) * P, :]).then_inc(x_landed[t], 16)
            chunk(1)
            small = [(wuk[:, :], w_uk[0]), (wuv[:, :], w_uv[0]), (kvg[:, :], kv_norm_g[0].unsqueeze(1)),
                     (rw[:, :, 0:NG], rg_w[0].rearrange("(k p) g -> p k g", p=P)),
                     (rw[:, :, NG:], re_w[0].rearrange("(k p) g e -> p k (g e)", p=P)),
                     (rb[:, 0:NG], rg_b[0].partition_broadcast(P)),
                     (rb[:, NG:], re_b[0].rearrange("g e -> (g e)").partition_broadcast(P)),
                     (sinks_row[:, :], a_sinks[0].partition_broadcast(P))]
            for dst, src in small:
                sp.dma_start(dst, src).then_inc(small_landed, 16)
            for c in range(2, 23):
                chunk(c)

            def expert(e, slot):
                sp.dma_start(ex_gu[slot][:, 0].rearrange("p k f -> p (k f)"),
                             w_gate[0, e].rearrange("(p k) f -> p (k f)", p=P)).then_inc(gu_landed[slot], 16)
                sp.dma_start(ex_gu[slot][:, 1].rearrange("p k f -> p (k f)"),
                             w_up[0, e].rearrange("(p k) f -> p (k f)", p=P)).then_inc(gu_landed[slot], 16)
                sp.dma_start(ex_d[slot].rearrange("p k n -> p (k n)"),
                             w_down[0, e].rearrange("(p k) n -> p (k n)", p=P)).then_inc(d_landed[slot], 16)

            sp.wait_ge(o_copied, len(ITEMS))
            for h in range(2):
                rows = slice(h * D // 2, (h + 1) * D // 2)
                sp.dma_start(w_o[:, h * DT // 2:(h + 1) * DT // 2, :],
                             w_out[0, rows, :].rearrange("(k p) n -> p k n", p=P)).then_inc(wo_landed, 16)
                chunk(23 + h)
            expert(3, 3)
            for c in range(25, len(CHUNKS)):
                chunk(c)
            sp.wait_ge(unit_done, LAST_OF_CHUNK[25] + 1)
            sp.dma_start(ln1g, ln1_g[0].partition_broadcast(P)).then_inc(ln1_landed, 16)
            sp.dma_start(ln1b, ln1_b[0].partition_broadcast(P)).then_inc(ln1_landed, 16)
            sp.wait_ge(unit_done, UNIT["a", 7] + 1)
            for t in range(TT):
                sp.dma_start(h1[:, t, :], x[0, t * P:(t + 1) * P, :]).then_inc(x2_landed[t], 16)
            sp.wait_ge(unit_done, UNIT["b", 7] + 1)
            expert(0, 0)
            sp.wait_ge(m_ready, 8)
            expert(1, 1)
            expert(2, 2)
            for t in range(TT):
                if t == TT - 1:
                    sp.wait_ge(unit_done, UNIT["out", 7] + 1)
                    expert(4, 4)
                sp.wait_ge(h1_ready, t + 1)
                sp.dma_start(h1_dram[t * P:(t + 1) * P, :], h1[:, t, :]).then_inc(h1_stored, 16)
            sp.wait_ge(routed, 1)
            expert(5, 5)
            sp.dma_start(ln2g, ln2_g[0].partition_broadcast(P)).then_inc(ln2_landed, 16)
            sp.dma_start(ln2b, ln2_b[0].partition_broadcast(P)).then_inc(ln2_landed, 16)
            sp.wait_ge(table_set, 16 * 2 * TT)
            sp.dma_start(table_sb[:, :], table_dram.rearrange("(b s) o -> b (s o)", s=CAP)
                         ).then_inc(table_loaded, 16)

            def store_y(b, s):
                sp.wait_ge(y_copied, b + 2)
                for half in range(2):
                    sp.dma_start(y_dram[bass.ds(b * CAP, CAP), half * 512:(half + 1) * 512],
                                 y_sb[s % 2][half * CAP:(half + 1) * CAP, :]).then_inc(y_stored[s % 2], 16)

            def refill(b, s):
                sp.wait_ge(d_done, b + 1)
                expert(b + EXS, s)
                store_y(b, s)

            with sp.Fori(0, (NE - EXS) // EXS) as i:
                for s in range(EXS):
                    refill(i * EXS + s, s)
            for b in range((NE - EXS) // EXS * EXS, NE - EXS):
                refill(b, b % EXS)
            for b in range(NE - EXS, NE):
                store_y(b, b % EXS)
            sp.wait_ge(over_ready, 1)
            n_over = sp.value_load(over_i[0:1, MAX_OVER:MAX_OVER + 1], min_val=0, max_val=MAX_OVER - 1)
            with sp.If(n_over > 0):
                with sp.Fori(0, MAX_OVER // EXS) as i:
                    for s in range(EXS):
                        b = i * EXS + (NE + s)
                        eid = sp.value_load(over_i[0:1, bass.ds(i * EXS + s, 1)], min_val=0, max_val=NE - 1)
                        sp.wait_ge(d_done, b - (EXS - 1))
                        expert(eid, (NE + s) % EXS)
                        store_y(b, s)
            for t in range(TT):
                sp.wait_ge(out_ready, t + 1)
                sp.dma_start(out[0, t * P:(t + 1) * P, :], h1[:, t, :]).then_inc(out_stored, 16)
            sp.wait_ge(out_stored, 16 * TT)

        @block.gpsimd
        def _(pool):
            step = Steps(pool, pool_step)
            nc.gpsimd.memset(ident[:, :], 0.0).then_inc(pool_step, 1)
            nc.gpsimd.memset(ones[:, :], 1.0).then_inc(pool_step, 1)
            step.count = 2
            pool.wait_ge(pool_step, 2)
            nc.gpsimd.affine_select(out=ident[:, :], in_=ident[:, :], compare_op=ALU.not_equal, fill=1.0, base=0,
                                    pattern=[[-1, P]], channel_multiplier=1).then_inc(const_ready, 1)

            def split(c):
                pool.wait_ge(w_high, c + 1)
                nc.gpsimd.tensor_tensor(w_lo[c % RING], w_raw[c % RING], w_hi[c % RING].bitcast(F32), ALU.subtract
                                        ).then_inc(w_split, 1)

            split(0)
            nc.gpsimd.affine_select(out=upper[:, :], in_=ones[:, :], compare_op=ALU.is_gt, fill=0.0, base=0,
                                    pattern=[[1, P]], channel_multiplier=-1).then_inc(const_ready, 1)
            nc.gpsimd.iota(negd, [[1, 512]], base=-384, channel_multiplier=-1,
                           allow_small_or_imprecise_dtypes=True).then_inc(const_ready, 1)
            nc.gpsimd.iota(desc[:, :], [[-1, NE]], base=NE, channel_multiplier=0,
                           allow_small_or_imprecise_dtypes=True).then_inc(const_ready, 1)
            nc.gpsimd.iota(base0[:, :], [[CAP, NE]], base=0, channel_multiplier=0,
                           allow_small_or_imprecise_dtypes=True).then_inc(const_ready, 1)
            nc.gpsimd.iota(jrow[:, :], [[1, MAX_OVER]], base=0, channel_multiplier=0,
                           allow_small_or_imprecise_dtypes=True).then_inc(const_ready, 1)
            nc.gpsimd.iota(tokid[:, :], [[P, TT]], base=0, channel_multiplier=1,
                           allow_small_or_imprecise_dtypes=True).then_inc(const_ready, 1)
            nc.gpsimd.memset(half_neg[:, :], -0.5).then_inc(const_ready, 1)
            nc.gpsimd.memset(zero_tab[:, :], 0.0).then_inc(zero_ready, 1)
            pool.wait_ge(zero_ready, 1)
            pool.dma_start(table_dram.rearrange("(b s) o -> b (s o)", s=CAP), zero_tab[:, :]
                           ).then_inc(table_zeroed, 16)
            split(1)
            pool.wait_ge(const_ready, 8)
            pool.wait_ge(var_c_ready, 1)
            nc.gpsimd.tensor_tensor(rstd_c[:, :], var_c[:, :], half_neg[:, :], ALU.pow).then_inc(rstd_c_ready, 1)
            pool.wait_ge(small_landed, 16 * 8)
            for q in range(4):
                nc.gpsimd.tensor_copy(sinks[:, q, :].rearrange("p (r i) -> p r i", r=2),
                                      sinks_row[:, 4 * q:4 * q + 4].rearrange("p (i r) -> p r i", r=2)
                                      ).then_inc(sinks_ready, 1)
            for c in range(2, 8):
                split(c)
            zeros = gaT[:, 0:2, :].rearrange("p a b -> p (a b)")
            nc.gpsimd.memset(zeros, 0.0).then_inc(zero_ready, 1)
            pool.wait_ge(zero_ready, 2)
            pool.dma_start(y_dram[NE * CAP:, :].rearrange("(p r) d -> p r d", p=P),
                           zeros.unsqueeze(1).to_broadcast([P, MAX_OVER * CAP // P, D])).then_inc(rows_zeroed, 16)
            for c in range(8, len(CHUNKS)):
                split(c)
            for t in range(TT):
                pool.wait_ge(var_ready, t + 1)
                nc.gpsimd.tensor_tensor(ln[:, 0, 4, t:t + 1], ln[:, 0, 3, t:t + 1], half_neg[:, 0:1], ALU.pow
                                        ).then_inc(rstd_ready, 1)
            pool.wait_ge(table_zeroed, 16)
            pool.wait_ge(slots_ready, 1)
            for k in range(2):
                for t in range(TT):
                    pool.indirect_dma_start(out=table_dram, out_offset=bass.IndirectOffsetOnAxis(
                        ap=slot_i[:, k, t:t + 1], axis=0), in_=tokid[:, t:t + 1], in_offset=None
                        ).then_inc(table_set, 16)
            pool.wait_ge(tok_ready, 1)
            pool.wait_ge(h1_stored, 16 * TT)

            def gather(b, s, n):
                nc.gpsimd.tensor_copy(idx[s][:, :], tok_i[:, bass.ds(b, 1)]).then_inc(idx_ready, 1)
                pool.wait_ge(idx_ready, n + 1)
                pool.sem_inc(pool_passed, 1)
                pool.indirect_dma_start(out=xg[s][0:CAP, :], out_offset=None, in_=h1_dram,
                                        in_offset=bass.IndirectOffsetOnAxis(ap=idx[s][:, 0:1], axis=0)
                                        ).then_inc(xg_landed[s], 16)

            for b in range(XGS):
                gather(b, b, b)

            def next_gathers(first, end):
                with pool.Fori(first, end) as i:
                    for s in range(EXS):
                        b = i * EXS + (XGS + s)
                        pool.wait_ge(xgt_done, b - (XGS - 1))
                        gather(b, s % XGS, b)

            next_gathers(0, NE // EXS)
            pool.wait_ge(over_ready, 1)
            n_over = pool.value_load(over_i[0:1, MAX_OVER:MAX_OVER + 1], min_val=0, max_val=MAX_OVER - 1)
            for p in range(2):
                pool.wait_ge(y_stored[p], 32 * NE // 2 + 1)
            with pool.If(n_over > 0):
                next_gathers(NE // EXS, NBLK // EXS)
                for p in range(2):
                    pool.wait_ge(y_stored[p], 32 * NBLK // 2 + 1)
            for t in range(TT):
                for k in range(2):
                    pool.indirect_dma_start(out=yk[t][k], out_offset=None, in_=y_dram,
                                            in_offset=bass.IndirectOffsetOnAxis(ap=slot_i[:, k, t:t + 1], axis=0)
                                            ).then_inc(yk_landed[t][k], 16)
                if t >= 1:
                    pool.wait_ge(var2_ready, t)
                    nc.gpsimd.tensor_tensor(ln[:, 1, 4, t - 1:t], ln[:, 1, 3, t - 1:t], half_neg[:, 0:1], ALU.pow
                                            ).then_inc(rstd2_ready, 1)
            pool.wait_ge(var2_ready, TT)
            nc.gpsimd.tensor_tensor(ln[:, 1, 4, TT - 1:TT], ln[:, 1, 3, TT - 1:TT], half_neg[:, 0:1], ALU.pow
                                    ).then_inc(rstd2_ready, 1)

        @block.tensor
        def _(pe):
            pe.wait_ge(const_ready, 1)
            for t in range(TT):
                pe.wait_ge(x_landed[t], 16)
                for h in range(2):
                    n = 2 * t + h
                    if n >= 6:
                        pe.wait_ge(xt_split, n - 5)
                    for k in range(4):
                        ins = nc.tensor.transpose(psum[:, n % 6, k * P:(k + 1) * P],
                                                  x_nat[:, t, (4 * h + k) * P:(4 * h + k + 1) * P], ident[:, :])
                    ins.then_inc(xt_done, 1)
            pe.wait_ge(xt_split, 2 * TT)

            def unit(u, k0=0, k1=DT):
                kind, i, c, col = UNITS[u]
                ps = psum[:, bank_of(u), :]
                if k0 == 0:
                    unit_wait(pe, u)
                if kind == "out":
                    pe.wait_ge(wo_landed, 32)
                    t = i // 2
                    for k in range(DT):
                        ins = nc.tensor.matmul(ps, gaT[:, k, t * P:(t + 1) * P], w_o[:, k, col:col + 512],
                                               start=k == 0, stop=k == DT - 1)
                    ins.then_inc(unit_done, 1)
                    return
                hi, lo = w_hi[c % RING], w_lo[c % RING]
                if k0 == 0:
                    pe.wait_ge(w_split, c + 1)
                xh, xl = (branch_hi[kind], branch_lo[kind]) if kind in ("a", "b") else (x_hi, x_lo)
                for k in range(k0, k1):
                    if kind in ("a", "b") and i == 0:
                        pe.wait_ge(o_split, DT * (kind == "b") + k + 1)
                    for p, (wp, xp) in enumerate(((hi, xh), (hi, xl), (lo, xh))):
                        ins = nc.tensor.matmul(ps, wp[:, k, col:col + P], xp[:, k, :],
                                               start=k == 0 and p == 0, stop=k == DT - 1 and p == 2)
                if k1 == DT:
                    ins.then_inc(unit_done, 1)

            unit(UNIT["ckv", 0])
            unit(UNIT["qi", 0])
            pe.wait_ge(csq_ready, 1)
            for t in range(TT):
                ins = nc.tensor.matmul(psum[:, 5, 2 * t:2 * t + 2], c_sq[:, t * P:(t + 1) * P], ones[:, 0:2],
                                       start=True, stop=True)
            ins.then_inc(css_done, 1)
            for u in range(UNIT["qi", 1], UNIT["qi", 2] + 1):
                unit(u)
            pe.wait_ge(diag_ready, TT)
            nc.tensor.matmul(psum[:, 4, :], ones[:, :], rstd_diag, start=True, stop=True).then_inc(rstd_spread, 1)
            for u in range(UNIT["qi", 3], UNIT["ki", 0] + 1):
                unit(u)
            pe.wait_ge(c_ready, 1)
            pe.wait_ge(small_landed, 16 * 8)
            nc.tensor.matmul(psum[0:HD, 5, :], wuk[:, :], cT, start=True, stop=True).then_inc(c_done, 1)
            for t in range(TT):
                ins = nc.tensor.matmul(psum[:, 4, t * HD:(t + 1) * HD], cT[:, t * P:(t + 1) * P], wuv[:, :],
                                       start=True, stop=True)
            ins.then_inc(c_done, 1)
            pe.wait_ge(unit_copied, UNIT["ki", 0] + 1)
            for t in range(TT):
                ins = nc.tensor.transpose(psum[:, 7, t * HD:(t + 1) * HD], wiT[HD:P, t * P:(t + 1) * P],
                                          ident[HD:P, HD:P])
            ins.then_inc(wi_turned, 1)
            n = 0
            for t in range(1, TT):
                for h in range(IH):
                    if n >= 4:
                        pe.wait_ge(rel_ready, n - 3)
                    r = slice(HD * (h % 2), HD * (h % 2) + HD)
                    nc.tensor.matmul(psum[:, n % 4, 0:P * (t + 1)], qiT[r, h // 2, t * P:(t + 1) * P],
                                     kiT[r, 0:P * (t + 1)], start=True, stop=True).then_inc(idx_scored, 1)
                    n += 1
            pe.wait_ge(wi_copied, 1)
            for u in range(UNIT["ka", 0], UNIT["qa", 7] + 1):
                unit(u)
                if u == UNIT["qa", 0]:
                    pe.wait_ge(unit_copied, UNIT["va", 0] + 1)
                    pe.wait_ge(c_copied, 2)
                    for t in range(TT):
                        ins = nc.tensor.transpose(psum[:, 4, t * P:(t + 1) * P], ckvT[:, t * P:(t + 1) * P],
                                                  ident[:, :])
                    ins.then_inc(va_turned, 1)

            def scores(n):
                kind, g, t, w0, w = item_shape(n)
                if n >= 2:
                    pe.wait_ge(s_taken, n - 1)
                if n <= 1:
                    pe.wait_ge(rel_ready, 3 * IH)
                    pe.wait_ge(c_copied, 2)
                if kind == "A":
                    pe.wait_ge(unit_copied, UNIT["qa", 2 * g + 1] + 1)
                else:
                    pe.wait_ge(unit_copied, UNIT["qb", g] + 1)
                for i in range(2 if kind == "A" else 1):
                    for par in range(2):
                        r = slice(HD * par, HD * par + HD)
                        if kind == "A":
                            q, k = qaT[r, 2 * g + i, t * P:(t + 1) * P], kaT[r, g // 2, P * t - CHUNK + w0:P * (t + 1)]
                        else:
                            q, k = qbT[r, g, t * P:(t + 1) * P], kbT[r, 0:w]
                        ins = nc.tensor.matmul(psum[:, 2 * (n % 2) + par, 256 * i:256 * i + w], q, k,
                                               start=True, stop=True)
                ins.then_inc(s_done, 1)

            def turn(n):
                kind, g, t, w0, w = item_shape(n)
                pe.wait_ge(p_ready, n + 1)
                if n >= 1:
                    pe.wait_ge(pt_copied, n)
                else:
                    pe.wait_ge(va_copied, 1)
                if kind == "A":
                    s = s_sb[n % 2][:, 0:4 * w].rearrange("p (h w) -> p h w", h=4)
                    for h in range(4):
                        ins = nc.tensor.transpose(psum[:, 4, h * P:(h + 1) * P], s[:, h, w - P:w], ident[:, :])
                    if t:
                        for h in range(4):
                            ins = nc.tensor.transpose(psum[0:CHUNK, 5, h * P:(h + 1) * P], s[:, h, 0:CHUNK],
                                                      ident[:, :])
                else:
                    s = s_sb[n % 2][:, 0:2 * w].rearrange("p (h w) -> p h w", h=2)
                    for kt in range(t + 1):
                        for par in range(2):
                            c = (kt % 2) * 256 + par * P
                            ins = nc.tensor.transpose(psum[:, 4 + kt // 2, c:c + P], s[:, par, kt * P:(kt + 1) * P],
                                                      ident[:, :])
                ins.then_inc(pt_done, 1)

            def values(n):
                kind, g, t, w0, w = item_shape(n)
                pe.wait_ge(pt_copied, n + 1)
                if n >= 1:
                    pe.wait_ge(o_copied, n)
                pt = pt_sb[n % 2]
                if kind == "A":
                    kv = slice(HD * (g // 2), HD * (g // 2) + HD)
                    for par in range(2):
                        ins = nc.tensor.matmul(psum[HD * par:HD * par + HD, 7, 0:256], va[:, t, kv],
                                               pt[:, 256 * par:256 * par + 256], start=True, stop=t == 0)
                    if t:
                        for par in range(2):
                            ins = nc.tensor.matmul(psum[HD * par:HD * par + HD, 7, 0:256], va_hi[0:CHUNK, t - 1, kv],
                                                   pt[0:CHUNK, 512 + 256 * par:512 + 256 * par + 256],
                                                   start=False, stop=True)
                else:
                    for kt in range(t + 1):
                        for par in range(2):
                            c = 256 * kt + P * par
                            ins = nc.tensor.matmul(psum[HD * par:HD * par + HD, 7, 0:P], vb[:, kt, :],
                                                   pt[:, c:c + P], start=kt == 0, stop=kt == t)
                ins.then_inc(pv_done, 1)

            pe.wait_ge(unit_copied, UNIT["qa", 7] + 1)
            scores(0)
            scores(1)
            for n in range(len(ITEMS)):
                if n + 2 < len(ITEMS):
                    scores(n + 2)
                u, k = UNIT["qb", 0] + n // 2, 4 * (n % 2)
                unit(u, k, k + 2)
                turn(n)
                unit(u, k + 2, k + 4)
                if n >= 1:
                    values(n - 1)
            values(len(ITEMS) - 1)

            pe.wait_ge(o_copied, len(ITEMS))
            for u in range(UNIT["a", 0], UNIT["out", 0]):
                unit(u)
            pe.wait_ge(m_ready, 8)

            def turn_h1(t):
                pe.wait_ge(h1_ready, t + 1)
                for h in range(2):
                    n = 2 * t + h
                    if n >= 2:
                        pe.wait_ge(h1t_copied, n - 1)
                    for k in range(4):
                        ins = nc.tensor.transpose(psum[:, n % 2, k * P:(k + 1) * P],
                                                  h1[:, t, (4 * h + k) * P:(4 * h + k + 1) * P], ident[:, :])
                    ins.then_inc(h1t_done, 1)

            for t in range(TT):
                unit(UNIT["out", 2 * t])
                unit(UNIT["out", 2 * t + 1])
                if t:
                    turn_h1(t - 1)
            turn_h1(TT - 1)
            pe.wait_ge(h1t_copied, 2 * TT)
            for t in range(TT):
                for k in range(DT):
                    ins = nc.tensor.matmul(psum[:, 2, t * (NG + NE):(t + 1) * (NG + NE)], h1T[:, k, t * P:(t + 1) * P],
                                           rw[:, k, :], start=k == 0, stop=k == DT - 1)
            ins.then_inc(routed, 1)
            pe.wait_ge(oh_ready, 1)
            pe.wait_ge(const_ready, 8)
            for t in range(TT + 1):
                for v in range(min(t + 1, TT)):
                    ins = nc.tensor.matmul(psum[:, 3, t * NE:(t + 1) * NE], (upper if v == t else ones)[:, :],
                                           oh[:, 2, v, :], start=v == 0, stop=v == min(t, TT - 1))
            ins.then_inc(ranked, 1)
            pe.wait_ge(table_loaded, 16)
            nc.tensor.transpose(psum[0:CAP, 0, 0:NBLK + 1], table_sb[:, :], ident[0:NBLK + 1, 0:NBLK + 1]
                                ).then_inc(table_t, 1)

            def turn_x(b, i, s):
                pe.wait_ge(xg_landed[s % XGS], i * (EXS // XGS * 16) + (s // XGS + 1) * 16)
                pe.sem_inc(pe_passed, 1)
                rows = xg[s % XGS][0:CAP, :].rearrange("s (p k) -> s k p", k=DT)
                for k in range(DT):
                    ins = nc.tensor.transpose(psum[:, 0, k * CAP:(k + 1) * CAP], rows[:, k, :],
                                              ident[0:CAP, 0:CAP])
                ins.then_inc(xgt_done, 1)

            def expert(b, i, s):
                slot, use = s % EXS, i + s // EXS
                pe.wait_ge(gu_landed[slot], use * 32 + 32)
                pe.wait_ge(xgt_copied, b + 1)
                for k in range(DT):
                    for g in range(2):
                        ins = nc.tensor.matmul(psum[CAP * g:CAP * g + CAP, 2 + s % 2, 0:FF], xgT[s % 2][:, k, :],
                                               ex_gu[slot][:, g, k, :], start=k == 0, stop=k == DT - 1)
                ins.then_inc(gu_done, 1)
                turn_x(b + 1, i, s + 1)
                pe.wait_ge(h_ready, b + 1)
                pe.sem_inc(pe_passed, 1)
                rows = hid[s % 2][0:CAP, :].rearrange("s (p k) -> s k p", k=2)
                for k in range(2):
                    ins = nc.tensor.transpose(psum[:, 1, k * CAP:(k + 1) * CAP], rows[:, k, :],
                                              ident[0:CAP, 0:CAP])
                ins.then_inc(ht_done, 1)
                pe.wait_ge(ht_copied, b + 1)
                pe.wait_ge(d_landed[slot], use * 16 + 16)
                pe.wait_ge(y_copied, b + 1)
                for k in range(2):
                    for half in range(2):
                        ins = nc.tensor.matmul(psum[CAP * half:CAP * half + CAP, 4 + s % 2, :], hidT[s % 2][:, k, :],
                                               ex_d[slot][:, k, 512 * half:512 * half + 512], start=k == 0,
                                               stop=k == 1)
                ins.then_inc(d_done, 1)

            pe.wait_ge(tok_ready, 1)
            turn_x(0, 0, 0)
            blocks(pe, expert)

        @block.scalar
        def _(act):
            step = Steps(act, act_step)

            def high(c):
                act.wait_ge(w_landed[c % RING], 16 * (c // RING + 1))
                nc.scalar.activation(w_hi[c % RING], w_raw[c % RING], ACT.Copy).then_inc(w_high, 1)

            high(0)
            for n in range(2 * TT):
                act.wait_ge(xt_done, n + 1)
                t, h = n // 2, n % 2
                nc.scalar.activation(x_hi[:, 4 * h:4 * h + 4, t * P:(t + 1) * P],
                                     psum[:, n % 6, :].rearrange("p (k c) -> p k c", k=4), ACT.Copy
                                     ).then_inc(xt_high, 1)
            high(1)

            def copy_unit(u):
                kind, i, c, _ = UNITS[u]
                if u == LAST_OF_CHUNK[c]:
                    high(c + 2)
                act.wait_ge(unit_done, u + 1)
                ps = psum[:, bank_of(u), :]
                if kind in ("ckv", "va"):
                    if kind == "va":
                        act.wait_ge(c_ready, 1)
                    ins = nc.scalar.activation(ckvT, ps, ACT.Copy)
                elif kind == "qi":
                    ins = nc.scalar.activation(qiT[:, i, :], ps, ACT.Copy)
                elif kind == "ki":
                    nc.scalar.activation(kiT[0:HD, :], ps[0:HD, :], ACT.Copy)
                    nc.scalar.activation(kiT[HD:P, :], ps[0:HD, :], ACT.Copy)
                    ins = nc.scalar.activation(wiT[HD:P, :], ps[HD:P, :], ACT.Copy, scale=IDX_SCALE)
                elif kind == "ka":
                    for g in range(AG):
                        for half in range(2):
                            ins = nc.scalar.activation(kaT[HD * half:HD * half + HD, g, :],
                                                       ps[HD * g:HD * g + HD, :], ACT.Copy)
                elif kind in ("qa", "qb"):
                    ins = nc.scalar.activation((qaT if kind == "qa" else qbT)[:, i, :], ps, ACT.Copy,
                                               scale=HD ** -0.5)
                else:
                    ins = nc.scalar.activation((gaT if i < 8 else gbT)[:, i % 8, :], ps, ACT.Tanh, scale=0.5)
                ins.then_inc(unit_copied, 1)

            act.wait_ge(unit_done, 1)
            nc.scalar.activation(c_sq, psum[:, bank_of(0), :], ACT.Square).then_inc(csq_ready, 1)
            copy_unit(0)
            act.wait_ge(const_ready, 3)
            step(nc.scalar.activation(negd, negd, ACT.Abs))
            nc.scalar.activation(negd, negd, ACT.Copy, scale=-1.0).then_inc(abs_ready, 1)
            for u in range(1, UNIT["ki", 0] + 1):
                copy_unit(u)
            act.wait_ge(c_done, 1)
            nc.scalar.activation(kbT[0:HD, :], psum[0:HD, 5, :], ACT.Copy)
            nc.scalar.activation(kbT[HD:P, :], psum[0:HD, 5, :], ACT.Copy).then_inc(c_copied, 1)
            act.wait_ge(c_done, 2)
            nc.scalar.activation(vb, psum[:, 4, 0:TT * HD].rearrange("p (t c) -> p t c", t=TT), ACT.Copy
                                 ).then_inc(c_copied, 1)
            act.wait_ge(wi_turned, 1)
            nc.scalar.activation(wis[:, :, :], psum[:, 7, 0:TT * HD].rearrange("p (t c) -> p t c", t=TT)[:, :, 0:IH],
                                 ACT.Copy).then_inc(wi_copied, 1)
            n = 0
            for t in range(1, TT):
                for h in range(IH):
                    act.wait_ge(idx_scored, n + 1)
                    if n >= 2:
                        act.wait_ge(rel_added, n - 1)
                    nc.scalar.activation(rel[n % 2][:, 0:P * (t + 1)], psum[:, n % 4, 0:P * (t + 1)], ACT.Relu
                                         ).then_inc(rel_ready, 1)
                    n += 1
            for u in range(UNIT["ka", 0], UNIT["qa", 7] + 1):
                copy_unit(u)
                if u == UNIT["qa", 0]:
                    act.wait_ge(va_turned, 1)
                    v = psum[:, 4, :].rearrange("p (t c) -> p t c", t=TT)
                    nc.scalar.activation(va, v, ACT.Copy)
                    nc.scalar.activation(va_hi[0:CHUNK], v[CHUNK:P], ACT.Copy).then_inc(va_copied, 1)

            def exps(n):
                kind, g, t, w0, w = item_shape(n)
                heads = 4 if kind == "A" else 2
                s = s_sb[n % 2][:, 0:heads * w].rearrange("p (h w) -> p h w", h=heads)
                act.wait_ge(negm_ready, n + 1)
                for h in range(heads):
                    ins = nc.scalar.activation(s[:, h, :], s[:, h, :], ACT.Exp, bias=negm[:, n % 4, h:h + 1],
                                               accum_out=den[:, n % 4, h:h + 1])
                if kind == "A":
                    ins = nc.scalar.activation(sink_e[:, n % 4, :], sink_e[:, n % 4, :], ACT.Exp)
                ins.then_inc(exp_done, 1)

            def copy_pt(n):
                kind, g, t, w0, w = item_shape(n)
                act.wait_ge(pt_done, n + 1)
                if n >= 2:
                    act.wait_ge(pv_done, n - 1)
                pt = pt_sb[n % 2]
                if kind == "A":
                    ins = nc.scalar.activation(pt[:, 0:512], psum[:, 4, :], ACT.Copy)
                    if t:
                        ins = nc.scalar.activation(pt[0:CHUNK, 512:1024], psum[0:CHUNK, 5, :], ACT.Copy)
                else:
                    ins = nc.scalar.activation(pt[:, 0:256 * (t + 1)],
                                               psum[:, 4:6, :].rearrange("p b c -> p (b c)")[:, 0:256 * (t + 1)],
                                               ACT.Copy)
                ins.then_inc(pt_copied, 1)

            def copy_o(n):
                kind, g, t, w0, w = item_shape(n)
                act.wait_ge(pv_done, n + 1)
                if kind == "A":
                    ins = nc.scalar.activation(qaT[:, 2 * g:2 * g + 2, t * P:(t + 1) * P],
                                               psum[:, 7, 0:256].rearrange("p (i c) -> p i c", i=2), ACT.Copy)
                else:
                    ins = nc.scalar.activation(qbT[:, g, t * P:(t + 1) * P], psum[:, 7, 0:P], ACT.Copy)
                ins.then_inc(o_copied, 1)

            exps(0)
            for n in range(len(ITEMS)):
                if n + 1 < len(ITEMS):
                    exps(n + 1)
                copy_pt(n)
                if n % 2:
                    if UNIT["qb", 0] + n // 2 == UNIT["gate", 0]:
                        act.wait_ge(rows_zeroed, 16)
                    copy_unit(UNIT["qb", 0] + n // 2)
                if n >= 1:
                    copy_o(n - 1)
            copy_o(len(ITEMS) - 1)

            for n, (heads, part) in enumerate([(qaT, branch_hi["a"]), (qbT, branch_hi["b"])]):
                for k in range(DT):
                    if n == 0 and k == 0:
                        act.wait_ge(o_copied, len(ITEMS))
                    nc.scalar.activation(part[:, k, :], heads[:, k, :], ACT.Copy).then_inc(o_high, 1)
            for c in range(22, len(CHUNKS)):
                high(c)
            for t in range(TT):
                act.wait_ge(x2_landed[t], 16)
                nc.scalar.activation(h1[:, t, :], h1[:, t, :], ACT.Copy, scale=ALPHA).then_inc(ax_ready, 1)

            def squares(i, t, ready, done):
                act.wait_ge(ready, t + 1)
                nc.scalar.activation(junk, h1[:, t, :], ACT.Square, bias=ln[:, i, 1, t:t + 1],
                                     accum_out=ln[:, i, 2, t:t + 1]).then_inc(done, 1)

            def copy_h1t(t):
                for h in range(2):
                    n = 2 * t + h
                    act.wait_ge(h1t_done, n + 1)
                    nc.scalar.activation(h1T[:, 4 * h:4 * h + 4, t * P:(t + 1) * P],
                                         psum[:, n % 2, :].rearrange("p (k c) -> p k c", k=4), ACT.Copy
                                         ).then_inc(h1t_copied, 1)

            junk = qbT.rearrange("p k c -> p (k c)")[:, 0:D]
            for t in range(TT):
                squares(0, t, mean_ready, ssq_ready)
                if t:
                    copy_h1t(t - 1)
            copy_h1t(TT - 1)
            act.wait_ge(gd_ready, 1)
            nc.scalar.activation(g4[:, 1], g4[:, 0], ACT.Exp).then_inc(ge_ready, 1)
            act.wait_ge(md_ready, 1)
            nc.scalar.activation(g1[:, 6, :], g1[:, 5, :], ACT.Exp).then_inc(me_ready, 1)
            act.wait_ge(h1_stored, 16 * TT)
            for t in range(TT):
                nc.scalar.activation(h1[:, t, :], h1[:, t, :], ACT.Copy, scale=ALPHA).then_inc(ah_ready, 1)

            def copy_xgt(n, s):
                act.wait_ge(xgt_done, n + 1)
                nc.scalar.activation(xgT[s % 2], psum[:, 0, :].rearrange("p (k c) -> p k c", k=DT), ACT.Copy
                                     ).then_inc(xgt_copied, 1)

            def expert(b, i, s):
                act.wait_ge(gu_done, b + 1)
                nc.scalar.activation(th[s % 2][0:CAP, :], psum[0:CAP, 2 + s % 2, 0:FF], ACT.Tanh, scale=0.5
                                     ).then_inc(th_done, 1)
                copy_xgt(b + 1, s + 1)
                act.wait_ge(d_done, b + 1)
                act.wait_ge(y_stored[s % 2], i * (EXS // 2 * 32) + (32 * (s // 2) + 1))
                nc.scalar.activation(y_sb[s % 2], psum[:, 4 + s % 2, :], ACT.Copy).then_inc(y_copied, 1)

            act.sem_inc(y_copied, 1)
            for p in range(2):
                act.sem_inc(y_stored[p], 1)
            copy_xgt(0, 0)
            blocks(act, expert)
            for t in range(TT):
                squares(1, t, mean2_ready, ssq2_ready)

        @block.vector
        def _(dve):
            step = Steps(dve, dve_step)
            V = nc.vector
            for n in range(2 * TT):
                dve.wait_ge(xt_high, n + 1)
                t, h = n // 2, n % 2
                part = slice(4 * h, 4 * h + 4), slice(t * P, (t + 1) * P)
                V.tensor_tensor(x_lo[:, part[0], part[1]], psum[:, n % 6, :].rearrange("p (k c) -> p k c", k=4),
                                x_hi[:, part[0], part[1]].bitcast(F32), ALU.subtract).then_inc(xt_split, 1)
            dve.wait_ge(abs_ready, 1)
            step(V.tensor_copy(strip[:, :], negd[:, 320:512]))
            step(V.memset(strip[0:CHUNK, 128:192], MASKED))
            step(V.memset(strip[CHUNK:P, 0:CHUNK], MASKED))
            step(V.tensor_copy(dm[0], negd[:, 384:512]))
            step(V.memset(dm[0][0:CHUNK, CHUNK:P], MASKED))
            dve.wait_ge(css_done, 1)
            V.tensor_scalar(var_c[:, :], psum[:, 5, 0:2 * TT].rearrange("p (t o) -> p t o", o=2)[:, :, 0],
                            1.0 / RANK, RMS_EPS, ALU.mult, ALU.add).then_inc(var_c_ready, 1)
            dve.wait_ge(rstd_c_ready, 1)
            for t in range(TT):
                V.tensor_scalar(rstd_diag[:, t * P:(t + 1) * P], ident[:, :], rstd_c[:, t:t + 1], None, ALU.mult
                                ).then_inc(diag_ready, 1)
            dve.wait_ge(rstd_spread, 1)
            dve.wait_ge(small_landed, 16 * 8)
            dve.wait_ge(unit_copied, UNIT["ckv", 0] + 1)
            V.scalar_tensor_tensor(cT, ckvT, kvg[:, 0:1], psum[:, 4, :], ALU.mult, ALU.mult).then_inc(c_ready, 1)
            dve.wait_ge(wi_copied, 1)
            n = 0
            for t in range(1, TT):
                w = P * (t + 1)
                for h in range(IH):
                    dve.wait_ge(rel_ready, n + 1)
                    if h:
                        dve.wait_ge(rel_added, n)
                        ins = V.scalar_tensor_tensor(work[t], rel[n % 2][:, 0:w], wis[:, t, h:h + 1], work[t],
                                                     ALU.mult, ALU.add)
                    else:
                        ins = V.tensor_scalar(work[t], rel[n % 2][:, 0:w], wis[:, t, 0:1], None, ALU.mult)
                    ins.then_inc(rel_added, 1)
                    n += 1
            dve.wait_ge(rel_added, n)
            for t in range(1, TT):
                w = P * (t + 1)
                step(V.memset(work[t][0:CHUNK, w - CHUNK:w], OUT_OF_REACH))
                for _ in range(TOPK // 8):
                    step(V.max(m8[:, t - 1, :], work[t]))
                    step(V.match_replace(work[t], m8[:, t - 1, :], work[t], TAKEN))
                step(V.tensor_scalar(work[t], work[t], 2 * OUT_OF_REACH, MASKED, ALU.is_gt, ALU.mult))
                step(V.tensor_tensor(dm[t], work[t], negd[:, 512 - w:512], ALU.add))

            def soften(n):
                kind, g, t, w0, w = item_shape(n)
                heads = 4 if kind == "A" else 2
                s = s_sb[n % 2][:, 0:heads * w].rearrange("p (h w) -> p h w", h=heads)
                dve.wait_ge(s_done, n + 1)
                if n >= 2:
                    dve.wait_ge(pt_done, n - 1)
                if kind == "A":
                    for h in range(4):
                        par, i = h // 2, h % 2
                        ins = V.scalar_tensor_tensor(s[:, h, :], strip[:, w0:192], SLOPE[4 * g + 2 * i + par],
                                                     psum[:, 2 * (n % 2) + par, 256 * i:256 * i + w],
                                                     ALU.mult, ALU.add)
                    ins.then_inc(s_taken, 1)
                else:
                    for par in range(2):
                        ins = V.scalar_tensor_tensor(s[:, par, :], dm[t], SLOPE[2 * g + par],
                                                     psum[:, 2 * (n % 2) + par, 0:w], ALU.mult, ALU.add)
                    ins.then_inc(s_taken, 1)
                dve.wait_ge(s_taken, n + 1)
                step(V.tensor_reduce(mx[:, n % 4, 0:heads], s, AX.X, ALU.max))
                if kind == "A":
                    step(V.tensor_tensor(mx[:, n % 4, :], mx[:, n % 4, :], sinks[:, g, :], ALU.max))
                    step(V.tensor_tensor(sink_e[:, n % 4, :], sinks[:, g, :], mx[:, n % 4, :], ALU.subtract))
                V.tensor_scalar(negm[:, n % 4, 0:heads], mx[:, n % 4, 0:heads], -1.0, None, ALU.mult).then_inc(negm_ready, 1)

            def normalise(n):
                kind, g, t, w0, w = item_shape(n)
                heads = 4 if kind == "A" else 2
                s = s_sb[n % 2][:, 0:heads * w].rearrange("p (h w) -> p h w", h=heads)
                dve.wait_ge(exp_done, n + 1)
                if kind == "A":
                    step(V.tensor_tensor(den[:, n % 4, :], den[:, n % 4, :], sink_e[:, n % 4, :], ALU.add))
                step(V.reciprocal(mx[:, n % 4, 0:heads], den[:, n % 4, 0:heads]))
                for h in range(heads):
                    ins = V.tensor_scalar(s[:, h, :], s[:, h, :], mx[:, n % 4, h:h + 1], None, ALU.mult)
                ins.then_inc(p_ready, 1)

            dve.wait_ge(sinks_ready, 4)
            soften(0)
            for n in range(len(ITEMS)):
                if n + 1 < len(ITEMS):
                    soften(n + 1)
                normalise(n)

            for n, (heads, hi, lo) in enumerate([(qaT, branch_hi["a"], branch_lo["a"]),
                                                 (qbT, branch_hi["b"], branch_lo["b"])]):
                for k in range(DT):
                    dve.wait_ge(o_high, DT * n + k + 1)
                    V.tensor_tensor(lo[:, k, :], heads[:, k, :], hi[:, k, :].bitcast(F32), ALU.subtract
                                    ).then_inc(o_split, 1)
            dve.wait_ge(unit_copied, UNIT["gate", 15] + 1)
            for m in range(8):
                for kind, g in (("a", gaT), ("b", gbT)):
                    u = UNIT[kind, m]
                    dve.wait_ge(unit_done, u + 1)
                    V.scalar_tensor_tensor(g[:, m, :], g[:, m, :], 1.0, psum[:, bank_of(u), :], ALU.add, ALU.mult
                                           ).then_inc(merged_read, 1)
                dve.wait_ge(merged_read, 2 * m + 2)
                V.tensor_tensor(gaT[:, m, :], gaT[:, m, :], gbT[:, m, :], ALU.add).then_inc(m_ready, 1)

            def norm(i, t, read, mean, ssq, var, rstd, g, b, ready):
                V.tensor_scalar(ln[:, i, 1, t:t + 1], ln[:, i, 0, t:t + 1], -1.0 / D, None, ALU.mult
                                ).then_inc(mean, 1)
                dve.wait_ge(ssq, t + 1)
                V.tensor_scalar(ln[:, i, 3, t:t + 1], ln[:, i, 2, t:t + 1], 1.0 / D, LN_EPS, ALU.mult, ALU.add
                                ).then_inc(var, 1)
                dve.wait_ge(rstd, t + 1)
                step(V.tensor_scalar(h1[:, t, :], h1[:, t, :], ln[:, i, 1, t:t + 1], ln[:, i, 4, t:t + 1],
                                     ALU.add, ALU.mult))
                step(V.tensor_tensor(h1[:, t, :], h1[:, t, :], g, ALU.mult))
                V.tensor_tensor(h1[:, t, :], h1[:, t, :], b, ALU.add).then_inc(ready, 1)

            dve.wait_ge(ln1_landed, 32)
            for t in range(TT):
                u = UNIT["out", 2 * t + 1]
                dve.wait_ge(ax_ready, t + 1)
                dve.wait_ge(unit_done, u + 1)
                V.scalar_tensor_tensor(h1[:, t, :], psum[:, bank_of(u) - 1:bank_of(u) + 1, :].rearrange(
                    "p b c -> p (b c)"), 0.5, h1[:, t, :], ALU.mult, ALU.add, accum_out=ln[:, 0, 0, t:t + 1]
                    ).then_inc(r_ready, 1)
                dve.wait_ge(r_ready, t + 1)
                norm(0, t, r_ready, mean_ready, ssq_ready, var_ready, rstd_ready, ln1g, ln1b, h1_ready)

            N36 = NG + NE
            dve.wait_ge(routed, 1)
            step(V.tensor_tensor(lg[:, :, :], psum[:, 2, 0:TT * N36].rearrange("p (t c) -> p t c", t=TT),
                                 rb[:, :].unsqueeze(1).to_broadcast([P, TT, N36]), ALU.add))

            def row(v):
                return v.unsqueeze(2)

            gl = lg[:, :, 0:NG]
            step(V.tensor_reduce(g1[:, 0, :], gl, AX.X, ALU.max))
            V.tensor_tensor(g4[:, 0], gl, row(g1[:, 0, :]).to_broadcast([P, TT, NG]), ALU.subtract
                            ).then_inc(gd_ready, 1)

            def first_best(dst, score, best, v, m, n):
                step(V.tensor_tensor(v, score, row(best).to_broadcast([P, TT, n]), ALU.is_equal))
                step(V.tensor_tensor(v, v, desc[:, 0:n].unsqueeze(1).to_broadcast([P, TT, n]), ALU.mult))
                step(V.tensor_reduce(m, v, AX.X, ALU.max))
                step(V.tensor_tensor(dst, v, row(m).to_broadcast([P, TT, n]), ALU.is_equal))

            first_best(g4[:, 3], gl, g1[:, 0, :], g4[:, 2], g1[:, 1, :], NG)
            step(V.tensor_scalar(g4[:, 3], g4[:, 3], -MASKED, MASKED, ALU.mult, ALU.add))
            step(V.tensor_tensor(e32[:, 0].rearrange("p t (g e) -> p t g e", g=NG),
                                 lg[:, :, NG:].rearrange("p t (g e) -> p t g e", g=NG),
                                 g4[:, 3].unsqueeze(3).to_broadcast([P, TT, NG, EPG]), ALU.add))
            step(V.tensor_reduce(g1[:, 2, :], e32[:, 0], AX.X, ALU.max))
            first_best(oh[:, 0], e32[:, 0], g1[:, 2, :], e32[:, 1], g1[:, 3, :], NE)
            step(V.scalar_tensor_tensor(e32[:, 2], oh[:, 0], 2 * MASKED, e32[:, 0], ALU.mult, ALU.add))
            step(V.tensor_reduce(g1[:, 4, :], e32[:, 2], AX.X, ALU.max))
            first_best(oh[:, 1], e32[:, 2], g1[:, 4, :], e32[:, 3], g1[:, 3, :], NE)
            V.tensor_tensor(oh[:, 2], oh[:, 0], oh[:, 1], ALU.add).then_inc(oh_ready, 1)
            V.tensor_tensor(g1[:, 5, :], g1[:, 4, :], g1[:, 2, :], ALU.subtract).then_inc(md_ready, 1)
            dve.wait_ge(ranked, 1)
            step(V.tensor_copy(e32[:, 4].rearrange("p t e -> p (t e)"), psum[:, 3, 0:TT * NE]))
            step(V.tensor_copy(cnt[:, 0, :], psum[:, 3, TT * NE:(TT + 1) * NE]))
            step(V.tensor_scalar(cnt[:, 1, :], cnt[:, 0, :], float(CAP), None, ALU.is_gt))
            for m in range(2, T // CAP):
                step(V.scalar_tensor_tensor(cnt[:, 1, :], cnt[:, 0, :], float(CAP * m), cnt[:, 1, :],
                                            ALU.is_gt, ALU.add))
            step(V.tensor_tensor_scan(cnt[:, 2, :], ones[:, 0:NE], cnt[:, 1, :], 0.0, ALU.mult, ALU.add))
            step(V.tensor_tensor(cnt[:, 3, :], cnt[:, 2, :], cnt[:, 1, :], ALU.subtract))
            step(V.tensor_scalar(cnt[:, 3, :], cnt[:, 3, :], float(CAP), float(CAP * (NE - 1)), ALU.mult, ALU.add))
            step(V.tensor_tensor(cnt[:, 3, :], cnt[:, 3, :], base0[:, :], ALU.subtract))
            step(V.tensor_scalar(e32[:, 5], e32[:, 4], float(CAP), None, ALU.is_ge))
            step(V.tensor_tensor(e32[:, 5], e32[:, 5], cnt[:, 3, :].unsqueeze(1).to_broadcast([P, TT, NE]), ALU.mult))
            step(V.tensor_tensor(e32[:, 4], e32[:, 4], base0[:, :].unsqueeze(1).to_broadcast([P, TT, NE]), ALU.add))
            step(V.tensor_tensor(e32[:, 4], e32[:, 4], e32[:, 5], ALU.add))
            for k in range(2):
                step(V.tensor_tensor(e32[:, 6], oh[:, k], e32[:, 4], ALU.mult))
                step(V.tensor_reduce(slot_f[:, k, :], e32[:, 6], AX.X, ALU.add))
            V.tensor_copy(slot_i[:, :, :], slot_f[:, :, :]).then_inc(slots_ready, 1)
            step(V.tensor_tensor(over_cmp[:, :, :], cnt[0:1, 2, :].unsqueeze(1).to_broadcast([1, MAX_OVER, NE]),
                                 jrow[:, :].unsqueeze(2).to_broadcast([1, MAX_OVER, NE]), ALU.is_le))
            step(V.tensor_reduce(over_f[:, 0:MAX_OVER], over_cmp[:, :, :], AX.X, ALU.add))
            step(V.tensor_scalar(over_f[:, 0:MAX_OVER], over_f[:, 0:MAX_OVER], float(NE - 1), None, ALU.min))
            step(V.tensor_copy(over_f[:, MAX_OVER:], cnt[0:1, 2, NE - 1:NE]))
            V.tensor_copy(over_i[:, :], over_f[:, :]).then_inc(over_ready, 1)
            dve.wait_ge(ge_ready, 1)
            dve.wait_ge(me_ready, 1)
            step(V.tensor_reduce(g1[:, 7, :], g4[:, 1], AX.X, ALU.add))
            step(V.tensor_scalar(g1[:, 8, :], g1[:, 6, :], 1.0, None, ALU.add))
            step(V.tensor_tensor(g1[:, 7, :], g1[:, 7, :], g1[:, 8, :], ALU.mult))
            step(V.reciprocal(g1[:, 8, :], g1[:, 7, :]))
            step(V.tensor_scalar(comb[:, 0, :], g1[:, 8, :], 0.5, None, ALU.mult))
            step(V.tensor_tensor(comb[:, 1, :], comb[:, 0, :], g1[:, 6, :], ALU.mult))
            dve.wait_ge(table_t, 1)
            V.tensor_copy(tok_i[:, :], psum[0:CAP, 0, 0:NBLK + 1]).then_inc(tok_ready, 1)

            def expert(b, i, s):
                dve.wait_ge(th_done, b + 1)
                V.scalar_tensor_tensor(gated[s % 2][CAP:P, :], th[s % 2][0:CAP, :], 1.0,
                                       psum[0:CAP, 2 + s % 2, 0:FF], ALU.add, ALU.mult).then_inc(gated_ready, 1)
                dve.wait_ge(gated_ready, b + 1)
                V.tensor_tensor(hid[s % 2][0:CAP, :], gated[s % 2][CAP:P, :], psum[CAP:P, 2 + s % 2, 0:FF], ALU.mult
                                ).then_inc(h_ready, 1)
                dve.wait_ge(ht_done, b + 1)
                V.tensor_copy(hidT[s % 2], psum[:, 1, 0:2 * CAP].rearrange("p (k c) -> p k c", k=2)
                              ).then_inc(ht_copied, 1)

            blocks(dve, expert)
            dve.wait_ge(ah_ready, TT)
            dve.wait_ge(ln2_landed, 32)
            for t in range(TT):
                dve.wait_ge(yk_landed[t][0], 16)
                step(V.scalar_tensor_tensor(h1[:, t, :], yk[t][0], comb[:, 0, t:t + 1], h1[:, t, :],
                                            ALU.mult, ALU.add))
                dve.wait_ge(yk_landed[t][1], 16)
                V.scalar_tensor_tensor(h1[:, t, :], yk[t][1], comb[:, 1, t:t + 1], h1[:, t, :],
                                       ALU.mult, ALU.add, accum_out=ln[:, 1, 0, t:t + 1]).then_inc(r2_ready, 1)
                dve.wait_ge(r2_ready, t + 1)
                norm(1, t, r2_ready, mean2_ready, ssq2_ready, var2_ready, rstd2_ready, ln2g, ln2b, out_ready)


_INS = ['x', 'w_in', 'a_sinks', 'kv_norm_g', 'w_uk', 'w_uv', 'w_branch_a', 'w_branch_b', 'w_out', 'ln1_g', 'ln1_b',
        'router_group_w', 'router_group_b', 'router_expert_w', 'router_expert_b', 'w_gate', 'w_up', 'w_down',
        'ln2_g', 'ln2_b']
_OUTS = [((1, T, D), 'float32')]


def kernel(**inputs):
    import numpy as _np
    import concourse.bacc as _bacc
    from concourse import mybir as _mybir
    from concourse.bass_utils import run_bass_kernel_spmd as _run

    nc = _bacc.Bacc("TRN2", target_bir_lowering=False, num_devices=1)
    arrays, args = {}, []
    for name in _INS:
        a = _np.ascontiguousarray(inputs[name])
        if name in ('w_gate', 'w_up', 'w_down'):
            a = a.reshape(a.shape[0], NE, *a.shape[3:])
        arrays[f"in_{name}_dram"] = a
        args.append(nc.dram_tensor(f"in_{name}_dram", a.shape, _mybir.dt.from_np(a.dtype), kind="ExternalInput").ap())
    for i, (shape, dtype) in enumerate(_OUTS):
        dt = _mybir.dt.from_np(_np.dtype(dtype))
        args.append(nc.dram_tensor(f"out_{i}_dram", shape, dt, kind="ExternalOutput").ap())
    build(nc, *args)
    r = _run(nc, [arrays], core_ids=[0])
    got = tuple(r.results[0][f"out_{i}_dram"] for i in range(len(_OUTS)))
    return got[0]
```

```python
import concourse.bass as bass
from concourse import mybir
from contextlib import ExitStack
import math

F32 = mybir.dt.float32
F32R = mybir.dt.float32r
F16 = mybir.dt.float16
BF16 = mybir.dt.bfloat16
I32 = mybir.dt.int32
ALU = mybir.AluOpType
ACT = mybir.ActivationFunctionType
AX = mybir.AxisListType

P = 128
T, D = 512, 1024
TT, DT = T // P, D // P
CHUNK, HD = 64, 64
AH, AG = 16, 2
BH = 16
RANK = 128
IH = 8
TOPK = min(256, T // 4)
NG, EPG, FF = 4, 8, 256
NE = NG * EPG
CAP = 64
N_TOP = 2
PAIRS = N_TOP * T
MAX_OVER = 18
NBLK = NE + MAX_OVER
NTAB = NBLK + 2
MORE = T // CAP - 1
ALPHA = 2.0 ** 0.25
LN_EPS, RMS_EPS = 1e-5, 1e-6
IDX_SCALE = (HD ** -0.5) * (IH ** -0.5)
MASKED = -1e30
OUT_OF_REACH = -1e38
TAKEN = -3e38

C_QA = 0
C_KA = C_QA + AH * HD
C_VA = C_KA + AG * HD
C_QB = C_VA + AG * HD
C_CKV = C_QB + BH * HD
C_QI = C_CKV + RANK
C_KI = C_QI + IH * HD
C_WI = C_KI + HD
C_GA = C_WI + IH
C_GB = C_GA + D
C_END = C_GB + D

SLOPE = [2.0 ** (-8.0 * (h + 1) / 16) for h in range(16)]
WCOLS = 256
WPART = DT * WCOLS
EXW = DT * 2 * FF + 2 * D


def weight_chunks():
    out = [("in", C_CKV + WCOLS * i) for i in range(3)] + [("in", C_KA)]
    out += [("in", C_QA + WCOLS * i) for i in range(4)]
    out += [("in", C_QB + WCOLS * i) for i in range(4)]
    out += [("in", C_GA + WCOLS * i) for i in range(8)]
    for i in range(4):
        out += [("a", WCOLS * i), ("b", WCOLS * i)]
    return out


def units():
    out = [("ckv", 0, 0, 0), ("qi", 0, 0, 128), ("qi", 1, 1, 0), ("qi", 2, 1, 128), ("qi", 3, 2, 0)]
    out += [("ki", 0, 2, 128)]
    out += [("ka", 0, 3, 0), ("va", 0, 3, 128)]
    out += [("qa", m, 4 + m // 2, 128 * (m % 2)) for m in range(8)]
    out += [("qb", m, 8 + m // 2, 128 * (m % 2)) for m in range(8)]
    out += [("gate", m, 12 + m // 2, 128 * (m % 2)) for m in range(16)]
    for i in range(4):
        out += [("a", 2 * i + j, 20 + 2 * i, 128 * j) for j in range(2)]
        out += [("b", 2 * i + j, 21 + 2 * i, 128 * j) for j in range(2)]
    out += [("out", 2 * t + i, None, 512 * i) for t in range(TT) for i in range(2)]
    return out


CHUNKS, UNITS = weight_chunks(), units()
UNIT = {(kind, i): n for n, (kind, i, _, _) in enumerate(UNITS)}
LAST_OF_CHUNK = {c: n for n, (_, _, c, _) in enumerate(UNITS)}
SPLIT = 6
RING = 3
EXS = 6
ZERO_AFTER = range(8, 8 + MAX_OVER * CAP // P)
WO_AFTER = {23 + i: range(2 * i, 2 * i + 2) for i in range(SPLIT // 2)}
XGS = 3


def bank_of(u):
    kind, i, _, _ = UNITS[u]
    if kind == "out":
        return 4 + 2 * ((i // 2) % 2) + i % 2
    if kind in "ab":
        return 2 * (i % 2) + (kind == "b")
    if kind in ("qb", "gate"):
        return 6
    return 6 + u % 2


ITEMS = [("A", q, t) for q in range(4) for t in range(TT)] + [("B", j, t) for t in range(TT) for j in range(8)]


def build(nc, x, w_in, a_sinks, kv_norm_g, w_uk, w_uv, w_branch_a, w_branch_b, w_out, ln1_g, ln1_b,
          rg_w, rg_b, re_w, re_b, w_gate, w_up, w_down, ln2_g, ln2_b, out):
    ctx = ExitStack()
    with ctx:
        sem = lambda name: ctx.enter_context(nc.semaphore(name))
        sb = lambda name, shape, dt=F32: ctx.enter_context(nc.sbuf_tensor(name, shape, dt))

        h1_dram = nc.dram_tensor("h1_rows", (T, D), F32, kind="Internal").ap()
        y_dram = nc.dram_tensor("expert_rows", (NBLK * CAP, D), F32, kind="Internal").ap()

        ARENA = EXS * EXW + 2 * D + DT * T + TT * D
        arena_at = -(-nc.sbuf_base // 32) * 32
        sb("arena", [P, ARENA])

        def shaped(v, shape):
            if len(shape) == 2:
                return v.rearrange("p (a b) -> p a b", a=shape[0])
            if len(shape) == 3:
                return v.rearrange("p (a b c) -> p a b c", a=shape[0], b=shape[1])
            return v

        names = [0]

        def view(off, *shape, dt=F32):
            names[0] += 1
            v = nc.alloc_sbuf_tensor_at(f"arena_{names[0]}", [P, math.prod(shape)], dt, offset=arena_at + 4 * off)
            return shaped(v[:, :], shape)

        def view_r(off, *shape):
            return view(off, *shape, dt=F32R)

        at = [0]

        def region(n):
            at[0] += n
            return at[0] - n

        r_ring = region(RING * 2 * WPART)
        r_gb = region(DT * T)
        r_xlo = region(DT * T)
        r_att = region(7296)
        r_qi = region(4 * T)
        r_sp = region(4096)
        r_zero = region(896)
        r_xhi = region(DT * T)
        r_qb = region(DT * T)
        r_qa = region(DT * T)
        assert at[0] == ARENA, at
        ga_at = -(-nc.sbuf_base // 32) * 32
        ga_t = sb("gate_a_T", [P, DT, T])
        slot_off = [r_ring + 2 * WPART * ((i + 2) % RING) for i in range(RING)]
        w_raw = [view(f, DT, WCOLS) for f in slot_off]
        w_lo = [view_r(f, DT, WCOLS) for f in slot_off]
        w_hi = [view_r(f + WPART, DT, WCOLS) for f in slot_off]
        gaT = ga_t[:, :, :]
        gbT = view(r_gb, DT, T)
        x_nat = view(r_gb, TT, D)
        o = r_att

        def take(n):
            nonlocal o
            o += n
            return o - n

        kiT = view(take(512), T)
        kaT = view(take(1024), AG, T)
        va = view(take(512), TT, AG * HD)
        va_hi = view(take(512), TT, AG * HD)
        ckvT = view(take(512), T)
        cT = view(take(512), T)
        kbT = view(take(512), T)
        vb = view(take(256), TT, HD)
        negd = view(take(512), 512)
        dm_off = take(1280)
        work_off = take(1152)
        assert o == r_qi
        dm = [view(dm_off + P * t * (t + 1) // 2, P * (t + 1)) for t in range(TT)]
        work = [None] + [view(work_off + P * (t * (t + 1) // 2 - 1), P * (t + 1)) for t in range(1, TT)]
        qiT = view(r_qi, 4, T)
        rel = [view(r_sp + 512 * i, 512) for i in range(2)]
        c_sq, rstd_diag, wiT = (view(r_sp + 1024 + 512 * i, 512) for i in range(3))
        s_sb = [view(r_sp + 1024 * i, 1024) for i in range(2)]
        pt_sb = [view(r_sp + 2048 + 1024 * i, 1024) for i in range(2)]
        x_hi, x_lo = view_r(r_xhi, DT, T), view_r(r_xlo, DT, T)
        qaT = view(r_qa, DT, T)
        qbT = view(r_qb, DT, T)
        branch_hi = {"a": x_hi, "b": x_lo}
        branch_lo = {"a": view_r(r_qa, DT, T), "b": view_r(r_qb, DT, T)}
        ln1g, ln1b = view(0, D), view(D, D)
        ln2g, ln2b = ln1g, ln1b
        w_o = view(r_xhi - DT * D, DT, D)
        w_o_hi = view_r(r_att, SPLIT, D)
        w_o_lo = view_r(r_xhi - DT * D, SPLIT, D)
        m_hi = view_r(r_qb + D, SPLIT, T)
        m_lo = shaped(nc.alloc_sbuf_tensor_at("merged_low", [P, SPLIT * T], F32R, offset=ga_at)[:, :], (SPLIT, T))
        assert r_att + SPLIT * D <= r_xhi - DT * D
        h1 = view(r_qa, TT, D)
        h1T = view(r_xhi, DT, T)
        xg = [view(r_qb + D * i, D) for i in range(XGS)]
        ex_off = [2 * D + EXW * i for i in range(EXS)]
        assert ex_off[-1] + EXW == r_qb and ex_off[3] + EXW <= r_xhi - DT * D
        assert ex_off[3] >= r_att and ex_off[5] + EXW > r_xhi
        ex_gu = [view(f, 2, DT, FF) for f in ex_off]
        ex_d = [view(f + 2 * DT * FF, 2, D) for f in ex_off]
        moe = ga_t[:, :, :].rearrange("p k c -> p (k c)")

        def small(off, *shape):
            return shaped(moe[:, off:off + math.prod(shape)], shape)

        xgT = [small(512 * i, DT, CAP) for i in range(2)]
        th = [small(1024 + 256 * i, FF) for i in range(2)]
        gated = [small(1536 + 256 * i, FF) for i in range(2)]
        hid = [small(2048 + 256 * i, FF) for i in range(2)]
        hidT = [small(2560 + 128 * i, 2, CAP) for i in range(2)]
        y_sb = [small(2816 + 512 * i, 512) for i in range(2)]
        squared = [[view(r_qb, D)] * TT, [view(ex_off[3] + D * t, D) for t in range(TT)]]
        yk = [[view(2 * D + D * (2 * t + k), D) for k in range(2)] for t in range(TT)]

        ident = sb("ident", [P, P])
        ones = sb("ones", [P, P])
        upper = sb("upper", [P, P])
        wuk = sb("wuk", [P, HD])
        wuv = sb("wuv", [P, HD])
        kvg = sb("kvg", [P, 1])
        var_c = sb("var_c", [P, TT])
        rstd_c = sb("rstd_c", [P, TT])
        sinks_row = sb("sinks_row", [P, AH])
        sinks = sb("sinks", [P, 4, 4])
        rw = sb("rw", [P, DT, NG + NE])
        rb = sb("rb", [P, NG + NE])
        wis = sb("wis", [P, TT, IH])
        m8 = sb("m8", [P, 3, 8])
        half_neg = sb("half_neg", [P, 4])
        strip = sb("strip", [P, 192])
        mx = sb("mx", [P, 4, 4])
        negm = sb("negm", [P, 4, 4])
        den = sb("den", [P, 4, 4])
        sink_e = sb("sink_e", [P, 4, 4])
        ln = sb("ln", [P, 2, 5, 4])
        r_route = r_qb + XGS * D
        lg = view(r_route, TT, NG + NE)
        g4 = view(r_route + 144, 4, TT * NG).rearrange("p a (t g) -> p a t g", t=TT)
        g1 = view(r_route + 208, 10, TT)
        cnt = view(r_route + 248, 4, NE)
        e32 = view(r_qb, 4, TT * NE).rearrange("p a (t e) -> p a t e", t=TT)
        slot_of = view(r_qb + 512, TT, NE)
        paid = view(r_qb + 640, TT, NE)
        oh = view(r_qb + 1024, 2, TT * NE).rearrange("p a (t e) -> p a t e", t=TT)
        oh_both = view(r_qb + 1280, TT * NE, dt=BF16).rearrange("p (t e) -> p t e", t=TT)
        full_cmp = view(r_qb + 1344, NE, MORE)
        over_cmp = view(r_route + 376, MAX_OVER, NE)[0:1]
        in_slot = view(r_qb + 2144, N_TOP * TT, CAP, dt=F16)
        in_block = view(r_qb + 2400, N_TOP * TT, NTAB, dt=F16)
        picked = view(r_qb + 2608, 2, TT * NE)
        desc = sb("desc", [P, NE])
        base0 = sb("base0", [P, NE])
        jrow = sb("jrow", [1, MAX_OVER])
        over_f = sb("over_f", [1, MAX_OVER + 1])
        over_i = sb("over_i", [1, MAX_OVER + 1], I32)
        slot_f = sb("slot_f", [P, 2, TT])
        slot_i = sb("slot_i", [P, 2, TT], I32)
        comb = sb("comb", [P, 2, TT])
        tokid = sb("tokid", [P, TT])
        base1 = sb("base1", [P, NE])
        fulls = sb("fulls", [P, MORE])
        col_s = sb("col_s", [P, CAP])
        col_b = sb("col_b", [P, NTAB])
        pair_s = sb("pair_s", [P, N_TOP * TT])
        pair_i = sb("pair_i", [P, N_TOP * TT], I32)
        pair_b = sb("pair_b", [P, N_TOP * TT])
        upper_h = sb("upper_h", [P, P], BF16)
        ones_h = sb("ones_h", [P, P], BF16)
        tok_i = sb("tok_i", [CAP, NBLK + 1], I32)
        idx = [sb(f"idx{i}", [CAP, 1], I32) for i in range(XGS)]
        psum = ctx.enter_context(nc.psum_tensor("psum", [P, 8, 512], F32))

        x_landed = [sem(f"x_landed{t}") for t in range(TT)]
        small_landed = sem("small_landed")
        ln1_landed, ln2_landed, x2_landed = sem("ln1_landed"), sem("ln2_landed"), [sem(f"x2_landed{t}") for t in range(TT)]
        w_high, w_split, wo_landed = sem("w_high"), sem("w_split"), sem("wo_landed")
        o_high, o_split = sem("o_high"), sem("o_split")
        wo_high, wo_split, m_high, m_split = sem("wo_high"), sem("wo_split"), sem("m_high"), sem("m_split")
        w_landed = [sem(f"w_landed{i}") for i in range(RING)]
        const_ready = sem("const_ready")
        pool_step = sem("pool_step")
        abs_ready, sinks_ready = sem("abs_ready"), sem("sinks_ready")
        xt_done, xt_high, xt_split = sem("xt_done"), sem("xt_high"), sem("xt_split")
        unit_done, unit_copied = sem("unit_done"), sem("unit_copied")
        act_step, dve_step = sem("act_step"), sem("dve_step")
        csq_ready, css_done, var_c_ready, rstd_c_ready, diag_ready, rstd_spread, c_ready = (
            sem("csq_ready"), sem("css_done"), sem("var_c_ready"), sem("rstd_c_ready"),
            sem("diag_ready"), sem("rstd_spread"), sem("c_ready"))
        c_done, c_copied = sem("c_done"), sem("c_copied")
        wi_turned, wi_copied, va_turned, va_copied = (sem("wi_turned"), sem("wi_copied"), sem("va_turned"),
                                                      sem("va_copied"))
        idx_scored, rel_ready, rel_added = sem("idx_scored"), sem("rel_ready"), sem("rel_added")
        s_done, s_taken, negm_ready, exp_done = sem("s_done"), sem("s_taken"), sem("negm_ready"), sem("exp_done")
        p_ready, pt_done, pt_copied = sem("p_ready"), sem("pt_done"), sem("pt_copied")
        pv_done, o_copied = sem("pv_done"), sem("o_copied")
        merged_read, m_ready = sem("merged_read"), sem("m_ready")
        ax_ready = sem("ax_ready")
        r_ready, mean_ready, ssq_ready, var_ready, rstd_ready, h1_ready = (
            sem("r_ready"), sem("mean_ready"), sem("ssq_ready"), sem("var_ready"), sem("rstd_ready"),
            sem("h1_ready"))
        h1_stored, h1t_done, h1t_copied = sem("h1_stored"), sem("h1t_done"), sem("h1t_copied")
        routed, gd_ready, ge_ready, md_ready, me_ready = (sem("routed"), sem("gd_ready"), sem("ge_ready"),
                                                          sem("md_ready"), sem("me_ready"))
        oh_ready, ranked, slots_ready, over_ready = (sem("oh_ready"), sem("ranked"), sem("slots_ready"),
                                                     sem("over_ready"))
        zero_ready, pairs_ready, table_done, tok_ready = (sem("zero_ready"), sem("pairs_ready"), sem("table_done"),
                                                          sem("tok_ready"))
        ah_ready = sem("ah_ready")
        gu_landed = [sem(f"gu_landed{i}") for i in range(EXS)]
        d_landed = [sem(f"d_landed{i}") for i in range(EXS)]
        xg_landed = [sem(f"xg_landed{i}") for i in range(XGS)]
        idx_ready = sem("idx_ready")
        xgt_done, xgt_copied, gu_done, th_done, h_ready, ht_done, ht_copied, d_done, y_copied = (
            sem("xgt_done"), sem("xgt_copied"), sem("gu_done"), sem("th_done"), sem("h_ready"), sem("ht_done"),
            sem("ht_copied"), sem("d_done"), sem("y_copied"))
        gated_ready, rows_zeroed = sem("gated_ready"), sem("rows_zeroed")
        pe_passed, pool_passed = sem("pe_passed"), sem("pool_passed")
        y_stored = [sem(f"y_stored{i}") for i in range(2)]
        yk_landed = [[sem(f"yk_landed{i}{k}") for k in range(2)] for i in range(TT)]
        last_ready = sem("last_ready")
        offset2_ready, normed2_ready, scaled2_ready = (sem("offset2_ready"), sem("normed2_ready"),
                                                       sem("scaled2_ready"))
        r2_ready, mean2_ready, ssq2_ready, var2_ready, rstd2_ready, out_ready, out_stored = (
            sem("r2_ready"), sem("mean2_ready"), sem("ssq2_ready"), sem("var2_ready"), sem("rstd2_ready"),
            sem("out_ready"), sem("out_stored"))

        CONSTS = 14

        class Steps:

            def __init__(self, eng, s, count=0):
                self.eng, self.s, self.count = eng, s, count

            def __call__(self, ins):
                self.count += 1
                ins.then_inc(self.s, 1)
                self.eng.wait_ge(self.s, self.count)

        def item_shape(n):
            kind, g, t = ITEMS[n]
            if kind == "A":
                w0 = 0 if t else CHUNK
                return kind, g, t, w0, 192 - w0
            return kind, g, t, 0, P * (t + 1)

        def unit_wait(eng, u):
            before = [v for v in range(u) if bank_of(v) == bank_of(u)]
            kind = UNITS[u][0]
            if kind in ("a", "b"):
                if UNITS[u][1] >= 2:
                    eng.wait_ge(merged_read, before[-1] - UNIT["a", 0] + 1)
            elif kind == "out":
                if UNITS[u][1] >= 4:
                    eng.wait_ge(r_ready, UNITS[u][1] // 2 - 1)
            elif before:
                eng.wait_ge(unit_copied, before[-1] + 1)

        def blocks(eng, finish, start=None):
            if start:
                start(0, 0, 0)
            with eng.Fori(0, NE // EXS) as i:
                for s in range(EXS):
                    if start:
                        start(i * EXS + (s + 1), i, s + 1)
                    finish(i * EXS + s, i, s)
            for b in range(NE // EXS * EXS, NE):
                i, s = b // EXS, b % EXS
                if start and b + 1 < NE:
                    start(b + 1, i, s + 1)
                finish(b, i, s)
            eng.wait_ge(over_ready, 1)
            n_over = eng.value_load(over_i[0:1, MAX_OVER:MAX_OVER + 1], min_val=0, max_val=MAX_OVER - 1)
            with eng.If(n_over > 0):
                with eng.Fori(NE // EXS, NBLK // EXS) as i:
                    for s in range(NE % EXS, NE % EXS + EXS):
                        if start:
                            start(i * EXS + s, i, s)
                        finish(i * EXS + s, i, s)

        block = ctx.enter_context(nc.Block())

        @block.sync
        def _(sp):
            mats = {"in": w_in, "a": w_branch_a, "b": w_branch_b}

            def chunk(c):
                mat, c0 = CHUNKS[c]
                if c >= RING:
                    sp.wait_ge(unit_done, LAST_OF_CHUNK[c - RING] + 1)
                sp.dma_start(w_raw[c % RING], mats[mat][0, :, c0:c0 + WCOLS].rearrange("(k p) n -> p k n", p=P)
                             ).then_inc(w_landed[c % RING], 16)

            chunk(0)
            for t in range(TT):
                sp.dma_start(x_nat[:, t, :], x[0, t * P:(t + 1) * P, :]).then_inc(x_landed[t], 16)
            chunk(1)
            small = [(wuk[:, :], w_uk[0]), (wuv[:, :], w_uv[0]), (kvg[:, :], kv_norm_g[0].unsqueeze(1)),
                     (rw[:, :, 0:NG], rg_w[0].rearrange("(k p) g -> p k g", p=P)),
                     (rw[:, :, NG:], re_w[0].rearrange("(k p) g e -> p k (g e)", p=P)),
                     (rb[:, 0:NG], rg_b[0].partition_broadcast(P)),
                     (rb[:, NG:], re_b[0].rearrange("g e -> (g e)").partition_broadcast(P)),
                     (sinks_row[:, :], a_sinks[0].partition_broadcast(P))]
            for dst, src in small:
                sp.dma_start(dst, src).then_inc(small_landed, 16)
            for c in range(2, 23):
                chunk(c)

            def gate_up(e, slot):
                sp.dma_start(ex_gu[slot][:, 0].rearrange("p k f -> p (k f)"),
                             w_gate[0, e].rearrange("(p k) f -> p (k f)", p=P)).then_inc(gu_landed[slot], 16)
                sp.dma_start(ex_gu[slot][:, 1].rearrange("p k f -> p (k f)"),
                             w_up[0, e].rearrange("(p k) f -> p (k f)", p=P)).then_inc(gu_landed[slot], 16)

            def down(e, slot):
                sp.dma_start(ex_d[slot].rearrange("p k n -> p (k n)"),
                             w_down[0, e].rearrange("(p k) n -> p (k n)", p=P)).then_inc(d_landed[slot], 16)

            def expert(e, slot):
                gate_up(e, slot)
                down(e, slot)

            sp.wait_ge(o_copied, len(ITEMS))
            sp.wait_ge(rows_zeroed, 16 * len(ZERO_AFTER))
            for h in range(2):
                rows = slice(h * D // 2, (h + 1) * D // 2)
                sp.dma_start(w_o[:, h * DT // 2:(h + 1) * DT // 2, :],
                             w_out[0, rows, :].rearrange("(k p) n -> p k n", p=P)).then_inc(wo_landed, 16)
                chunk(23 + h)
            for c in range(25, len(CHUNKS)):
                chunk(c)
            sp.wait_ge(unit_done, LAST_OF_CHUNK[25] + 1)
            sp.dma_start(ln1g, ln1_g[0].partition_broadcast(P)).then_inc(ln1_landed, 16)
            sp.dma_start(ln1b, ln1_b[0].partition_broadcast(P)).then_inc(ln1_landed, 16)
            sp.wait_ge(unit_done, UNIT["a", 7] + 1)
            for t in range(TT):
                sp.dma_start(h1[:, t, :], x[0, t * P:(t + 1) * P, :]).then_inc(x2_landed[t], 16)
            sp.wait_ge(unit_done, UNIT["b", 7] + 1)
            expert(0, 0)
            sp.wait_ge(m_ready, 8)
            expert(1, 1)
            expert(2, 2)
            for t in range(TT):
                if t == TT - 1:
                    sp.wait_ge(unit_done, UNIT["out", 7] + 1)
                    expert(3, 3)
                sp.wait_ge(h1_ready, t + 1)
                sp.dma_start(h1_dram[t * P:(t + 1) * P, :], h1[:, t, :]).then_inc(h1_stored, 16)
            expert(4, 4)
            sp.wait_ge(routed, 2)
            for g in range(XGS):
                sp.wait_ge(xg_landed[g], 16)
            expert(5, 5)

            def store_y(b, s):
                sp.wait_ge(y_copied, b + 2)
                for half in range(2):
                    sp.dma_start(y_dram[bass.ds(b * CAP, CAP), half * 512:(half + 1) * 512],
                                 y_sb[s % 2][half * CAP:(half + 1) * CAP, :]).then_inc(y_stored[s % 2], 16)

            def refill_gate_up(b, s):
                sp.wait_ge(gu_done, b + 1)
                gate_up(b + EXS, s % EXS)

            def refill_down(b, s):
                sp.wait_ge(d_done, b + 1)
                down(b + EXS, s)
                store_y(b, s)

            refill_gate_up(0, 0)
            with sp.Fori(0, (NE - EXS) // EXS) as i:
                for s in range(EXS):
                    refill_gate_up(i * EXS + (s + 1), s + 1)
                    refill_down(i * EXS + s, s)
            for b in range((NE - EXS) // EXS * EXS, NE - EXS):
                if b + 1 < NE - EXS:
                    refill_gate_up(b + 1, b % EXS + 1)
                refill_down(b, b % EXS)
            for b in range(NE - EXS, NE):
                if b == NE - 2:
                    sp.dma_start(ln2g, ln2_g[0].partition_broadcast(P)).then_inc(ln2_landed, 16)
                    sp.dma_start(ln2b, ln2_b[0].partition_broadcast(P)).then_inc(ln2_landed, 16)
                store_y(b, b % EXS)
            sp.wait_ge(over_ready, 1)
            n_over = sp.value_load(over_i[0:1, MAX_OVER:MAX_OVER + 1], min_val=0, max_val=MAX_OVER - 1)
            with sp.If(n_over > 0):
                with sp.Fori(0, MAX_OVER // EXS) as i:
                    for s in range(EXS):
                        b = i * EXS + (NE + s)
                        eid = sp.value_load(over_i[0:1, bass.ds(i * EXS + s, 1)], min_val=0, max_val=NE - 1)
                        sp.wait_ge(d_done, b - (EXS - 1))
                        expert(eid, (NE + s) % EXS)
                        store_y(b, s)
            for t in range(TT):
                if t < TT - 1:
                    sp.wait_ge(out_ready, t + 1)
                else:
                    sp.wait_ge(last_ready, 1)
                sp.dma_start(out[0, t * P:(t + 1) * P, :], h1[:, t, :]).then_inc(out_stored, 16)
            sp.wait_ge(out_stored, 16 * TT)

        @block.gpsimd
        def _(pool):
            nc.gpsimd.memset(ident[:, :], 0.0).then_inc(pool_step, 1)
            nc.gpsimd.memset(ones[:, :], 1.0).then_inc(pool_step, 1)
            pool.wait_ge(pool_step, 2)
            nc.gpsimd.affine_select(out=ident[:, :], in_=ident[:, :], compare_op=ALU.not_equal, fill=1.0, base=0,
                                    pattern=[[-1, P]], channel_multiplier=1).then_inc(const_ready, 1)

            def split(c):
                pool.wait_ge(w_high, c + 1)
                nc.gpsimd.tensor_tensor(w_lo[c % RING], w_raw[c % RING], w_hi[c % RING].bitcast(F32), ALU.subtract
                                        ).then_inc(w_split, 1)

            split(0)
            nc.gpsimd.affine_select(out=upper[:, :], in_=ones[:, :], compare_op=ALU.is_gt, fill=0.0, base=0,
                                    pattern=[[1, P]], channel_multiplier=-1).then_inc(const_ready, 1)
            nc.gpsimd.iota(negd, [[1, 512]], base=-384, channel_multiplier=-1,
                           allow_small_or_imprecise_dtypes=True).then_inc(const_ready, 1)
            nc.gpsimd.iota(desc[:, :], [[-1, NE]], base=NE, channel_multiplier=0,
                           allow_small_or_imprecise_dtypes=True).then_inc(const_ready, 1)
            nc.gpsimd.iota(base0[:, :], [[CAP, NE]], base=0, channel_multiplier=0,
                           allow_small_or_imprecise_dtypes=True).then_inc(const_ready, 1)
            nc.gpsimd.iota(jrow[:, :], [[1, MAX_OVER]], base=0, channel_multiplier=0,
                           allow_small_or_imprecise_dtypes=True).then_inc(const_ready, 1)
            nc.gpsimd.iota(tokid[:, :], [[P, TT]], base=0, channel_multiplier=1,
                           allow_small_or_imprecise_dtypes=True).then_inc(const_ready, 1)
            nc.gpsimd.memset(half_neg[:, :], -0.5).then_inc(const_ready, 1)
            nc.gpsimd.iota(base1[:, :], [[CAP, NE]], base=-CAP * (NE - 1), channel_multiplier=0,
                           allow_small_or_imprecise_dtypes=True).then_inc(const_ready, 1)
            nc.gpsimd.iota(fulls[:, :], [[CAP, MORE]], base=CAP, channel_multiplier=0,
                           allow_small_or_imprecise_dtypes=True).then_inc(const_ready, 1)
            nc.gpsimd.iota(col_s[:, :], [[1, CAP]], base=0, channel_multiplier=0,
                           allow_small_or_imprecise_dtypes=True).then_inc(const_ready, 1)
            nc.gpsimd.iota(col_b[:, :], [[CAP, NTAB]], base=0, channel_multiplier=0,
                           allow_small_or_imprecise_dtypes=True).then_inc(const_ready, 1)
            pool.wait_ge(const_ready, 2)
            nc.gpsimd.tensor_copy(upper_h[:, :], upper[:, :]).then_inc(const_ready, 1)
            nc.gpsimd.tensor_copy(ones_h[:, :], ones[:, :]).then_inc(const_ready, 1)
            split(1)
            pool.wait_ge(const_ready, CONSTS)
            pool.wait_ge(var_c_ready, 1)
            nc.gpsimd.tensor_tensor(rstd_c[:, :], var_c[:, :], half_neg[:, :], ALU.pow).then_inc(rstd_c_ready, 1)
            pool.wait_ge(small_landed, 16 * 8)
            for q in range(4):
                nc.gpsimd.tensor_copy(sinks[:, q, :].rearrange("p (r i) -> p r i", r=2),
                                      sinks_row[:, 4 * q:4 * q + 4].rearrange("p (i r) -> p r i", r=2)
                                      ).then_inc(sinks_ready, 1)
            zeros = view(r_zero, D // 2)
            nc.gpsimd.memset(zeros, 0.0).then_inc(zero_ready, 1)
            pool.wait_ge(zero_ready, 1)
            for c in range(2, len(CHUNKS)):
                split(c)
                for k in WO_AFTER.get(c, ()):
                    pool.wait_ge(wo_high, k + 1)
                    nc.gpsimd.tensor_tensor(w_o_lo[:, k, :], w_o[:, k, :], w_o_hi[:, k, :].bitcast(F32),
                                            ALU.subtract).then_inc(wo_split, 1)
                if c in ZERO_AFTER:
                    row0 = NE * CAP + (c - ZERO_AFTER[0]) * P
                    pool.dma_start(y_dram[row0:row0 + P, :].rearrange("p (h c) -> p h c", h=2),
                                   zeros.unsqueeze(1).to_broadcast([P, 2, D // 2])).then_inc(rows_zeroed, 16)
            for t in range(TT):
                pool.wait_ge(var_ready, t + 1)
                nc.gpsimd.tensor_tensor(ln[:, 0, 4, t:t + 1], ln[:, 0, 3, t:t + 1], half_neg[:, 0:1], ALU.pow
                                        ).then_inc(rstd_ready, 1)
            pool.wait_ge(tok_ready, 1)
            pool.wait_ge(h1_stored, 16 * TT)

            def gather(b, s, n):
                nc.gpsimd.tensor_copy(idx[s][:, :], tok_i[:, bass.ds(b, 1)]).then_inc(idx_ready, 1)
                pool.wait_ge(idx_ready, n + 1)
                pool.sem_inc(pool_passed, 1)
                pool.indirect_dma_start(out=xg[s][0:CAP, :], out_offset=None, in_=h1_dram,
                                        in_offset=bass.IndirectOffsetOnAxis(ap=idx[s][:, 0:1], axis=0)
                                        ).then_inc(xg_landed[s], 16)

            for b in range(XGS):
                gather(b, b, b)

            def next_gathers(first, end):
                with pool.Fori(first, end) as i:
                    for s in range(EXS):
                        b = i * EXS + (XGS + s)
                        pool.wait_ge(xgt_done, b - (XGS - 1))
                        gather(b, s % XGS, b)

            next_gathers(0, NE // EXS)
            pool.wait_ge(over_ready, 1)
            n_over = pool.value_load(over_i[0:1, MAX_OVER:MAX_OVER + 1], min_val=0, max_val=MAX_OVER - 1)
            for p in range(2):
                pool.wait_ge(y_stored[p], 32 * NE // 2 + 1)
            with pool.If(n_over > 0):
                next_gathers(NE // EXS, NBLK // EXS)
                for p in range(2):
                    pool.wait_ge(y_stored[p], 32 * NBLK // 2 + 1)
            pool.wait_ge(slots_ready, 1)
            for t in range(TT):
                for k in range(2):
                    pool.indirect_dma_start(out=yk[t][k], out_offset=None, in_=y_dram,
                                            in_offset=bass.IndirectOffsetOnAxis(ap=slot_i[:, k, t:t + 1], axis=0)
                                            ).then_inc(yk_landed[t][k], 16)
            for t in range(TT + 1):
                if t < TT:
                    pool.wait_ge(ssq2_ready, t + 1)
                    nc.gpsimd.tensor_scalar(ln[:, 1, 3, t:t + 1], ln[:, 1, 2, t:t + 1], 1.0 / D, LN_EPS,
                                            ALU.mult, ALU.add).then_inc(var2_ready, 1)
                    pool.wait_ge(var2_ready, t + 1)
                    nc.gpsimd.tensor_tensor(ln[:, 1, 4, t:t + 1], ln[:, 1, 3, t:t + 1], half_neg[:, 0:1], ALU.pow
                                            ).then_inc(rstd2_ready, 1)
                    pool.wait_ge(rstd2_ready, t + 1)
                    nc.gpsimd.tensor_tensor(ln[:, 1, 0, t:t + 1], ln[:, 1, 1, t:t + 1], ln[:, 1, 4, t:t + 1],
                                            ALU.mult).then_inc(offset2_ready, 1)
                if t >= 2:
                    pool.wait_ge(scaled2_ready, t - 1)
                    nc.gpsimd.tensor_tensor(h1[:, t - 2, :], h1[:, t - 2, :], ln2b, ALU.add
                                            ).then_inc(out_ready, 1)

        @block.tensor
        def _(pe):
            pe.wait_ge(const_ready, 1)
            for t in range(TT):
                pe.wait_ge(x_landed[t], 16)
                for h in range(2):
                    n = 2 * t + h
                    if n >= 6:
                        pe.wait_ge(xt_split, n - 5)
                    for k in range(4):
                        ins = nc.tensor.transpose(psum[:, n % 6, k * P:(k + 1) * P],
                                                  x_nat[:, t, (4 * h + k) * P:(4 * h + k + 1) * P], ident[:, :])
                    ins.then_inc(xt_done, 1)
            pe.wait_ge(xt_split, 2 * TT)

            def unit(u, k0=0, k1=DT):
                kind, i, c, col = UNITS[u]
                ps = psum[:, bank_of(u), :]
                if k0 == 0:
                    unit_wait(pe, u)
                if kind == "out":
                    pe.wait_ge(wo_landed, 32)
                    t = i // 2
                    tok, cols = slice(t * P, (t + 1) * P), slice(col, col + 512)
                    for k in range(SPLIT, DT):
                        nc.tensor.matmul(ps, gaT[:, k, tok], w_o[:, k, cols], start=k == SPLIT, stop=False)
                    for k in range(SPLIT):
                        if i == 0:
                            pe.wait_ge(wo_split, k + 1)
                            pe.wait_ge(m_split, k + 1)
                        for p, (mp, wp) in enumerate(((m_hi, w_o_hi), (m_hi, w_o_lo), (m_lo, w_o_hi))):
                            ins = nc.tensor.matmul(ps, mp[:, k, tok], wp[:, k, cols], start=False,
                                                   stop=k == SPLIT - 1 and p == 2)
                    ins.then_inc(unit_done, 1)
                    return
                hi, lo = w_hi[c % RING], w_lo[c % RING]
                if k0 == 0:
                    pe.wait_ge(w_split, c + 1)
                xh, xl = (branch_hi[kind], branch_lo[kind]) if kind in ("a", "b") else (x_hi, x_lo)
                for k in range(k0, k1):
                    if kind in ("a", "b") and i == 0:
                        pe.wait_ge(o_split, DT * (kind == "b") + k + 1)
                    for p, (wp, xp) in enumerate(((hi, xh), (hi, xl), (lo, xh))):
                        ins = nc.tensor.matmul(ps, wp[:, k, col:col + P], xp[:, k, :],
                                               start=k == 0 and p == 0, stop=k == DT - 1 and p == 2)
                if k1 == DT:
                    ins.then_inc(unit_done, 1)

            unit(UNIT["ckv", 0])
            unit(UNIT["qi", 0])
            pe.wait_ge(csq_ready, 1)
            for t in range(TT):
                ins = nc.tensor.matmul(psum[:, 5, 2 * t:2 * t + 2], c_sq[:, t * P:(t + 1) * P], ones[:, 0:2],
                                       start=True, stop=True)
            ins.then_inc(css_done, 1)
            for u in range(UNIT["qi", 1], UNIT["qi", 2] + 1):
                unit(u)
            pe.wait_ge(diag_ready, TT)
            nc.tensor.matmul(psum[:, 4, :], ones[:, :], rstd_diag, start=True, stop=True).then_inc(rstd_spread, 1)
            for u in range(UNIT["qi", 3], UNIT["ki", 0] + 1):
                unit(u)
            pe.wait_ge(c_ready, 1)
            pe.wait_ge(small_landed, 16 * 8)
            nc.tensor.matmul(psum[0:HD, 5, :], wuk[:, :], cT, start=True, stop=True).then_inc(c_done, 1)
            for t in range(TT):
                ins = nc.tensor.matmul(psum[:, 4, t * HD:(t + 1) * HD], cT[:, t * P:(t + 1) * P], wuv[:, :],
                                       start=True, stop=True)
            ins.then_inc(c_done, 1)
            pe.wait_ge(unit_copied, UNIT["ki", 0] + 1)
            for t in range(TT):
                ins = nc.tensor.transpose(psum[:, 7, t * HD:(t + 1) * HD], wiT[HD:P, t * P:(t + 1) * P],
                                          ident[HD:P, HD:P])
            ins.then_inc(wi_turned, 1)
            n = 0
            for t in range(1, TT):
                for h in range(IH):
                    if n >= 4:
                        pe.wait_ge(rel_ready, n - 3)
                    r = slice(HD * (h % 2), HD * (h % 2) + HD)
                    nc.tensor.matmul(psum[:, n % 4, 0:P * (t + 1)], qiT[r, h // 2, t * P:(t + 1) * P],
                                     kiT[r, 0:P * (t + 1)], start=True, stop=True).then_inc(idx_scored, 1)
                    n += 1
            pe.wait_ge(wi_copied, 1)
            for u in range(UNIT["ka", 0], UNIT["qa", 7] + 1):
                unit(u)
                if u == UNIT["qa", 0]:
                    pe.wait_ge(unit_copied, UNIT["va", 0] + 1)
                    pe.wait_ge(c_copied, 2)
                    for t in range(TT):
                        ins = nc.tensor.transpose(psum[:, 4, t * P:(t + 1) * P], ckvT[:, t * P:(t + 1) * P],
                                                  ident[:, :])
                    ins.then_inc(va_turned, 1)

            def scores(n):
                kind, g, t, w0, w = item_shape(n)
                if n >= 2:
                    pe.wait_ge(s_taken, n - 1)
                if n <= 1:
                    pe.wait_ge(rel_ready, 3 * IH)
                    pe.wait_ge(c_copied, 2)
                if kind == "A":
                    pe.wait_ge(unit_copied, UNIT["qa", 2 * g + 1] + 1)
                else:
                    pe.wait_ge(unit_copied, UNIT["qb", g] + 1)
                for i in range(2 if kind == "A" else 1):
                    for par in range(2):
                        r = slice(HD * par, HD * par + HD)
                        if kind == "A":
                            q, k = qaT[r, 2 * g + i, t * P:(t + 1) * P], kaT[r, g // 2, P * t - CHUNK + w0:P * (t + 1)]
                        else:
                            q, k = qbT[r, g, t * P:(t + 1) * P], kbT[r, 0:w]
                        ins = nc.tensor.matmul(psum[:, 2 * (n % 2) + par, 256 * i:256 * i + w], q, k,
                                               start=True, stop=True)
                ins.then_inc(s_done, 1)

            def turn(n):
                kind, g, t, w0, w = item_shape(n)
                pe.wait_ge(p_ready, n + 1)
                if n >= 1:
                    pe.wait_ge(pt_copied, n)
                else:
                    pe.wait_ge(va_copied, 1)
                if kind == "A":
                    s = s_sb[n % 2][:, 0:4 * w].rearrange("p (h w) -> p h w", h=4)
                    for h in range(4):
                        ins = nc.tensor.transpose(psum[:, 4, h * P:(h + 1) * P], s[:, h, w - P:w], ident[:, :])
                    if t:
                        for h in range(4):
                            ins = nc.tensor.transpose(psum[0:CHUNK, 5, h * P:(h + 1) * P], s[:, h, 0:CHUNK],
                                                      ident[:, :])
                else:
                    s = s_sb[n % 2][:, 0:2 * w].rearrange("p (h w) -> p h w", h=2)
                    for kt in range(t + 1):
                        for par in range(2):
                            c = (kt % 2) * 256 + par * P
                            ins = nc.tensor.transpose(psum[:, 4 + kt // 2, c:c + P], s[:, par, kt * P:(kt + 1) * P],
                                                      ident[:, :])
                ins.then_inc(pt_done, 1)

            def values(n):
                kind, g, t, w0, w = item_shape(n)
                pe.wait_ge(pt_copied, n + 1)
                if n >= 1:
                    pe.wait_ge(o_copied, n)
                pt = pt_sb[n % 2]
                if kind == "A":
                    kv = slice(HD * (g // 2), HD * (g // 2) + HD)
                    for par in range(2):
                        ins = nc.tensor.matmul(psum[HD * par:HD * par + HD, 7, 0:256], va[:, t, kv],
                                               pt[:, 256 * par:256 * par + 256], start=True, stop=t == 0)
                    if t:
                        for par in range(2):
                            ins = nc.tensor.matmul(psum[HD * par:HD * par + HD, 7, 0:256], va_hi[0:CHUNK, t - 1, kv],
                                                   pt[0:CHUNK, 512 + 256 * par:512 + 256 * par + 256],
                                                   start=False, stop=True)
                else:
                    for kt in range(t + 1):
                        for par in range(2):
                            c = 256 * kt + P * par
                            ins = nc.tensor.matmul(psum[HD * par:HD * par + HD, 7, 0:P], vb[:, kt, :],
                                                   pt[:, c:c + P], start=kt == 0, stop=kt == t)
                ins.then_inc(pv_done, 1)

            pe.wait_ge(unit_copied, UNIT["qa", 7] + 1)
            scores(0)
            scores(1)
            for n in range(len(ITEMS)):
                if n + 2 < len(ITEMS):
                    scores(n + 2)
                u, k = UNIT["qb", 0] + n // 2, 4 * (n % 2)
                unit(u, k, k + 2)
                turn(n)
                unit(u, k + 2, k + 4)
                if n >= 1:
                    values(n - 1)
            values(len(ITEMS) - 1)

            pe.wait_ge(o_copied, len(ITEMS))
            for u in range(UNIT["a", 0], UNIT["out", 0]):
                unit(u)
            pe.wait_ge(m_ready, 8)

            def turn_h1(t):
                pe.wait_ge(h1_ready, t + 1)
                for h in range(2):
                    n = 2 * t + h
                    if n >= 2:
                        pe.wait_ge(h1t_copied, n - 1)
                    for k in range(4):
                        ins = nc.tensor.transpose(psum[:, n % 2, k * P:(k + 1) * P],
                                                  h1[:, t, (4 * h + k) * P:(4 * h + k + 1) * P], ident[:, :])
                    ins.then_inc(h1t_done, 1)

            def router(t):
                pe.wait_ge(h1t_copied, 2 * t + 2)
                n = NG + NE
                ps = psum[:, 3, 0:n] if t == TT - 1 else psum[:, 2, t * n:(t + 1) * n]
                for k in range(DT):
                    ins = nc.tensor.matmul(ps, h1T[:, k, t * P:(t + 1) * P], rw[:, k, :], start=k == 0,
                                           stop=k == DT - 1)
                if t >= TT - 2:
                    ins.then_inc(routed, 1)

            def rank(t):
                for v in range(min(t + 1, TT)):
                    ins = nc.tensor.matmul(psum[:, 5, t * NE:(t + 1) * NE], (upper_h if v == t else ones_h)[:, :],
                                           oh_both[:, v, :], start=v == 0, stop=v == min(t, TT - 1))
                return ins

            for t in range(TT):
                unit(UNIT["out", 2 * t])
                unit(UNIT["out", 2 * t + 1])
                if t:
                    turn_h1(t - 1)
                if t >= 2:
                    router(t - 2)
            router(TT - 2)
            turn_h1(TT - 1)
            router(TT - 1)
            pe.wait_ge(oh_ready, 1)
            pe.wait_ge(const_ready, CONSTS)
            for v in range(TT - 1):
                rank(v)
            pe.wait_ge(oh_ready, 2)
            rank(TT - 1)
            rank(TT).then_inc(ranked, 1)
            pe.wait_ge(pairs_ready, 1)
            for j in range(N_TOP * TT):
                ins = nc.tensor.matmul(psum[0:CAP, 4, 0:NTAB], in_slot[:, j, :], in_block[:, j, :], start=j == 0,
                                       stop=j == N_TOP * TT - 1)
            ins.then_inc(table_done, 1)

            def turn_x(b, i, s):
                pe.wait_ge(xg_landed[s % XGS], i * (EXS // XGS * 16) + (s // XGS + 1) * 16)
                pe.sem_inc(pe_passed, 1)
                rows = xg[s % XGS][0:CAP, :].rearrange("s (p k) -> s k p", k=DT)
                for k in range(DT):
                    ins = nc.tensor.transpose(psum[:, 0, k * CAP:(k + 1) * CAP], rows[:, k, :],
                                              ident[0:CAP, 0:CAP])
                ins.then_inc(xgt_done, 1)

            def start(b, i, s):
                slot, use = s % EXS, i + s // EXS
                pe.wait_ge(gu_landed[slot], use * 32 + 32)
                pe.wait_ge(xgt_copied, b + 1)
                for k in range(DT):
                    for g in range(2):
                        ins = nc.tensor.matmul(psum[CAP * g:CAP * g + CAP, 2 + s % 2, 0:FF], xgT[s % 2][:, k, :],
                                               ex_gu[slot][:, g, k, :], start=k == 0, stop=k == DT - 1)
                ins.then_inc(gu_done, 1)
                turn_x(b + 1, i, s + 1)

            def finish(b, i, s):
                slot, use = s % EXS, i + s // EXS
                pe.wait_ge(h_ready, b + 1)
                pe.sem_inc(pe_passed, 1)
                rows = hid[s % 2][0:CAP, :].rearrange("s (p k) -> s k p", k=2)
                for k in range(2):
                    ins = nc.tensor.transpose(psum[:, 1, k * CAP:(k + 1) * CAP], rows[:, k, :],
                                              ident[0:CAP, 0:CAP])
                ins.then_inc(ht_done, 1)
                pe.wait_ge(ht_copied, b + 1)
                pe.wait_ge(d_landed[slot], use * 16 + 16)
                pe.wait_ge(y_copied, b + 1)
                for k in range(2):
                    for half in range(2):
                        ins = nc.tensor.matmul(psum[CAP * half:CAP * half + CAP, 4 + s % 2, :], hidT[s % 2][:, k, :],
                                               ex_d[slot][:, k, 512 * half:512 * half + 512], start=k == 0,
                                               stop=k == 1)
                ins.then_inc(d_done, 1)

            pe.wait_ge(tok_ready, 1)
            turn_x(0, 0, 0)
            blocks(pe, finish, start)

        @block.scalar
        def _(act):
            step = Steps(act, act_step)

            def high(c):
                act.wait_ge(w_landed[c % RING], 16 * (c // RING + 1))
                nc.scalar.activation(w_hi[c % RING], w_raw[c % RING], ACT.Copy).then_inc(w_high, 1)

            high(0)
            for n in range(2 * TT):
                act.wait_ge(xt_done, n + 1)
                t, h = n // 2, n % 2
                nc.scalar.activation(x_hi[:, 4 * h:4 * h + 4, t * P:(t + 1) * P],
                                     psum[:, n % 6, :].rearrange("p (k c) -> p k c", k=4), ACT.Copy
                                     ).then_inc(xt_high, 1)
            high(1)

            def copy_unit(u):
                kind, i, c, _ = UNITS[u]
                if u == LAST_OF_CHUNK[c]:
                    high(c + 2)
                act.wait_ge(unit_done, u + 1)
                ps = psum[:, bank_of(u), :]
                if kind in ("ckv", "va"):
                    if kind == "va":
                        act.wait_ge(c_ready, 1)
                    ins = nc.scalar.activation(ckvT, ps, ACT.Copy)
                elif kind == "qi":
                    ins = nc.scalar.activation(qiT[:, i, :], ps, ACT.Copy)
                elif kind == "ki":
                    nc.scalar.activation(kiT[0:HD, :], ps[0:HD, :], ACT.Copy)
                    nc.scalar.activation(kiT[HD:P, :], ps[0:HD, :], ACT.Copy)
                    ins = nc.scalar.activation(wiT[HD:P, :], ps[HD:P, :], ACT.Copy, scale=IDX_SCALE)
                elif kind == "ka":
                    for g in range(AG):
                        for half in range(2):
                            ins = nc.scalar.activation(kaT[HD * half:HD * half + HD, g, :],
                                                       ps[HD * g:HD * g + HD, :], ACT.Copy)
                elif kind in ("qa", "qb"):
                    ins = nc.scalar.activation((qaT if kind == "qa" else qbT)[:, i, :], ps, ACT.Copy,
                                               scale=HD ** -0.5)
                else:
                    ins = nc.scalar.activation((gaT if i < 8 else gbT)[:, i % 8, :], ps, ACT.Tanh, scale=0.5)
                ins.then_inc(unit_copied, 1)

            act.wait_ge(unit_done, 1)
            nc.scalar.activation(c_sq, psum[:, bank_of(0), :], ACT.Square).then_inc(csq_ready, 1)
            copy_unit(0)
            act.wait_ge(const_ready, 3)
            step(nc.scalar.activation(negd, negd, ACT.Abs))
            nc.scalar.activation(negd, negd, ACT.Copy, scale=-1.0).then_inc(abs_ready, 1)
            for u in range(1, UNIT["ki", 0] + 1):
                copy_unit(u)
            act.wait_ge(c_done, 1)
            nc.scalar.activation(kbT[0:HD, :], psum[0:HD, 5, :], ACT.Copy)
            nc.scalar.activation(kbT[HD:P, :], psum[0:HD, 5, :], ACT.Copy).then_inc(c_copied, 1)
            act.wait_ge(c_done, 2)
            nc.scalar.activation(vb, psum[:, 4, 0:TT * HD].rearrange("p (t c) -> p t c", t=TT), ACT.Copy
                                 ).then_inc(c_copied, 1)
            act.wait_ge(wi_turned, 1)
            nc.scalar.activation(wis[:, :, :], psum[:, 7, 0:TT * HD].rearrange("p (t c) -> p t c", t=TT)[:, :, 0:IH],
                                 ACT.Copy).then_inc(wi_copied, 1)
            n = 0
            for t in range(1, TT):
                for h in range(IH):
                    act.wait_ge(idx_scored, n + 1)
                    if n >= 2:
                        act.wait_ge(rel_added, n - 1)
                    nc.scalar.activation(rel[n % 2][:, 0:P * (t + 1)], psum[:, n % 4, 0:P * (t + 1)], ACT.Relu
                                         ).then_inc(rel_ready, 1)
                    n += 1
            for u in range(UNIT["ka", 0], UNIT["qa", 7] + 1):
                copy_unit(u)
                if u == UNIT["qa", 0]:
                    act.wait_ge(va_turned, 1)
                    v = psum[:, 4, :].rearrange("p (t c) -> p t c", t=TT)
                    nc.scalar.activation(va, v, ACT.Copy)
                    nc.scalar.activation(va_hi[0:CHUNK], v[CHUNK:P], ACT.Copy).then_inc(va_copied, 1)

            def exps(n):
                kind, g, t, w0, w = item_shape(n)
                heads = 4 if kind == "A" else 2
                s = s_sb[n % 2][:, 0:heads * w].rearrange("p (h w) -> p h w", h=heads)
                act.wait_ge(negm_ready, n + 1)
                for h in range(heads):
                    ins = nc.scalar.activation(s[:, h, :], s[:, h, :], ACT.Exp, bias=negm[:, n % 4, h:h + 1],
                                               accum_out=den[:, n % 4, h:h + 1])
                if kind == "A":
                    ins = nc.scalar.activation(sink_e[:, n % 4, :], sink_e[:, n % 4, :], ACT.Exp)
                ins.then_inc(exp_done, 1)

            def copy_pt(n):
                kind, g, t, w0, w = item_shape(n)
                act.wait_ge(pt_done, n + 1)
                if n >= 2:
                    act.wait_ge(pv_done, n - 1)
                pt = pt_sb[n % 2]
                if kind == "A":
                    ins = nc.scalar.activation(pt[:, 0:512], psum[:, 4, :], ACT.Copy)
                    if t:
                        ins = nc.scalar.activation(pt[0:CHUNK, 512:1024], psum[0:CHUNK, 5, :], ACT.Copy)
                else:
                    ins = nc.scalar.activation(pt[:, 0:256 * (t + 1)],
                                               psum[:, 4:6, :].rearrange("p b c -> p (b c)")[:, 0:256 * (t + 1)],
                                               ACT.Copy)
                ins.then_inc(pt_copied, 1)

            def copy_o(n):
                kind, g, t, w0, w = item_shape(n)
                act.wait_ge(pv_done, n + 1)
                if kind == "A":
                    ins = nc.scalar.activation(qaT[:, 2 * g:2 * g + 2, t * P:(t + 1) * P],
                                               psum[:, 7, 0:256].rearrange("p (i c) -> p i c", i=2), ACT.Copy)
                else:
                    ins = nc.scalar.activation(qbT[:, g, t * P:(t + 1) * P], psum[:, 7, 0:P], ACT.Copy)
                ins.then_inc(o_copied, 1)

            exps(0)
            for n in range(len(ITEMS)):
                if n + 1 < len(ITEMS):
                    exps(n + 1)
                copy_pt(n)
                if n % 2:
                    copy_unit(UNIT["qb", 0] + n // 2)
                if n >= 1:
                    copy_o(n - 1)
            copy_o(len(ITEMS) - 1)

            for n, (heads, part) in enumerate([(qaT, branch_hi["a"]), (qbT, branch_hi["b"])]):
                for k in range(DT):
                    if n == 0 and k == 0:
                        act.wait_ge(o_copied, len(ITEMS))
                    nc.scalar.activation(part[:, k, :], heads[:, k, :], ACT.Copy).then_inc(o_high, 1)
            for c in range(22, len(CHUNKS)):
                high(c)
                for k in WO_AFTER.get(c, ()):
                    act.wait_ge(wo_landed, 32)
                    nc.scalar.activation(w_o_hi[:, k, :], w_o[:, k, :], ACT.Copy).then_inc(wo_high, 1)
            act.wait_ge(unit_done, UNIT["b", 7] + 1)
            for k in range(SPLIT):
                act.wait_ge(m_ready, k + 1)
                nc.scalar.activation(m_hi[:, k, :], gaT[:, k, :], ACT.Copy).then_inc(m_high, 1)
            for t in range(TT):
                act.wait_ge(x2_landed[t], 16)
                nc.scalar.activation(h1[:, t, :], h1[:, t, :], ACT.Copy, scale=ALPHA).then_inc(ax_ready, 1)

            def squares(i, t, ready, done):
                act.wait_ge(ready, t + 1)
                nc.scalar.activation(squared[i][t], h1[:, t, :], ACT.Square, bias=ln[:, i, 1, t:t + 1],
                                     accum_out=ln[:, i, 2, t:t + 1]).then_inc(done, 1)

            def copy_h1t(t):
                for h in range(2):
                    n = 2 * t + h
                    act.wait_ge(h1t_done, n + 1)
                    nc.scalar.activation(h1T[:, 4 * h:4 * h + 4, t * P:(t + 1) * P],
                                         psum[:, n % 2, :].rearrange("p (k c) -> p k c", k=4), ACT.Copy
                                         ).then_inc(h1t_copied, 1)

            for t in range(TT):
                squares(0, t, mean_ready, ssq_ready)
                if t:
                    copy_h1t(t - 1)
            copy_h1t(TT - 1)
            for n in range(2):
                ts = slice(0, TT - 1) if n == 0 else slice(TT - 1, TT)
                act.wait_ge(gd_ready, n + 1)
                nc.scalar.activation(g4[:, 1, ts], g4[:, 0, ts], ACT.Exp).then_inc(ge_ready, 1)
                act.wait_ge(md_ready, n + 1)
                nc.scalar.activation(g1[:, 6, ts], g1[:, 5, ts], ACT.Exp).then_inc(me_ready, 1)
            act.wait_ge(h1_stored, 16 * TT)
            for t in range(TT):
                nc.scalar.activation(h1[:, t, :], h1[:, t, :], ACT.Copy, scale=ALPHA).then_inc(ah_ready, 1)

            def copy_xgt(n, s):
                act.wait_ge(xgt_done, n + 1)
                nc.scalar.activation(xgT[s % 2], psum[:, 0, :].rearrange("p (k c) -> p k c", k=DT), ACT.Copy
                                     ).then_inc(xgt_copied, 1)

            def start(b, i, s):
                act.wait_ge(gu_done, b + 1)
                nc.scalar.activation(th[s % 2][0:CAP, :], psum[0:CAP, 2 + s % 2, 0:FF], ACT.Tanh, scale=0.5
                                     ).then_inc(th_done, 1)
                copy_xgt(b + 1, s + 1)

            def finish(b, i, s):
                act.wait_ge(d_done, b + 1)
                act.wait_ge(y_stored[s % 2], i * (EXS // 2 * 32) + (32 * (s // 2) + 1))
                nc.scalar.activation(y_sb[s % 2], psum[:, 4 + s % 2, :], ACT.Copy).then_inc(y_copied, 1)

            act.sem_inc(y_copied, 1)
            for p in range(2):
                act.sem_inc(y_stored[p], 1)
            copy_xgt(0, 0)
            blocks(act, finish, start)
            for t in range(TT + 1):
                if t < TT:
                    squares(1, t, mean2_ready, ssq2_ready)
                if t:
                    act.wait_ge(offset2_ready, t)
                    nc.scalar.activation(h1[:, t - 1, :], h1[:, t - 1, :], ACT.Identity,
                                         scale=ln[:, 1, 4, t - 1:t], bias=ln[:, 1, 0, t - 1:t]
                                         ).then_inc(normed2_ready, 1)

        @block.vector
        def _(dve):
            step = Steps(dve, dve_step)
            V = nc.vector
            for n in range(2 * TT):
                dve.wait_ge(xt_high, n + 1)
                t, h = n // 2, n % 2
                part = slice(4 * h, 4 * h + 4), slice(t * P, (t + 1) * P)
                V.tensor_tensor(x_lo[:, part[0], part[1]], psum[:, n % 6, :].rearrange("p (k c) -> p k c", k=4),
                                x_hi[:, part[0], part[1]].bitcast(F32), ALU.subtract).then_inc(xt_split, 1)
            dve.wait_ge(abs_ready, 1)
            step(V.tensor_copy(strip[:, :], negd[:, 320:512]))
            step(V.memset(strip[0:CHUNK, 128:192], MASKED))
            step(V.memset(strip[CHUNK:P, 0:CHUNK], MASKED))
            step(V.tensor_copy(dm[0], negd[:, 384:512]))
            step(V.memset(dm[0][0:CHUNK, CHUNK:P], MASKED))
            dve.wait_ge(css_done, 1)
            V.tensor_scalar(var_c[:, :], psum[:, 5, 0:2 * TT].rearrange("p (t o) -> p t o", o=2)[:, :, 0],
                            1.0 / RANK, RMS_EPS, ALU.mult, ALU.add).then_inc(var_c_ready, 1)
            dve.wait_ge(rstd_c_ready, 1)
            for t in range(TT):
                V.tensor_scalar(rstd_diag[:, t * P:(t + 1) * P], ident[:, :], rstd_c[:, t:t + 1], None, ALU.mult
                                ).then_inc(diag_ready, 1)
            dve.wait_ge(rstd_spread, 1)
            dve.wait_ge(small_landed, 16 * 8)
            dve.wait_ge(unit_copied, UNIT["ckv", 0] + 1)
            V.scalar_tensor_tensor(cT, ckvT, kvg[:, 0:1], psum[:, 4, :], ALU.mult, ALU.mult).then_inc(c_ready, 1)
            dve.wait_ge(wi_copied, 1)
            n = 0
            for t in range(1, TT):
                w = P * (t + 1)
                for h in range(IH):
                    dve.wait_ge(rel_ready, n + 1)
                    if h:
                        dve.wait_ge(rel_added, n)
                        ins = V.scalar_tensor_tensor(work[t], rel[n % 2][:, 0:w], wis[:, t, h:h + 1], work[t],
                                                     ALU.mult, ALU.add)
                    else:
                        ins = V.tensor_scalar(work[t], rel[n % 2][:, 0:w], wis[:, t, 0:1], None, ALU.mult)
                    ins.then_inc(rel_added, 1)
                    n += 1
            dve.wait_ge(rel_added, n)

            def take_best(t):
                step(V.max(m8[:, t - 1, :], work[t]))
                step(V.match_replace(work[t], m8[:, t - 1, :], work[t], TAKEN))

            def mask(t):
                step(V.tensor_scalar(work[t], work[t], 2 * OUT_OF_REACH, MASKED, ALU.is_gt, ALU.mult))
                step(V.tensor_tensor(dm[t], work[t], negd[:, 512 - P * (t + 1):512], ALU.add))

            for t in range(1, TT):
                w = P * (t + 1)
                step(V.memset(work[t][0:CHUNK, w - CHUNK:w], OUT_OF_REACH))
                if t < TT - 1:
                    for _ in range(TOPK // 8):
                        take_best(t)
                    mask(t)

            def soften(n):
                kind, g, t, w0, w = item_shape(n)
                heads = 4 if kind == "A" else 2
                s = s_sb[n % 2][:, 0:heads * w].rearrange("p (h w) -> p h w", h=heads)
                dve.wait_ge(s_done, n + 1)
                if n >= 2:
                    dve.wait_ge(pt_done, n - 1)
                if kind == "A":
                    for h in range(4):
                        par, i = h // 2, h % 2
                        ins = V.scalar_tensor_tensor(s[:, h, :], strip[:, w0:192], SLOPE[4 * g + 2 * i + par],
                                                     psum[:, 2 * (n % 2) + par, 256 * i:256 * i + w],
                                                     ALU.mult, ALU.add)
                    ins.then_inc(s_taken, 1)
                else:
                    for par in range(2):
                        ins = V.scalar_tensor_tensor(s[:, par, :], dm[t], SLOPE[2 * g + par],
                                                     psum[:, 2 * (n % 2) + par, 0:w], ALU.mult, ALU.add)
                    ins.then_inc(s_taken, 1)
                dve.wait_ge(s_taken, n + 1)
                step(V.tensor_reduce(mx[:, n % 4, 0:heads], s, AX.X, ALU.max))
                if kind == "A":
                    step(V.tensor_tensor(mx[:, n % 4, :], mx[:, n % 4, :], sinks[:, g, :], ALU.max))
                    step(V.tensor_tensor(sink_e[:, n % 4, :], sinks[:, g, :], mx[:, n % 4, :], ALU.subtract))
                V.tensor_scalar(negm[:, n % 4, 0:heads], mx[:, n % 4, 0:heads], -1.0, None, ALU.mult).then_inc(negm_ready, 1)

            def normalise(n):
                kind, g, t, w0, w = item_shape(n)
                heads = 4 if kind == "A" else 2
                s = s_sb[n % 2][:, 0:heads * w].rearrange("p (h w) -> p h w", h=heads)
                dve.wait_ge(exp_done, n + 1)
                if kind == "A":
                    step(V.tensor_tensor(den[:, n % 4, :], den[:, n % 4, :], sink_e[:, n % 4, :], ALU.add))
                step(V.reciprocal(mx[:, n % 4, 0:heads], den[:, n % 4, 0:heads]))
                for h in range(heads):
                    ins = V.tensor_scalar(s[:, h, :], s[:, h, :], mx[:, n % 4, h:h + 1], None, ALU.mult)
                ins.then_inc(p_ready, 1)

            dve.wait_ge(sinks_ready, 4)
            soften(0)
            for n in range(len(ITEMS)):
                if n + 1 < len(ITEMS):
                    soften(n + 1)
                normalise(n)
                if n < TOPK // 8:
                    take_best(TT - 1)
                elif n == TOPK // 8:
                    mask(TT - 1)

            for n, (heads, hi, lo) in enumerate([(qaT, branch_hi["a"], branch_lo["a"]),
                                                 (qbT, branch_hi["b"], branch_lo["b"])]):
                for k in range(DT):
                    dve.wait_ge(o_high, DT * n + k + 1)
                    V.tensor_tensor(lo[:, k, :], heads[:, k, :], hi[:, k, :].bitcast(F32), ALU.subtract
                                    ).then_inc(o_split, 1)
            dve.wait_ge(unit_copied, UNIT["gate", 15] + 1)
            for u in range(UNIT["a", 0], UNIT["out", 0]):
                kind, m, _, _ = UNITS[u]
                g = gaT if kind == "a" else gbT
                dve.wait_ge(unit_done, u + 1)
                V.scalar_tensor_tensor(g[:, m, :], g[:, m, :], 1.0, psum[:, bank_of(u), :], ALU.add, ALU.mult
                                       ).then_inc(merged_read, 1)
                if kind == "b":
                    dve.wait_ge(merged_read, u - UNIT["a", 0] + 1)
                    V.tensor_tensor(gaT[:, m, :], gaT[:, m, :], gbT[:, m, :], ALU.add).then_inc(m_ready, 1)
            for k in range(SPLIT):
                dve.wait_ge(m_high, k + 1)
                V.tensor_tensor(m_lo[:, k, :], gaT[:, k, :], m_hi[:, k, :].bitcast(F32), ALU.subtract
                                ).then_inc(m_split, 1)

            def norm1(t):
                V.tensor_scalar(ln[:, 0, 1, t:t + 1], ln[:, 0, 0, t:t + 1], -1.0 / D, None, ALU.mult
                                ).then_inc(mean_ready, 1)
                dve.wait_ge(ssq_ready, t + 1)
                V.tensor_scalar(ln[:, 0, 3, t:t + 1], ln[:, 0, 2, t:t + 1], 1.0 / D, LN_EPS, ALU.mult, ALU.add
                                ).then_inc(var_ready, 1)
                dve.wait_ge(rstd_ready, t + 1)
                step(V.tensor_scalar(h1[:, t, :], h1[:, t, :], ln[:, 0, 1, t:t + 1], ln[:, 0, 4, t:t + 1],
                                     ALU.add, ALU.mult))
                step(V.tensor_tensor(h1[:, t, :], h1[:, t, :], ln1g, ALU.mult))
                V.tensor_tensor(h1[:, t, :], h1[:, t, :], ln1b, ALU.add).then_inc(h1_ready, 1)

            dve.wait_ge(ln1_landed, 32)
            for t in range(TT):
                u = UNIT["out", 2 * t + 1]
                dve.wait_ge(ax_ready, t + 1)
                dve.wait_ge(unit_done, u + 1)
                V.scalar_tensor_tensor(h1[:, t, :], psum[:, bank_of(u) - 1:bank_of(u) + 1, :].rearrange(
                    "p b c -> p (b c)"), 0.5, h1[:, t, :], ALU.mult, ALU.add, accum_out=ln[:, 0, 0, t:t + 1]
                    ).then_inc(r_ready, 1)
                dve.wait_ge(r_ready, t + 1)
                norm1(t)

            def select(ts):
                n = ts.stop - ts.start

                def over(v, m):
                    return v[:, ts].unsqueeze(2).to_broadcast([P, n, m])

                def first_best(dst, score, best, v, top, m):
                    step(V.tensor_tensor(v, score, over(best, m), ALU.is_equal))
                    step(V.tensor_tensor(v, v, desc[:, 0:m].unsqueeze(1).to_broadcast([P, n, m]), ALU.mult))
                    step(V.tensor_reduce(top[:, ts], v, AX.X, ALU.max))
                    step(V.tensor_tensor(dst, v, over(top, m), ALU.is_equal))

                gl, gd, gm = lg[:, ts, 0:NG], g4[:, 2, ts], g4[:, 3, ts]
                logits, v, rest = e32[:, 0, ts], e32[:, 1, ts], e32[:, 2, ts]
                step(V.tensor_reduce(g1[:, 0, ts], gl, AX.X, ALU.max))
                V.tensor_tensor(g4[:, 0, ts], gl, over(g1[:, 0], NG), ALU.subtract).then_inc(gd_ready, 1)
                first_best(gm, gl, g1[:, 0], gd, g1[:, 1], NG)
                step(V.tensor_scalar(gm, gm, -MASKED, MASKED, ALU.mult, ALU.add))
                step(V.tensor_tensor(logits.rearrange("p t (g e) -> p t g e", g=NG),
                                     lg[:, ts, NG:].rearrange("p t (g e) -> p t g e", g=NG),
                                     gm.unsqueeze(3).to_broadcast([P, n, NG, EPG]), ALU.add))
                step(V.tensor_reduce(g1[:, 2, ts], logits, AX.X, ALU.max))
                first_best(oh[:, 0, ts], logits, g1[:, 2], v, g1[:, 3], NE)
                step(V.scalar_tensor_tensor(rest, oh[:, 0, ts], 2 * MASKED, logits, ALU.mult, ALU.add))
                step(V.tensor_reduce(g1[:, 4, ts], rest, AX.X, ALU.max))
                first_best(oh[:, 1, ts], rest, g1[:, 4], v, g1[:, 3], NE)
                V.tensor_tensor(oh_both[:, ts], oh[:, 0, ts], oh[:, 1, ts], ALU.add).then_inc(oh_ready, 1)
                V.tensor_tensor(g1[:, 5, ts], g1[:, 4, ts], g1[:, 2, ts], ALU.subtract).then_inc(md_ready, 1)

            nl = NG + NE
            dve.wait_ge(routed, 1)
            step(V.tensor_tensor(lg[:, 0:TT - 1, :], psum[:, 2, 0:(TT - 1) * nl].rearrange("p (t c) -> p t c", c=nl),
                                 rb[:, :].unsqueeze(1).to_broadcast([P, TT - 1, nl]), ALU.add))
            select(slice(0, TT - 1))
            dve.wait_ge(routed, 2)
            step(V.tensor_tensor(lg[:, TT - 1, :], psum[:, 3, 0:nl], rb[:, :], ALU.add))
            select(slice(TT - 1, TT))
            dve.wait_ge(ranked, 1)
            dve.wait_ge(const_ready, CONSTS)
            ranks = psum[:, 5, 0:TT * NE].rearrange("p (t e) -> p t e", t=TT)
            step(V.tensor_tensor(full_cmp, psum[:, 5, TT * NE:(TT + 1) * NE].unsqueeze(2).to_broadcast([P, NE, MORE]),
                                 fulls[:, :].unsqueeze(1).to_broadcast([P, NE, MORE]), ALU.is_gt))
            step(V.tensor_reduce(cnt[:, 1, :], full_cmp, AX.X, ALU.add))
            step(V.tensor_tensor_scan(cnt[:, 2, :], ones[:, 0:NE], cnt[:, 1, :], 0.0, ALU.mult, ALU.add))
            step(V.tensor_tensor(cnt[:, 3, :], cnt[:, 2, :], cnt[:, 1, :], ALU.subtract))
            step(V.scalar_tensor_tensor(cnt[:, 3, :], cnt[:, 3, :], float(CAP), base1[:, :], ALU.mult, ALU.subtract))
            step(V.scalar_tensor_tensor(paid, ranks, float(CAP), cnt[:, 3, :].unsqueeze(1).to_broadcast([P, TT, NE]),
                                        ALU.is_ge, ALU.mult))
            step(V.tensor_tensor(slot_of, ranks, base0[:, :].unsqueeze(1).to_broadcast([P, TT, NE]), ALU.add))
            step(V.tensor_tensor(slot_of, slot_of, paid, ALU.add))
            for k in range(2):
                step(V.tensor_tensor(picked[:, k].rearrange("p (t e) -> p t e", t=TT), oh[:, k], slot_of, ALU.mult))
            step(V.tensor_reduce(slot_f[:, :, :], picked.rearrange("p k (t e) -> p k t e", t=TT), AX.X, ALU.add))
            flat = slot_f[:, :, :].rearrange("p k t -> p (k t)")
            V.tensor_copy(slot_i[:, :, :], slot_f[:, :, :]).then_inc(slots_ready, 1)
            dve.wait_ge(slots_ready, 1)
            step(V.tensor_scalar(pair_i[:, :], slot_i[:, :, :].rearrange("p k t -> p (k t)"), CAP - 1, None,
                                 ALU.bitwise_and))
            step(V.tensor_copy(pair_s[:, :], pair_i[:, :]))
            step(V.tensor_tensor(pair_b[:, :], flat, pair_s[:, :], ALU.subtract))
            V.tensor_tensor(in_slot, col_s[:, :].unsqueeze(1).to_broadcast([P, N_TOP * TT, CAP]),
                            pair_s[:, :].unsqueeze(2).to_broadcast([P, N_TOP * TT, CAP]), ALU.is_equal)
            for j in range(N_TOP * TT):
                ins = V.tensor_scalar(in_block[:, j, :], col_b[:, :], pair_b[:, j:j + 1], tokid[:, j % TT:j % TT + 1],
                                      ALU.is_equal, ALU.mult)
            ins.then_inc(pairs_ready, 1)
            dve.wait_ge(table_done, 1)
            V.tensor_copy(tok_i[:, :], psum[0:CAP, 4, 0:NBLK + 1]).then_inc(tok_ready, 1)
            step(V.tensor_tensor(over_cmp[:, :, :], cnt[0:1, 2, :].unsqueeze(1).to_broadcast([1, MAX_OVER, NE]),
                                 jrow[:, :].unsqueeze(2).to_broadcast([1, MAX_OVER, NE]), ALU.is_le))
            step(V.tensor_reduce(over_f[:, 0:MAX_OVER], over_cmp[:, :, :], AX.X, ALU.add))
            step(V.tensor_scalar(over_f[:, 0:MAX_OVER], over_f[:, 0:MAX_OVER], float(NE - 1), None, ALU.min))
            step(V.tensor_copy(over_f[:, MAX_OVER:], cnt[0:1, 2, NE - 1:NE]))
            V.tensor_copy(over_i[:, :], over_f[:, :]).then_inc(over_ready, 1)
            dve.wait_ge(ge_ready, 2)
            dve.wait_ge(me_ready, 2)
            step(V.tensor_reduce(g1[:, 7, :], g4[:, 1], AX.X, ALU.add))
            step(V.tensor_scalar(g1[:, 8, :], g1[:, 6, :], 1.0, None, ALU.add))
            step(V.tensor_tensor(g1[:, 7, :], g1[:, 7, :], g1[:, 8, :], ALU.mult))
            step(V.reciprocal(g1[:, 8, :], g1[:, 7, :]))
            step(V.tensor_scalar(comb[:, 0, :], g1[:, 8, :], 0.5, None, ALU.mult))
            step(V.tensor_tensor(comb[:, 1, :], comb[:, 0, :], g1[:, 6, :], ALU.mult))

            def expert(b, i, s):
                dve.wait_ge(th_done, b + 1)
                V.scalar_tensor_tensor(gated[s % 2][CAP:P, :], th[s % 2][0:CAP, :], 1.0,
                                       psum[0:CAP, 2 + s % 2, 0:FF], ALU.add, ALU.mult).then_inc(gated_ready, 1)
                dve.wait_ge(gated_ready, b + 1)
                V.tensor_tensor(hid[s % 2][0:CAP, :], gated[s % 2][CAP:P, :], psum[CAP:P, 2 + s % 2, 0:FF], ALU.mult
                                ).then_inc(h_ready, 1)
                dve.wait_ge(ht_done, b + 1)
                V.tensor_copy(hidT[s % 2], psum[:, 1, 0:2 * CAP].rearrange("p (k c) -> p k c", k=2)
                              ).then_inc(ht_copied, 1)

            blocks(dve, expert)
            dve.wait_ge(ah_ready, TT)
            dve.wait_ge(ln2_landed, 32)
            for t in range(TT + 2):
                if t < TT:
                    dve.wait_ge(yk_landed[t][0], 16)
                    step(V.scalar_tensor_tensor(h1[:, t, :], yk[t][0], comb[:, 0, t:t + 1], h1[:, t, :],
                                                ALU.mult, ALU.add))
                    dve.wait_ge(yk_landed[t][1], 16)
                    V.scalar_tensor_tensor(h1[:, t, :], yk[t][1], comb[:, 1, t:t + 1], h1[:, t, :],
                                           ALU.mult, ALU.add, accum_out=ln[:, 1, 0, t:t + 1]).then_inc(r2_ready, 1)
                    dve.wait_ge(r2_ready, t + 1)
                    V.tensor_scalar(ln[:, 1, 1, t:t + 1], ln[:, 1, 0, t:t + 1], -1.0 / D, None, ALU.mult
                                    ).then_inc(mean2_ready, 1)
                if t >= 2:
                    dve.wait_ge(normed2_ready, t - 1)
                    V.tensor_tensor(h1[:, t - 2, :], h1[:, t - 2, :], ln2g, ALU.mult).then_inc(scaled2_ready, 1)
            dve.wait_ge(scaled2_ready, TT)
            V.tensor_tensor(h1[:, TT - 1, :], h1[:, TT - 1, :], ln2b, ALU.add).then_inc(last_ready, 1)


_INS = ['x', 'w_in', 'a_sinks', 'kv_norm_g', 'w_uk', 'w_uv', 'w_branch_a', 'w_branch_b', 'w_out', 'ln1_g', 'ln1_b',
        'router_group_w', 'router_group_b', 'router_expert_w', 'router_expert_b', 'w_gate', 'w_up', 'w_down',
        'ln2_g', 'ln2_b']
_OUTS = [((1, T, D), 'float32')]


def kernel(**inputs):
    import numpy as _np
    import concourse.bacc as _bacc
    from concourse import mybir as _mybir
    from concourse.bass_utils import run_bass_kernel_spmd as _run

    nc = _bacc.Bacc("TRN2", target_bir_lowering=False, num_devices=1)
    arrays, args = {}, []
    for name in _INS:
        a = _np.ascontiguousarray(inputs[name])
        if name in ('w_gate', 'w_up', 'w_down'):
            a = a.reshape(a.shape[0], NE, *a.shape[3:])
        arrays[f"in_{name}_dram"] = a
        args.append(nc.dram_tensor(f"in_{name}_dram", a.shape, _mybir.dt.from_np(a.dtype), kind="ExternalInput").ap())
    for i, (shape, dtype) in enumerate(_OUTS):
        dt = _mybir.dt.from_np(_np.dtype(dtype))
        args.append(nc.dram_tensor(f"out_{i}_dram", shape, dt, kind="ExternalOutput").ap())
    build(nc, *args)
    r = _run(nc, [arrays], core_ids=[0])
    got = tuple(r.results[0][f"out_{i}_dram"] for i in range(len(_OUTS)))
    return got[0]
```
